# Optimizing a Trainium2 kernel written in Bass

```python
import math
import jax, jax.numpy as jnp
from jax import lax
import numpy as np

D_MODEL = 1024
BATCH = 1
SEQ = 1024
DEPTH = 1
DEC_BATCH = 8
DEC_SEQ = 16
PAST_LEN = 512

CHUNK = 64
N_META = 16
HEAD_DIM = 64
FOX_HEADS = 8
SWA_HEADS = 8
SWA_KV_HEADS = 2
WINDOW = 128
WINDOW_CHUNKS = WINDOW // CHUNK
SWA_BUF = min(WINDOW, PAST_LEN)
D_FF = 4 * D_MODEL
ROPE_THETA = 10000.0
Q_BLOCK = 128
EPS = 1e-6
FORGET_BIAS_INIT = 3.0
FOX_W = FOX_HEADS * HEAD_DIM
SWA_QW = SWA_HEADS * HEAD_DIM
SWA_KVW = SWA_KV_HEADS * HEAD_DIM
IN_SIZES = (FOX_W, FOX_W, FOX_W, FOX_HEADS, SWA_QW, SWA_KVW, SWA_KVW, D_MODEL, D_MODEL)
D_IN = sum(IN_SIZES)

kernel_name = "fox_swa_sink_meta_streaming_encoder_step"

def rmsnorm(x, g):
    xf = x.astype(jnp.float32)
    y = xf * lax.rsqrt(jnp.mean(xf * xf, axis=-1, keepdims=True) + EPS)
    return (y * g.astype(jnp.float32)).astype(x.dtype)

def rope(x, pos):
    half = HEAD_DIM // 2
    inv_freq = ROPE_THETA ** (-jnp.arange(half, dtype=jnp.float32) / half)
    ang = pos.astype(jnp.float32)[:, None] * inv_freq[None, :]
    cos = jnp.cos(ang)[:, None, :]
    sin = jnp.sin(ang)[:, None, :]
    xf = x.astype(jnp.float32)
    x1, x2 = xf[..., :half], xf[..., half:]
    return jnp.concatenate([x1 * cos - x2 * sin, x2 * cos + x1 * sin], axis=-1).astype(x.dtype)

def project(xn, w_in, b_forget, pos):
    y = jnp.einsum('bld,de->ble', xn, w_in)
    offs = np.cumsum(IN_SIZES)[:-1].tolist()
    q_a, k_a, v_a, f_a, q_b, k_b, v_b, g_a, g_b = jnp.split(y, offs, axis=-1)
    B, L = y.shape[0], y.shape[1]
    heads = lambda t, n: t.reshape(B, L, n, HEAD_DIM)
    logf = jax.nn.log_sigmoid((f_a + b_forget).astype(jnp.float32))
    q_b = rope(heads(q_b, SWA_HEADS), pos)
    k_b = rope(heads(k_b, SWA_KV_HEADS), pos)
    return (heads(q_a, FOX_HEADS), heads(k_a, FOX_HEADS), heads(v_a, FOX_HEADS), logf,
            q_b, k_b, heads(v_b, SWA_KV_HEADS), g_a, g_b)

def fox_attend(q, k_pre, v_pre, lf_pre, k, v, lf):
    B, L, H, dh = q.shape
    P = k_pre.shape[1]
    k_all = jnp.concatenate([k_pre, k], axis=1)
    v_all = jnp.concatenate([v_pre, v], axis=1)
    lf_all = jnp.concatenate([lf_pre.astype(jnp.float32), lf.astype(jnp.float32)], axis=1)
    c = jnp.cumsum(lf_all, axis=1)
    c_k = jnp.transpose(c, (0, 2, 1))[:, :, None, :]
    key_frame = jnp.arange(P + L) - P
    qb = Q_BLOCK if L % Q_BLOCK == 0 else L
    nb = L // qb
    q_blocks = q.reshape(B, nb, qb, H, dh).swapaxes(0, 1)
    cq_blocks = c[:, P:].reshape(B, nb, qb, H).swapaxes(0, 1)
    qi_blocks = jnp.arange(L).reshape(nb, qb)
    scale = dh ** -0.5

    def block(args):
        q_blk, cq_blk, qi = args
        s = jnp.einsum('bqhd,bkhd->bhqk', q_blk, k_all).astype(jnp.float32) * scale
        bias = jnp.transpose(cq_blk, (0, 2, 1))[:, :, :, None] - c_k
        mask = key_frame[None, :] <= qi[:, None]
        s = jnp.where(mask[None, None], s + bias, -jnp.inf)
        p = jax.nn.softmax(s, axis=-1).astype(v_all.dtype)
        return jnp.einsum('bhqk,bkhd->bqhd', p, v_all)

    out = lax.map(block, (q_blocks, cq_blocks, qi_blocks))
    return out.swapaxes(0, 1).reshape(B, L, H, dh)

def sink_softmax(s, sinks_gr):
    sk = sinks_gr.astype(jnp.float32)[:, :, None]
    m = jnp.maximum(jnp.max(s, axis=-1, keepdims=True), sk)
    e = jnp.exp(s - m)
    return e / (jnp.sum(e, axis=-1, keepdims=True) + jnp.exp(sk - m))

def swa_dense(q, k, v, sinks):
    B, Lq, H, dh = q.shape
    G = k.shape[2]
    R = H // G
    qg = q.reshape(B, Lq, G, R, dh)
    s = jnp.einsum('bqgrd,bkgd->bqgrk', qg, k).astype(jnp.float32) * (dh ** -0.5)
    p = sink_softmax(s, sinks.reshape(G, R)).astype(v.dtype)
    return jnp.einsum('bqgrk,bkgd->bqgrd', p, v).reshape(B, Lq, H, dh)

def swa_band(q, k, v, k_meta, v_meta, sinks):
    B, L, H, dh = q.shape
    G = k.shape[2]
    R = H // G
    nC = L // CHUNK
    pad = WINDOW_CHUNKS * CHUNK
    BK = (WINDOW_CHUNKS + 1) * CHUNK

    def bands(t):
        tp = jnp.pad(t, ((0, 0), (pad, 0), (0, 0), (0, 0))).reshape(B, nC + WINDOW_CHUNKS, CHUNK, G, dh)
        return jnp.concatenate([tp[:, i:i + nC] for i in range(WINDOW_CHUNKS + 1)], axis=2)

    kb, vb = bands(k), bands(v)
    qc = q.reshape(B, nC, CHUNK, G, R, dh)
    scale = dh ** -0.5
    s_meta = jnp.einsum('bcqgrd,bmgd->bcqgrm', qc, k_meta).astype(jnp.float32) * scale
    s_band = jnp.einsum('bcqgrd,bckgd->bcqgrk', qc, kb).astype(jnp.float32) * scale
    frame = (jnp.arange(nC)[:, None] - WINDOW_CHUNKS) * CHUNK + jnp.arange(BK)[None, :]
    valid = frame >= 0
    s_band = jnp.where(valid[None, :, None, None, None, :], s_band, -jnp.inf)
    M = k_meta.shape[1]
    p = sink_softmax(jnp.concatenate([s_meta, s_band], axis=-1), sinks.reshape(G, R)).astype(v.dtype)
    o = (jnp.einsum('bcqgrm,bmgd->bcqgrd', p[..., :M], v_meta)
         + jnp.einsum('bcqgrk,bckgd->bcqgrd', p[..., M:], vb))
    return o.reshape(B, L, H, dh)

def finish(h, o_a, o_b, g_a, g_b, w_o_fox, w_o_swa, w_out, g_post_mix, g_pre_mlp, g_post_mlp, w_up, w_down):
    B, L = h.shape[0], h.shape[1]
    y_a = jnp.einsum('ble,ed->bld', o_a.reshape(B, L, FOX_W), w_o_fox)
    y_b = jnp.einsum('ble,ed->bld', o_b.reshape(B, L, SWA_QW), w_o_swa)
    mix = jnp.einsum('bld,de->ble', jax.nn.sigmoid(g_a) * y_a + jax.nn.sigmoid(g_b) * y_b, w_out)
    h = h + rmsnorm(mix, g_post_mix)
    u = jnp.square(jax.nn.relu(jnp.einsum('bld,df->blf', rmsnorm(h, g_pre_mlp), w_up)))
    return h + rmsnorm(jnp.einsum('blf,fd->bld', u, w_down), g_post_mlp)

def setup_inputs(seed: int = 0) -> dict:
    key = jax.random.key(seed)
    ks = jax.random.split(key, 20)
    nrm = lambda k, shape, scale: jax.random.normal(k, shape, jnp.float32) * scale
    return {
        'x_prompt': nrm(ks[0], (BATCH, SEQ, D_MODEL), 1.0),
        'x_sample': nrm(ks[1], (DEC_BATCH, DEC_SEQ, D_MODEL), 1.0),
        'cache_fox_k': nrm(ks[2], (DEPTH, DEC_BATCH, PAST_LEN, FOX_HEADS, HEAD_DIM), 1.0),
        'cache_fox_v': nrm(ks[3], (DEPTH, DEC_BATCH, PAST_LEN, FOX_HEADS, HEAD_DIM), 1.0),
        'cache_fox_logf': jax.nn.log_sigmoid(FORGET_BIAS_INIT + nrm(ks[4], (DEPTH, DEC_BATCH, PAST_LEN, FOX_HEADS), 1.0)),
        'cache_swa_k': nrm(ks[5], (DEPTH, DEC_BATCH, SWA_BUF, SWA_KV_HEADS, HEAD_DIM), 1.0),
        'cache_swa_v': nrm(ks[6], (DEPTH, DEC_BATCH, SWA_BUF, SWA_KV_HEADS, HEAD_DIM), 1.0),
        'meta_tokens': nrm(ks[7], (N_META, D_MODEL), 1.0),
        'w_in': nrm(ks[8], (DEPTH, D_MODEL, D_IN), D_MODEL ** -0.5),
        'b_forget': FORGET_BIAS_INIT + nrm(ks[9], (DEPTH, FOX_HEADS), 0.1),
        'attn_sinks': nrm(ks[10], (DEPTH, SWA_HEADS), 0.5),
        'w_o_fox': nrm(ks[11], (DEPTH, FOX_W, D_MODEL), FOX_W ** -0.5),
        'w_o_swa': nrm(ks[12], (DEPTH, SWA_QW, D_MODEL), SWA_QW ** -0.5),
        'w_out': nrm(ks[13], (DEPTH, D_MODEL, D_MODEL), D_MODEL ** -0.5),
        'g_pre_mix': 1.0 + nrm(ks[14], (DEPTH, D_MODEL), 0.05),
        'g_post_mix': 1.0 + nrm(ks[15], (DEPTH, D_MODEL), 0.05),
        'g_pre_mlp': 1.0 + nrm(ks[16], (DEPTH, D_MODEL), 0.05),
        'g_post_mlp': 1.0 + nrm(ks[17], (DEPTH, D_MODEL), 0.05),
        'w_up': nrm(ks[18], (DEPTH, D_MODEL, D_FF), D_MODEL ** -0.5),
        'w_down': nrm(ks[19], (DEPTH, D_FF, D_MODEL), D_FF ** -0.5),
    }

def reference(x_prompt, x_sample, cache_fox_k, cache_fox_v, cache_fox_logf, cache_swa_k, cache_swa_v,
              meta_tokens, w_in, b_forget, attn_sinks, w_o_fox, w_o_swa, w_out,
              g_pre_mix, g_post_mix, g_pre_mlp, g_post_mlp, w_up, w_down):
    Bp, Lp = x_prompt.shape[0], x_prompt.shape[1]
    Bs, Ls = x_sample.shape[0], x_sample.shape[1]
    past = cache_fox_k.shape[2]
    pos_m = jnp.arange(N_META) - N_META
    pos_p = jnp.arange(Lp)
    pos_s = past + jnp.arange(Ls)
    bc = lambda t, b: jnp.broadcast_to(t, (b,) + t.shape[1:])

    h_m = meta_tokens[None].astype(x_prompt.dtype)
    h_p, h_s = x_prompt, x_sample
    fkp, fvp, flp, skp, svp = [], [], [], [], []
    fks, fvs, fls, sks, svs = [], [], [], [], []
    for l in range(DEPTH):
        qa_m, ka_m, va_m, lf_m, qb_m, kb_m, vb_m, ga_m, gb_m = project(rmsnorm(h_m, g_pre_mix[l]), w_in[l], b_forget[l], pos_m)
        qa_p, ka_p, va_p, lf_p, qb_p, kb_p, vb_p, ga_p, gb_p = project(rmsnorm(h_p, g_pre_mix[l]), w_in[l], b_forget[l], pos_p)
        qa_s, ka_s, va_s, lf_s, qb_s, kb_s, vb_s, ga_s, gb_s = project(rmsnorm(h_s, g_pre_mix[l]), w_in[l], b_forget[l], pos_s)

        ka_mp, va_mp, lf_mp = bc(ka_m, Bp), bc(va_m, Bp), bc(lf_m, Bp)
        oa_p = fox_attend(qa_p, ka_mp, va_mp, lf_mp, ka_p, va_p, lf_p)
        ob_p = swa_band(qb_p, kb_p, vb_p, bc(kb_m, Bp), bc(vb_m, Bp), attn_sinks[l])

        oa_s = fox_attend(qa_s, cache_fox_k[l], cache_fox_v[l], cache_fox_logf[l], ka_s, va_s, lf_s)
        k_win = jnp.concatenate([bc(kb_m, Bs), cache_swa_k[l], kb_s], axis=1)
        v_win = jnp.concatenate([bc(vb_m, Bs), cache_swa_v[l], vb_s], axis=1)
        ob_s = swa_dense(qb_s, k_win, v_win, attn_sinks[l])

        fkp.append(jnp.concatenate([ka_mp, ka_p], axis=1))
        fvp.append(jnp.concatenate([va_mp, va_p], axis=1))
        flp.append(jnp.concatenate([lf_mp, lf_p], axis=1))
        skp.append(kb_p[:, -min(WINDOW, Lp):])
        svp.append(vb_p[:, -min(WINDOW, Lp):])
        fks.append(ka_s)
        fvs.append(va_s)
        fls.append(lf_s)
        sks.append(kb_s)
        svs.append(vb_s)

        layer_w = (w_o_fox[l], w_o_swa[l], w_out[l], g_post_mix[l], g_pre_mlp[l], g_post_mlp[l], w_up[l], w_down[l])
        if l < DEPTH - 1:
            oa_m = fox_attend(qa_m, ka_m[:, :0], va_m[:, :0], lf_m[:, :0], ka_m, va_m, lf_m)
            ob_m = swa_dense(qb_m, kb_m, vb_m, attn_sinks[l])
            h_m = finish(h_m, oa_m, ob_m, ga_m, gb_m, *layer_w)
        h_p = finish(h_p, oa_p, ob_p, ga_p, gb_p, *layer_w)
        h_s = finish(h_s, oa_s, ob_s, ga_s, gb_s, *layer_w)

    return (h_p, h_s,
            jnp.stack(fkp), jnp.stack(fvp), jnp.stack(flp), jnp.stack(skp), jnp.stack(svp),
            jnp.stack(fks), jnp.stack(fvs), jnp.stack(fls), jnp.stack(sks), jnp.stack(svs))


_drawn_inputs = setup_inputs


def setup_inputs(seed=0):
    import zlib

    import numpy as np

    out = dict(_drawn_inputs(seed))
    spreads = {}
    factors = {'attn_sinks': 8.0}
    for name, (base, spread) in spreads.items():
        noise = np.random.default_rng([zlib.crc32(name.encode()), seed]).standard_normal(out[name].shape)
        drawn = base * np.exp(spread * noise) if base else spread * noise
        out[name] = __import__('jax').numpy.asarray(drawn.astype(out[name].dtype))
    for name, factor in factors.items():
        out[name] = (out[name] * factor).astype(out[name].dtype)
    return out
```

```python
from contextlib import ExitStack

import concourse.bass as bass
from concourse import mybir

P = 128
F32 = mybir.dt.float32
F32R = mybir.dt.float32r
ALU = mybir.AluOpType
ACT = mybir.ActivationFunctionType
AX_X = mybir.AxisListType.X

D = 1024
KT = D // P
META, SEQ, STREAMS, NEW = 16, 1024, 8, 16
PAST, SBUF_WIN = 512, 128
SAMPLE = STREAMS * NEW
TOK = SEQ + SAMPLE
NT = META + TOK
KEYS = META + SEQ
S0 = KEYS
HEADS, DH = 8, 64
FOX_W = HEADS * DH
DFF = 4 * D
EPS = 1e-6
SCALE = DH ** -0.5
BIG = 1e30
COL_QA, COL_KA, COL_VA, COL_F = 0, FOX_W, 2 * FOX_W, 3 * FOX_W
COL_QB = COL_F + HEADS
COL_KB, COL_VB = COL_QB + FOX_W, COL_QB + FOX_W + P
COL_GA = COL_VB + P
COL_GB = COL_GA + D
CHUNK_ALL = [(0, 400), (400, 784), (784, 1168)]
CHUNK_TOK = [(META + 384 * c, META + 384 * c + 384) for c in range(3)]
TT = TOK // P
GRP = 4
NGRP = DFF // (GRP * P)

C_ID, C_MASK, C_BAND, C_BAND0, C_NEW, C_SEL, C_NSEL = 0, 128, 256, 528, 672, 688, 1712
C_ALL = 1840

U_F, U_QA = 0, 1
U_FOX = 4
U_PEEL = U_FOX + 12
U_SWA = U_PEEL + 4
U_SPEEL = U_SWA + 6
U_SAM = U_SPEEL + 1
U_MIX = U_SAM + 8
SIDE = 16


def fox_chunks(i):
    w = META + P * (i + 1)
    if w <= 512:
        return [(0, w)]
    return [(0, 400), (400, w)] if w <= 912 else [(0, 400), (400, 912), (912, w)]


def fox_rounds(i):
    n = i + 2
    return [(a, min(a + 4, n)) for a in range(0, n, 4)]


FOX_C = [6 + sum(len(fox_chunks(m % 8)) for m in range(n)) for n in range(SIDE + 1)]
FOX_R = [6 + sum(len(fox_rounds(m % 8)) for m in range(n)) for n in range(SIDE + 1)]
FC, FR = FOX_C[SIDE], FOX_R[SIDE]
assert FC % 2 == 0 and FR % 2 == 0


class Unit:

    def __init__(self, b, per=0, it=0):
        self.n = b + per * it if per else b
        self.slot = b % 2
        self.nth = b // 2 + (per // 2) * it if per else b // 2


def layer(nc, I, O, scratch):
    o_scr, sig_scr, h_scr = scratch
    keep = ExitStack()
    with keep:
        def sb(name, shape, dt=F32, ctx=keep):
            return ctx.enter_context(nc.sbuf_tensor(name, shape, dt))

        def sem(name):
            return keep.enter_context(nc.semaphore(name))

        gb = [keep.enter_context(nc.psum_tensor(f"gb{c}", [P, 512], F32)) for c in range(3)]
        sc = [keep.enter_context(nc.psum_tensor(f"sc{c}", [P, 512], F32)) for c in range(2)]
        tp = [keep.enter_context(nc.psum_tensor(f"tp{c}", [P, 512], F32)) for c in range(2)]
        po = keep.enter_context(nc.psum_tensor("po", [P, 512], F32))
        dn = [sc[0], sc[1], tp[0], tp[1]]
        hb = [po, gb[2]]

        raw = [sb(f"raw{s}", [P, 1024]) for s in range(2)]
        wh = [sb(f"wh{s}", [P, 1024], F32R) for s in range(2)]
        wl = [sb(f"wl{s}", [P, 1024], F32R) for s in range(2)]
        ident = sb("ident", [P, P])
        ident_r = sb("ident_r", [P, P], F32R)
        mask_r = sb("mask_r", [P, P], F32R)
        osT_rl = sb("osT_rl", [P, 3 * 384])
        osT = osT_rl[:, 0:8 * SAMPLE]
        rl, rl2 = [osT_rl[:, 0:384], osT_rl[:, 384:768]], osT_rl[:, 768:1152]
        small = sb("small", [P, 160])
        mx, nm, ssum, rinv = small[:, 0:12], small[:, 12:16], small[:, 16:24], small[:, 24:28]
        esink, sinkcur, bf = small[:, 28:32], small[:, 32:34], small[0:8, 34:35]
        sinkb, sinkrow = small[:, 36:44], small[:, 44:45]
        ssq, var, rv, rstd = small[:, 48:60], small[:, 60:72], small[:, 72:84], small[:, 84:96]
        nt1, nt2, ssq2 = small[:, 96:108], small[:, 108:120], small[:, 120:140]

        A = ExitStack()
        cst = sb("cst", [P, C_ALL], ctx=A)
        Xh = sb("Xh", [P, KT * NT], F32R, A)
        Xl = sb("Xl", [P, KT * NT], F32R, A)
        A1 = ExitStack()
        xt = [sb(f"xt{t}", [P, D], ctx=A1) for t in range(10)]
        gpre = sb("gpre", [P, D], ctx=A1)
        junk = sb("junk", [P, D], ctx=A1)
        A1.close()
        A2k = ExitStack()
        qTs = sb("qTs", [P, 4 * P], ctx=A2k)
        kTs = sb("kTs", [P, 4 * P], ctx=A2k)
        vTs = sb("vTs", [P, 4 * P], ctx=A2k)
        qbs = sb("qbs", [P, 4 * P], ctx=A2k)
        kbT = sb("kbT", [P, NT], ctx=A2k)
        vball = sb("vball", [P, 12 * P], ctx=A2k)
        vbs = sb("vbs", [P, P], ctx=A2k)
        lfq = sb("lfq", [8, NT], ctx=A2k)
        cum_lf = sb("cum_lf", [8, KEYS], ctx=A2k)
        sig = sb("sig", [P, TOK], ctx=A2k)
        A2 = ExitStack()
        nA = sb("nA", [P, NT], ctx=A2)
        nB = sb("nB", [P, NT], ctx=A2)
        nC = sb("nC", [P, NT], ctx=A2)
        qcur = sb("qcur", [P, NT], ctx=A2)
        kcur = sb("kcur", [P, NT], ctx=A2)
        vcur = sb("vcur", [P, 10 * P], ctx=A2)
        ktm = sb("ktm", [P, 10 * P], ctx=A2)
        ckb = [sb(f"ckb{h}", [P, KEYS], ctx=A2) for h in range(2)]
        u = [sb(f"u{s}", [P, 9 * P], ctx=A2) for s in range(2)]
        PT = [sb(f"PT{s}", [P, 9 * P], ctx=A2) for s in range(2)]
        opair = sb("opair", [P, SEQ], ctx=A2)
        selcur = sb("selcur", [8, 2 * P], ctx=A2)
        sh = osT_rl[:, 0:400]
        A2.close()
        A3 = ExitStack()
        kc = [sb(f"kc{s}", [P, 4 * 512], ctx=A3) for s in range(2)]
        vc = [sb(f"vc{s}", [P, 4 * 512], ctx=A3) for s in range(2)]
        kw = [sb(f"kw{s}", [P, P], ctx=A3) for s in range(2)]
        vw = [sb(f"vw{s}", [P, P], ctx=A3) for s in range(2)]
        KcT = sb("KcT", [P, 4 * 512], ctx=A3)
        KwT = sb("KwT", [P, P], ctx=A3)
        qz = sb("qz", [P, 640], ctx=A3)
        qzs = sb("qzs", [P, P], ctx=A3)
        kvn = sb("kvn", [P, 10 * NEW], ctx=A3)
        vn = sb("vn", [NEW, 5 * P], ctx=A3)
        Ps = sb("Ps", [P, 5 * P], ctx=A3)
        Pw = sb("Pw", [P, 272], ctx=A3)
        PTs = sb("PTs", [P, 8 * P], ctx=A3)
        one8 = sb("one8", [8, 512], ctx=A3)
        clf = sb("clf", [P, 2 * 32], ctx=A3)
        lf16 = sb("lf16", [8, NEW], ctx=A3)
        cs = sb("cs", [8, 528], ctx=A3)
        A3.close()
        A2k.close()
        A.close()
        Mk = ExitStack()
        Mh = sb("Mh", [P, KT * TOK], F32R, Mk)
        Ml = sb("Ml", [P, KT * TOK], F32R, Mk)
        B1 = ExitStack()
        Oh = sb("Oh", [P, KT * TOK], F32R, B1)
        Ol = sb("Ol", [P, KT * TOK], F32R, B1)
        ot = [sb(f"ot{s}", [P, D], ctx=B1) for s in range(2)]
        sga = [sb(f"sga{s}", [P, TOK], ctx=B1) for s in range(2)]
        sgb = [sb(f"sgb{s}", [P, TOK], ctx=B1) for s in range(2)]
        B1.close()
        B2 = ExitStack()
        woh = sb("woh", [P, 8 * D], F32R, B2)
        wol = sb("wol", [P, 8 * D], F32R, B2)
        gpost = sb("gpost", [P, D], ctx=B2)
        gmlp = sb("gmlp", [P, D], ctx=B2)
        xr = [sb(f"xr{s}", [P, D], ctx=B2) for s in range(2)]
        tb = [sb(f"tb{s}", [P, D], ctx=B2) for s in range(2)]
        jk = sb("jk", [P, D], ctx=B2)
        B2.close()
        B3 = ExitStack()
        Uh = sb("Uh", [P, GRP * TOK], F32R, B3)
        Ul = sb("Ul", [P, GRP * TOK], F32R, B3)
        yacc = sb("yacc", [P, TT * D], ctx=B3)
        dh = sb("dh", [P, GRP * D], F32R, B3)
        dl = sb("dl", [P, GRP * D], F32R, B3)
        B3.close()
        Mk.close()
        E1 = ExitStack()
        hend = sb("hend", [P, TT * D], ctx=E1)
        gend = sb("gend", [P, D], ctx=E1)
        jend = sb("jend", [P, D], ctx=E1)
        E1.close()

        Xh3 = Xh[:, :].rearrange("p (k n) -> p k n", k=KT)
        Xl3 = Xl[:, :].rearrange("p (k n) -> p k n", k=KT)
        Mh3 = Mh[:, :].rearrange("p (k n) -> p k n", k=KT)
        Ml3 = Ml[:, :].rearrange("p (k n) -> p k n", k=KT)
        Oh3 = Oh[:, :].rearrange("p (k n) -> p k n", k=KT)
        Ol3 = Ol[:, :].rearrange("p (k n) -> p k n", k=KT)

        raw_full = [sem(f"raw_full{s}") for s in range(2)]
        w_hi, w_lo = sem("w_hi"), sem("w_lo")
        gemm_done = sem("gemm_done")
        bank_free = [sem(f"bank_free{c}") for c in range(3)]
        tp_full = sem("tp_full")
        tp_free = [sem(f"tp_free{s}") for s in range(2)]
        sc_full, sc_free = sem("sc_full"), sem("sc_free")
        cst_in, cst_r = sem("cst_in"), sem("cst_r")
        x_in = [sem(f"x_in{t}") for t in range(10)]
        g_in, ssq_done, rstd_done, x_chain = sem("g_in"), sem("ssq_done"), sem("rstd_done"), sem("x_chain")
        sq_done, xs_done, x_hi, x_lo = sem("sq_done"), sem("xs_done"), sem("x_hi"), sem("x_lo")
        lf_chain, lf_act, lf_done, lf_out = sem("lf_chain"), sem("lf_act"), sem("lf_done"), sem("lf_out")
        zero_u, zero_s, y_zero, one_set = sem("zero_u"), sem("zero_s"), sem("y_zero"), sem("one_set")
        cur_copied, kv_out, tab_in = sem("cur_copied"), sem("kv_out"), sem("tab_in")
        nm_done, p_done, sum_inv, m_done = sem("nm_done"), sem("p_done"), sem("sum_inv"), sem("m_done")
        pv_done, o_done, o_out = sem("pv_done"), sem("o_done"), sem("o_out")
        es_done, tot_done = sem("es_done"), sem("tot_done")
        gate_1, sig_done, sig_out = sem("gate_1"), sem("sig_done"), sem("sig_out")
        rope_sh, rope_a, rope_b = sem("rope_sh"), sem("rope_a"), sem("rope_b")
        vb_done, kb_out = sem("vb_done"), sem("kb_out")
        swa_cur = sem("swa_cur")
        c_in = [sem(f"c_in{e}") for e in range(2)]
        sam_free, s_stage, s_cs, s_red = sem("sam_free"), sem("s_stage"), sem("s_cs"), sem("s_red")
        s_exp, s_sum, s_scl = sem("s_exp"), sem("s_sum"), sem("s_scl")
        o_in = [sem(f"o_in{e}") for e in range(2)]
        sg_in = [sem(f"sg_in{e}") for e in range(2)]
        o_hi, o_lo, m_sum, m_hi, m_lo = sem("o_hi"), sem("o_lo"), sem("m_sum"), sem("m_hi"), sem("m_lo")
        wo_hi, wo_lo = sem("wo_hi"), [sem(f"wo_lo{e}") for e in range(2)]
        g2_in, g3_in, rv_done = sem("g2_in"), sem("g3_in"), sem("rv_done")
        xr_in = [sem(f"xr_in{e}") for e in range(2)]
        dn_full, dn_free = sem("dn_full"), sem("dn_free")
        hT_full, hT_free, h_hi = sem("hT_full"), [sem(f"hT_free{e}") for e in range(2)], sem("h_hi")
        h_done, hn_done, sq_a, sq_b = sem("h_done"), sem("hn_done"), sem("sq_a"), sem("sq_b")
        h_out = [sem(f"h_out{e}") for e in range(2)]
        u_hi, u_sq, u_lo, d_hi, d_lo = sem("u_hi"), sem("u_sq"), sem("u_lo"), sem("d_hi"), sem("d_lo")
        yn_done, y_done, y_out = sem("yn_done"), [sem(f"y_done{e}") for e in range(2)], sem("y_out")

        def cols_of(w, c0, reg=None, step=0):
            v = w.rearrange("(k p) n -> p k n", p=P)
            cs_ = bass.ds(reg * step + c0, P) if step else slice(c0, c0 + P)
            return [(lambda d: d[:, 0:4, :], v[:, 0:4, cs_]), (lambda d: d[:, 4:8, :], v[:, 4:8, cs_])]

        def cols_qb(reg):
            v = I["w_in"].rearrange("(k p) n -> p k n", p=P)
            return [(lambda d, g=g: d[:, :, g * DH:(g + 1) * DH],
                     v[:, :, bass.ds(reg * DH + (COL_QB + g * 4 * DH), DH)]) for g in range(2)]

        def cols_gate(g0, reg=None, step=0):
            return cols_of(I["w_in"], COL_GA + g0 * P, reg, step * P)

        def load(sp, U, parts):
            if not isinstance(U.n, int) or U.n >= 2:
                sp.wait_ge(w_lo, U.n - 1)
            dst = raw[U.slot][:, :].rearrange("p (k n) -> p k n", k=KT)
            for part, src in parts:
                sp.dma_start(part(dst), src).then_inc(raw_full[U.slot], 16)

        def hi(act, U, used=None):
            act.wait_ge(raw_full[U.slot], U.nth * 32 + 32)
            if not isinstance(U.n, int) or U.n >= 2:
                act.wait_ge(gemm_done, U.n * 3 - 3 if used is None else used)
            nc.scalar.activation(wh[U.slot][:, :], raw[U.slot][:, :], ACT.Copy).then_inc(w_hi, 1)

        def lo(pool, U):
            pool.wait_ge(w_hi, U.n + 1)
            nc.gpsimd.tensor_tensor(wl[U.slot][:, :], raw[U.slot][:, :], wh[U.slot][:, :].bitcast(F32),
                                    ALU.subtract).then_inc(w_lo, 1)

        def gemm(pe, U, c, cols):
            if c == 0:
                pe.wait_ge(w_lo, U.n + 1)
            if not isinstance(U.n, int) or U.n > 0:
                pe.wait_ge(bank_free[c], U.n)
            a, b = cols
            for k in range(KT):
                ws = slice(k * P, (k + 1) * P)
                for j, (w_, x_) in enumerate(((wh, Xh3), (wl, Xh3), (wh, Xl3))):
                    last = nc.tensor.matmul(gb[c][:, 0:b - a], w_[U.slot][:, ws], x_[:, k, a:b],
                                            start=(k == 0 and j == 0), stop=(k == KT - 1 and j == 2))
            last.then_inc(gemm_done, 1)

        def apart(eng):
            eng.wait_ge(cst_in, 32)

        def at(eng, x):
            return x if isinstance(x, int) else eng.snap(eng.to_reg(x))

        def gemm_wait(eng, U, c):
            eng.wait_ge(gemm_done, U.n * 3 + (c + 1))

        def four(bank):
            return bank[:, :].rearrange("p (j n) -> p j n", j=4)

        XROWS = [META] + [P] * 9
        XCOL = [0] + [META + P * t for t in range(9)]
        XSRC = [I["meta_tokens"]] + [I["x_prompt"][0, P * t:P * t + P, :] for t in range(8)] + [
            I["x_sample"].rearrange("b l d -> (b l) d")]

        def norm_sp(sp):
            sp.dma_start(ident[:, :], I["cst"][:, C_ID:C_ID + P]).then_inc(cst_in, 16)
            sp.dma_start(cst[:, :], I["cst"]).then_inc(cst_in, 16)
            for t in range(10):
                sp.dma_start(xt[t][0:XROWS[t], :], XSRC[t]).then_inc(x_in[t], 16)
                if t == 1:
                    load(sp, Unit(0), cols_of(I["w_in"], COL_F))
                    sp.dma_start(gpre[:, :], I["g_pre_mix"].to_broadcast([P, D])).then_inc(g_in, 16)
                    load(sp, Unit(1), cols_of(I["w_in"], COL_QA))
            sp.wait_ge(x_chain, 1)
            sp.dma_start(sinkb, I["attn_sinks"].to_broadcast([P, HEADS])).then_inc(g_in, 16)
            sp.dma_start(bf, I["b_forget"].rearrange("o h -> h o")).then_inc(g_in, 16)
            for h in range(HEADS):
                row = (h % 4) * 32 + (h // 4) * 16
                sp.dma_start(sinkrow[row:row + 16, :], I["attn_sinks"][:, h:h + 1].to_broadcast([16, 1])).then_inc(g_in, 16)

        def norm_act(act):
            act.wait_ge(x_chain, 1)
            for t in range(10):
                act.wait_ge(x_in[t], 16)
                if t:
                    act.wait_ge(ssq_done, t)
                nc.scalar.activation(junk[0:XROWS[t], :], xt[t][0:XROWS[t], :], ACT.Square,
                                     accum_out=ssq[0:XROWS[t], t:t + 1]).then_inc(ssq_done, 1)
            act.wait_ge(rstd_done, 1)
            nc.scalar.activation(rstd[:, 0:10], rv[:, 0:10], ACT.Sqrt).then_inc(sq_done, 1)
            hi(act, Unit(0))
            hi(act, Unit(1))
            for t in range(10):
                n, c0 = XROWS[t], XCOL[t]
                for h in range(2):
                    act.wait_ge(tp_full, 2 * t + h + 1)
                    nc.scalar.activation(Xh3[:, 4 * h:4 * h + 4, c0:c0 + n], four(tp[h])[:, :, 0:n],
                                         ACT.Copy).then_inc(x_hi, 1)

        def rsqrt_dve(v, n, base, y0_ready, y0_count):
            a, b = n
            v.wait_ge(y0_ready, y0_count)
            y, t1, t2, w = rstd[:, a:b], nt1[:, a:b], nt2[:, a:b], var[:, a:b]
            nc.vector.tensor_tensor(t1, y, y, ALU.mult).then_inc(x_chain, 1)
            v.wait_ge(x_chain, base + 1)
            nc.vector.tensor_tensor(t2, t1, w, ALU.mult).then_inc(x_chain, 1)
            v.wait_ge(x_chain, base + 2)
            nc.vector.tensor_scalar(t1, t2, -0.5, 1.5, ALU.mult, ALU.add).then_inc(x_chain, 1)
            v.wait_ge(x_chain, base + 3)
            nc.vector.tensor_tensor(y, y, t1, ALU.mult).then_inc(x_chain, 1)
            v.wait_ge(x_chain, base + 4)

        def norm_dve(v):
            nc.vector.memset(small[:, :], 1.0).then_inc(x_chain, 1)
            v.wait_ge(cst_in, 32)
            nc.vector.tensor_copy(ident_r[:, :], ident[:, :]).then_inc(cst_r, 1)
            nc.vector.tensor_copy(mask_r[:, :], cst[:, C_MASK:C_MASK + P]).then_inc(cst_r, 1)
            v.wait_ge(ssq_done, 10)
            nc.vector.tensor_scalar(var[:, 0:10], ssq[:, 0:10], 1.0 / D, EPS, ALU.mult, ALU.add).then_inc(x_chain, 1)
            v.wait_ge(x_chain, 2)
            nc.vector.reciprocal(rv[:, 0:10], var[:, 0:10]).then_inc(rstd_done, 1)
            rsqrt_dve(v, (0, 10), 2, sq_done, 1)
            v.wait_ge(g_in, 16 * 11)
            for t in range(11):
                if t < 10:
                    n = XROWS[t]
                    nc.vector.scalar_tensor_tensor(xt[t][0:n, :], xt[t][0:n, :], rstd[0:n, t:t + 1], gpre[0:n, :],
                                                   ALU.mult, ALU.mult).then_inc(xs_done, 1)
                if t >= 1:
                    s, n, c0 = t - 1, XROWS[t - 1], XCOL[t - 1]
                    for h in range(2):
                        v.wait_ge(x_hi, 2 * s + h + 1)
                        nc.vector.tensor_tensor(Xl3[:, 4 * h:4 * h + 4, c0:c0 + n], four(tp[h])[:, :, 0:n],
                                                Xh3[:, 4 * h:4 * h + 4, c0:c0 + n].bitcast(F32),
                                                ALU.subtract).then_inc(tp_free[h], 1)

        def norm_pe(pe):
            pe.wait_ge(cst_in, 32)
            for t in range(10):
                if t in (4, 7):
                    c = (t - 4) // 3
                    for h in range(2):
                        pe.wait_ge(tp_free[h], t)
                    gemm(pe, Unit(0), c, CHUNK_ALL[c])
                n = XROWS[t]
                pe.wait_ge(xs_done, t + 1)
                for h in range(2):
                    if t:
                        pe.wait_ge(tp_free[h], t)
                    for j in range(4):
                        k = 4 * h + j
                        last = nc.tensor.transpose(four(tp[h])[:, j, 0:n], xt[t][0:n, k * P:(k + 1) * P], ident[0:n, 0:n])
                    last.then_inc(tp_full, 1)
            for h in range(2):
                pe.wait_ge(tp_free[h], 10)
            gemm(pe, Unit(0), 2, CHUNK_ALL[2])

        NORM_R = 20

        class Count:

            def __init__(self, b, per=0, it=0):
                self.slot = b % 2
                self.n = b + per * it if per else b
                self.half = b // 2 + (per // 2) * it if per else b // 2

        def later(base, d):
            return Count(base[0] + d, base[1], base[2])

        def positive(x):
            return not isinstance(x, int) or x > 0

        def round_fill(pe, R, blocks, n=P, m=P):
            if positive(R.half):
                pe.wait_ge(tp_free[R.slot], R.half)
            for j, src in enumerate(blocks):
                last = nc.tensor.transpose(four(tp[R.slot])[0:n, j, 0:m], src, ident[0:m, 0:m])
            last.then_inc(tp_full, 1)

        def round_read(eng, R):
            eng.wait_ge(tp_free[R.slot], R.half + 1)

        def rounds_read(eng, Rs):
            last = [(R.slot, at(eng, R.half + 1)) for R in list({R.slot: R for R in Rs}.values())]
            apart(eng)
            for slot, n in last:
                eng.wait_ge(tp_free[slot], n)

        def chunk_slot(pe, C):
            if positive(C.n) and not (isinstance(C.n, int) and C.n < 2):
                pe.wait_ge(sc_free, C.n - 1)
            return sc[C.slot]

        lz, le, lw_, ll, ld = (t[0:8, 0:NT] for t in (qcur, kcur, nB, nC, ktm))

        def lf_dve_z(v, c):
            a, b = CHUNK_ALL[c]
            gemm_wait(v, Unit(U_F), c)
            nc.vector.tensor_scalar(lz[:, a:b], gb[c][0:8, 0:b - a], bf, None, ALU.add).then_inc(bank_free[c], 1)

        def lf_dve(v):
            for c in range(3):
                v.wait_ge(bank_free[c], 1)
            nc.vector.scalar_tensor_tensor(le, lz, -1.0, lz, ALU.mult, ALU.min).then_inc(lf_chain, 1)
            v.wait_ge(lf_act, 1)
            nc.vector.tensor_scalar(lw_, le, 1.0, None, ALU.add).then_inc(lf_chain, 1)
            v.wait_ge(lf_chain, 2)
            nc.vector.scalar_tensor_tensor(ld, lw_, -1.0, le, ALU.add, ALU.subtract).then_inc(lf_chain, 1)
            v.wait_ge(lf_act, 2)
            v.wait_ge(lf_chain, 3)
            nc.vector.reciprocal(le, lw_).then_inc(lf_chain, 1)
            v.wait_ge(lf_chain, 4)
            nc.vector.tensor_tensor(ld, ld, le, ALU.mult).then_inc(lf_chain, 1)
            nc.vector.scalar_tensor_tensor(lz, lz, 0.0, ll, ALU.min, ALU.subtract).then_inc(lf_chain, 1)
            v.wait_ge(lf_chain, 6)
            nc.vector.tensor_tensor(lfq[:, :], lz, ld, ALU.add).then_inc(lf_chain, 1)
            v.wait_ge(lf_chain, 7)
            nc.vector.memset(PT[0][0:8, 0:KEYS], 1.0).then_inc(lf_chain, 1)
            v.wait_ge(lf_chain, 8)
            nc.vector.tensor_tensor_scan(cum_lf[:, 0:KEYS], PT[0][0:8, 0:KEYS], lfq[:, 0:KEYS], 0.0,
                                         ALU.mult, ALU.add).then_inc(lf_done, 1)


        def lf_act_(act):
            act.wait_ge(lf_chain, 1)
            nc.scalar.activation(le, le, ACT.Exp).then_inc(lf_act, 1)
            act.wait_ge(lf_chain, 2)
            nc.scalar.activation(ll, lw_, ACT.Ln).then_inc(lf_act, 1)

        def unit_read(eng, U):
            n = at(eng, U.n + 1)
            apart(eng)
            for c in range(3):
                eng.wait_ge(bank_free[c], n)

        def q_read(act, U, c, p):
            if c == 0 and positive(p):
                act.wait_ge(cur_copied, p * 6)
            a, b = CHUNK_ALL[c]
            gemm_wait(act, U, c)
            nc.scalar.activation(nA[:, a:b], gb[c][:, 0:b - a], ACT.Copy, scale=SCALE).then_inc(bank_free[c], 1)

        def kv_read(v, U, c, p, dst, first_round):
            if c == 0 and positive(p):
                v.wait_ge(cur_copied, p * 6)
                v.wait_ge(tp_full, p * FR + (FOX_RB - FR + first_round + 3))
            a, b = CHUNK_ALL[c]
            gemm_wait(v, U, c)
            nc.vector.tensor_copy(dst[:, a:b], gb[c][:, 0:b - a]).then_inc(bank_free[c], 1)

        def gate_act(act, U, c, g):
            if c == 0 and positive(g):
                act.wait_ge(sig_out, g * 16)
            gemm_wait(act, U, c)
            nc.scalar.activation(sig[:, 384 * c:384 * c + 384], gb[c][:, 0:384], ACT.Exp,
                                 scale=-1.0).then_inc(bank_free[c], 1)

        def gate_dve(v, U, c, g):
            s_ = sig[:, 384 * c:384 * c + 384]
            v.wait_ge(bank_free[c], U.n + 1)
            nc.vector.tensor_scalar(s_, s_, 1.0, None, ALU.add).then_inc(gate_1, 1)
            v.wait_ge(gate_1, g * 3 + (c + 1))
            nc.vector.reciprocal(s_, s_).then_inc(sig_done, 1)

        def gate_store(sp, g):
            sp.wait_ge(sig_done, g * 3 + 3)
            dst = sig_scr[g * P:g * P + P, :] if isinstance(g, int) else sig_scr[bass.ds(g * P, P), :]
            sp.dma_start(dst, sig[:, :]).then_inc(sig_out, 16)

        def rope_act(act, U, c, m, scale):
            a, b = CHUNK_ALL[c]
            gemm_wait(act, U, c)
            if positive(m):
                act.wait_ge(rope_b, m)
            for h in range(4):
                o = h ^ 1
                nc.scalar.activation(sh[32 * h:32 * h + 32, 0:b - a], gb[c][32 * o:32 * o + 32, 0:b - a],
                                     ACT.Copy, scale=scale).then_inc(rope_sh, 1)

        def rope_dve(v, U, c, m, scale, dst):
            a, b = CHUNK_ALL[c]
            v.wait_ge(rope_sh, m * 4 + 4)
            nc.vector.scalar_tensor_tensor(dst[:, a:b], gb[c][:, 0:b - a], scale, nB[:, a:b],
                                           ALU.mult, ALU.mult).then_inc(bank_free[c], 1)

        def rope_pool(pool, U, c, m, dst):
            a, b = CHUNK_ALL[c]
            pool.wait_ge(rope_sh, m * 4 + 4)
            nc.gpsimd.tensor_tensor(sh[:, 0:b - a], sh[:, 0:b - a], nC[:, a:b], ALU.mult).then_inc(rope_a, 1)
            pool.wait_ge(rope_a, m + 1)
            pool.wait_ge(bank_free[c], U.n + 1)
            nc.gpsimd.tensor_tensor(dst[:, a:b], dst[:, a:b], sh[:, 0:b - a], ALU.add).then_inc(rope_b, 1)

        FOX_RB = NORM_R
        SWA_RB = FOX_RB + 4 * FR + 4
        SWA_CB = 4 * FC
        SAM_RB, SAM_CB = SWA_RB + 4 * SIDE, SWA_CB + 4 * SIDE

        class Fox:

            fox = True

            def __init__(self, p, it=None):
                self.p = p if it is None else it
                self.it = it
                self.N = self.p * SIDE

            def chunk(self, d):
                return Count(d, FC, self.it) if self.it is not None else Count(FC * self.p + d)

            def round(self, d):
                return Count(FOX_RB + d, FR, self.it) if self.it is not None else Count(FOX_RB + FR * self.p + d)

            def chunks(self, n):
                return [(self.chunk(FOX_C[n] + j), a, b) for j, (a, b) in enumerate(fox_chunks(n % 8))]

            def rounds(self, n):
                return [(self.round(FOX_R[n] + j), a, b) for j, (a, b) in enumerate(fox_rounds(n % 8))]

            def blocks(self, n):
                h, i = divmod(n, 8)
                return [(k, P * j, vcur[0:k, P * j + DH * h:P * j + DH * h + DH])
                        for j, k in enumerate([P] * (i + 1) + [META])]

        class Swa:

            fox = False

            def __init__(self, r, it=None):
                self.p = r if it is None else it
                self.it = it
                self.N = self.p * SIDE + 4 * SIDE

            def chunk(self, d):
                return Count(SWA_CB + d, SIDE, self.it) if self.it is not None else Count(SWA_CB + SIDE * self.p + d)

            def round(self, d):
                return Count(SWA_RB + d, SIDE, self.it) if self.it is not None else Count(SWA_RB + SIDE * self.p + d)

            def chunks(self, n):
                return [(self.chunk(n), 0, META + P if n % 8 == 0 else META + 2 * P)]

            def rounds(self, n):
                return [(self.round(n), 0, 2 if n % 8 == 0 else 3)]

            def blocks(self, n):
                h, i = divmod(n, 8)
                c0 = DH * h
                out = [(META, 0, vball[0:META, c0:c0 + DH])]
                for j, t in enumerate([0] if i == 0 else [i - 1, i]):
                    out.append((P, META + P * j, vball[:, P * (t + 1) + c0:P * (t + 1) + c0 + DH]))
                return out

        def item_scores(pe, A_, n):
            h, i = divmod(n, 8)
            hp = slice(DH * h, DH * h + DH)
            q_ = qcur[hp, META + P * i:META + P * i + P]
            for C, a, b in A_.chunks(n):
                bank = chunk_slot(pe, C)
                if A_.fox:
                    diag = b == META + P * (i + 1)
                    last = nc.tensor.matmul(bank[:, 0:b - a], q_, kcur[hp, a:b], start=True, stop=not diag)
                    if diag:
                        last = nc.tensor.matmul(bank[:, b - a - P:b - a], ident_r[:, :], mask_r[:, :],
                                                start=False, stop=True)
                elif i == 0:
                    last = nc.tensor.matmul(bank[:, 0:b], q_, kbT[hp, 0:b], start=True, stop=True)
                else:
                    nc.tensor.matmul(bank[:, 0:META], q_, kbT[hp, 0:META], start=True, stop=True)
                    s0 = META + P * (i - 1)
                    last = nc.tensor.matmul(bank[:, META:b], q_, kbT[hp, s0:s0 + 2 * P], start=True, stop=True)
                last.then_inc(sc_full, 1)

        def item_max(v, A_, n):
            h, i = divmod(n, 8)
            ms, us, parts = 3 * (n % 4), u[n % 2], A_.chunks(n)
            full = [at(v, C.n + 1) for C, _, _ in parts]
            turned = at(v, A_.round(0).n if n < 2 else A_.rounds(n - 2)[-1][0].n + 1)
            if n == 0:
                ready = at(v, A_.chunk(6).n if A_.fox else A_.p * 3 + 3)
            apart(v)
            v.wait_ge(tp_full, turned)
            if n == 0 and A_.fox:
                v.wait_ge(sc_free, ready)
            if n == 0 and not A_.fox:
                v.wait_ge(swa_cur, ready)
            for j, (C, a, b) in enumerate(parts):
                if j:
                    apart(v)
                v.wait_ge(sc_full, full[j])
                bias = ckb[h][:, a:b] if A_.fox else cst[:, C_BAND0:C_BAND0 + b] if i == 0 else cst[:, C_BAND:C_BAND + b]
                init = -3e38 if A_.fox else sinkcur[:, h:h + 1]
                nc.vector.tensor_tensor_reduce(us[:, a:b], sc[C.slot][:, 0:b - a], bias, 1.0, init, ALU.subtract,
                                               ALU.max, mx[:, ms + j:ms + j + 1]).then_inc(sc_free, 1)
            v.wait_ge(sc_free, parts[-1][0].n + 1)
            nc.vector.tensor_reduce(nm[:, n % 4:n % 4 + 1], mx[:, ms:ms + len(parts)], AX_X, ALU.max,
                                    negate=True).then_inc(nm_done, 1)

        def item_exp(act, A_, n):
            w = A_.chunks(n)[-1][2]
            us, m = u[n % 2][:, 0:w], nm[:, n % 4:n % 4 + 1]
            act.wait_ge(nm_done, A_.N + (n + 1))
            nc.scalar.activation(us, us, ACT.Exp, bias=m, accum_out=ssum[:, n % 4:n % 4 + 1]).then_inc(p_done, 1)
            if not A_.fox:
                h = n // 8
                nc.scalar.activation(esink[:, n % 4:n % 4 + 1], sinkcur[:, h:h + 1], ACT.Exp, bias=m).then_inc(es_done, 1)

        def item_inv(v, A_, n):
            s_ = slice(n % 4, n % 4 + 1)
            v.wait_ge(p_done, A_.N + (n + 1))
            if not A_.fox:
                t_ = slice(4 + n % 4, 5 + n % 4)
                v.wait_ge(es_done, A_.p * SIDE + (n + 1))
                nc.vector.tensor_tensor(ssum[:, t_], ssum[:, s_], esink[:, s_], ALU.add).then_inc(tot_done, 1)
                v.wait_ge(tot_done, A_.p * SIDE + (n + 1))
                s_ = t_
            nc.vector.reciprocal(rinv[:, n % 4:n % 4 + 1], ssum[:, s_]).then_inc(sum_inv, 1)

        def item_turn(pe, A_, n):
            pe.wait_ge(p_done, A_.N + (n + 1))
            bl = A_.blocks(n)
            for R, a, b in A_.rounds(n):
                round_fill(pe, R, [u[n % 2][:, c0:c0 + P] for _, c0, _ in bl[a:b]])

        def item_turned(act, A_, n):
            if positive(A_.N) or n >= 2:
                act.wait_ge(pv_done, A_.N + (n - 1))
            for R, a, b in A_.rounds(n):
                act.wait_ge(tp_full, R.n + 1)
                nc.scalar.activation(PT[n % 2][:, P * a:P * b], tp[R.slot][:, 0:P * (b - a)],
                                     ACT.Copy).then_inc(tp_free[R.slot], 1)

        def item_values(pe, A_, n):
            rounds_read(pe, [R for R, _, _ in A_.rounds(n)])
            if positive(A_.N) or n >= 1:
                pe.wait_ge(o_done, A_.N + n)
            bl = A_.blocks(n)
            for j, (k, _, val) in enumerate(bl):
                last = nc.tensor.matmul(po[:, 0:DH], PT[n % 2][0:k, P * j:P * j + P], val,
                                        start=(j == 0), stop=(j == len(bl) - 1))
            last.then_inc(pv_done, 1)

        def item_out(v, A_, n):
            h, i = divmod(n, 8)
            v.wait_ge(pv_done, A_.N + (n + 1))
            v.wait_ge(sum_inv, A_.N + (n + 1))
            if n == 0:
                if not A_.fox:
                    v.wait_ge(o_out, A_.p * 32 + 64)
                elif positive(A_.p):
                    v.wait_ge(o_out, A_.p * 16)
            nc.vector.tensor_scalar(opair[:, P * i + DH * h:P * i + DH * h + DH], po[:, 0:DH],
                                    rinv[:, n % 4:n % 4 + 1], None, ALU.mult).then_inc(o_done, 1)

        STEPS = SIDE + 3

        def spread(jobs):
            at = {11: [0, 1, 3, 5, 6, 8, 10, 12, 14, 16, 17], 6: [1, 4, 7, 10, 13, 17], 3: [3, 10, 17]}[len(jobs)]
            return dict(zip(at, jobs))

        def steps_pe(pe, A_, jobs):
            for s in range(STEPS):
                if 0 <= s - 2 < SIDE:
                    item_turn(pe, A_, s - 2)
                if s < SIDE:
                    item_scores(pe, A_, s)
                if s in jobs:
                    jobs[s](pe)
                if 0 <= s - 3 < SIDE:
                    item_values(pe, A_, s - 3)

        def steps_act(act, A_, jobs):
            for s in range(STEPS):
                if 0 <= s - 2 < SIDE:
                    item_turned(act, A_, s - 2)
                if s < SIDE:
                    item_exp(act, A_, s)
                if s in jobs:
                    jobs[s](act)

        def steps_dve(v, A_, jobs):
            for s in range(STEPS):
                if s < SIDE:
                    item_max(v, A_, s)
                if 0 <= s - 1 < SIDE:
                    item_inv(v, A_, s - 1)
                if 0 <= s - 3 < SIDE:
                    item_out(v, A_, s - 3)
                if s in jobs:
                    jobs[s](v)

        CKB = [(h, a, b) for h in range(2) for a, b in ((0, 400), (400, 912), (912, KEYS))]
        KVB = [P * j for j in range(9)] + [S0]

        def part(t, reg, size, c0=0):
            if isinstance(reg, int):
                return t[:, c0 + reg * size:c0 + reg * size + size]
            return t[:, bass.ds(reg * size + c0, size)]

        def ahead(U):
            V = Unit(0)
            V.n, V.slot, V.nth = U.n + 2, U.slot, U.nth + 1
            return V

        class FoxStep:

            def __init__(self, p, it=None):
                self.A = Fox(p, it)
                b = U_FOX if it is not None else U_FOX + 4 * p
                mk = (lambda n: Unit(n, 4, it)) if it is not None else Unit
                self.new = [mk(b + j) for j in range(4)]
                self.own = [mk(b - 3 + j) for j in range(3)]
                self.p = self.A.p
                self.last = it is None and p == 3

        FOX_JOBS = [(0, 1), (0, 2)] + [(j, c) for j in range(1, 4) for c in range(3)]

        def fox_setup_pe(pe, S):
            A_ = S.A
            pe.wait_ge(cur_copied, A_.p * 6 + 1)
            pe.wait_ge(lf_done, 1)
            for m, (h, a, b) in enumerate(CKB):
                bank = chunk_slot(pe, A_.chunk(m))
                nc.tensor.matmul(bank[:, 0:b - a], selcur[:, P * h:P * h + P], cum_lf[:, a:b],
                                 start=True, stop=True).then_inc(sc_full, 1)
            for src, r0, U in ((nC, 0, S.own[2]), (nB, 3, S.own[1])):
                unit_read(pe, U)
                for j in range(3):
                    round_fill(pe, A_.round(r0 + j), [src[:, c0:c0 + P] for c0 in KVB[4 * j:4 * j + 4]])
            pe.wait_ge(cur_copied, A_.p * 6 + 3)

        def fox_setup_dve(v, S):
            A_ = S.A
            for m, (h, a, b) in enumerate(CKB):
                C = A_.chunk(m)
                v.wait_ge(sc_full, C.n + 1)
                nc.vector.tensor_copy(ckb[h][:, a:b], sc[C.slot][:, 0:b - a]).then_inc(sc_free, 1)
            if positive(A_.p):
                v.wait_ge(kv_out, A_.p * 96)
                v.wait_ge(pv_done, A_.N)
            for j in range(3):
                R = A_.round(j)
                w = P * len(KVB[4 * j:4 * j + 4])
                v.wait_ge(tp_full, R.n + 1)
                nc.vector.tensor_copy(vcur[:, 512 * j:512 * j + w], tp[R.slot][:, 0:w]).then_inc(tp_free[R.slot], 1)

        def fox_setup_act(act, S):
            A_ = S.A
            if positive(A_.p):
                act.wait_ge(kv_out, A_.p * 96)
            act.wait_ge(lf_done, 1)
            for j in range(3):
                R = A_.round(3 + j)
                w = P * len(KVB[4 * j:4 * j + 4])
                act.wait_ge(tp_full, R.n + 1)
                nc.scalar.activation(ktm[:, 512 * j:512 * j + w], tp[R.slot][:, 0:w],
                                     ACT.Copy).then_inc(tp_free[R.slot], 1)

        def fox_setup_pool(pool, S):
            A_ = S.A
            if positive(A_.p):
                pool.wait_ge(sc_full, A_.chunk(0).n)
            pool.wait_ge(lf_done, 1)
            nc.gpsimd.tensor_copy(selcur[:, :], part(cst[0:8, :], A_.p, 2 * P, C_SEL)).then_inc(cur_copied, 1)
            for U, src, dst in ((S.own[0], nA, qcur), (S.own[1], nB, kcur)):
                unit_read(pool, U)
                nc.gpsimd.tensor_copy(dst[:, :], src[:, :]).then_inc(cur_copied, 1)
            unit_read(pool, S.own[2])
            for src, dst in ((nA, qTs), (nB, kTs), (nC, vTs)):
                nc.gpsimd.tensor_copy(part(dst, A_.p, P), src[:, S0:S0 + P]).then_inc(cur_copied, 1)

        def fox_store_kv(sp, A_):
            for tm, first, p_out, s_out in ((vcur, 0, "fox_v_p", "fox_v_s"), (ktm, 3, "fox_k_p", "fox_k_s")):
                rounds_read(sp, [A_.round(first + j) for j in range(3)])
                full = part(O[p_out][0:SEQ, :], A_.p, P).rearrange("(j t) n -> t j n", t=P)
                sp.dma_start(full, tm[:, 0:SEQ].rearrange("t (j n) -> t j n", j=8)).then_inc(kv_out, 16)
                sp.dma_start(part(O[p_out][SEQ:KEYS, :], A_.p, P), tm[0:META, SEQ:SEQ + P]).then_inc(kv_out, 16)
                sp.dma_start(part(O[s_out], A_.p, P), tm[:, 9 * P:10 * P]).then_inc(kv_out, 16)

        opair3 = opair[:, :].rearrange("t (i n) -> t i n", i=8)

        def fox_store_o(sp, p):
            sp.wait_ge(o_done, p * SIDE + SIDE)
            sp.dma_start(part(o_scr, p, P).rearrange("(i t) n -> t i n", t=P), opair3).then_inc(o_out, 16)

        def swa_store_o(sp, r):
            sp.wait_ge(o_done, r * SIDE + 5 * SIDE)
            for g in range(2):
                sp.dma_start(part(o_scr, r, DH, FOX_W + g * 4 * DH).rearrange("(i t) n -> t i n", t=P),
                             opair3[:, :, DH * g:DH * g + DH]).then_inc(o_out, 16)

        def fox_step_pe(pe, S):
            gemm(pe, S.new[0], 0, CHUNK_TOK[0])
            fox_setup_pe(pe, S)
            steps_pe(pe, S.A, spread([lambda e, j=j, c=c: gemm(e, S.new[j], c, CHUNK_ALL[c] if j else CHUNK_TOK[c])
                                      for j, c in FOX_JOBS]))

        def fox_step_act(act, S):
            gate_act(act, S.new[0], 0, S.p)
            fox_setup_act(act, S)

            def job(j, c):
                def run(e):
                    if j == 0:
                        gate_act(e, S.new[0], c, S.p)
                    elif j == 1 and not S.last:
                        q_read(e, S.new[1], c, S.p + 1)
                    elif j == 1:
                        rope_act(e, S.new[1], c, c, 1.0)
                    elif j == 3 and S.last:
                        rope_act(e, S.new[3], c, 3 + c, SCALE)
                    if c == 2:
                        hi(e, ahead(S.new[j]))
                return run
            steps_act(act, S.A, spread([job(j, c) for j, c in FOX_JOBS]))

        def fox_step_dve(v, S):
            gate_dve(v, S.new[0], 0, S.p)
            fox_setup_dve(v, S)

            def job(j, c):
                def run(e):
                    if j == 0:
                        gate_dve(e, S.new[0], c, S.p)
                    elif not S.last:
                        if j > 1:
                            kv_read(e, S.new[j], c, S.p + 1, (nB, nC)[j - 2], (3, 0)[j - 2])
                    elif j == 1:
                        e.wait_ge(tab_in, 32)
                        rope_dve(e, S.new[1], c, c, 1.0, kbT)
                    elif j == 3:
                        e.wait_ge(cur_copied, 4 * 6)
                        rope_dve(e, S.new[3], c, 3 + c, SCALE, nA)
                    else:
                        a, b = CHUNK_ALL[c]
                        e.wait_ge(kv_out, 4 * 96)
                        gemm_wait(e, S.new[2], c)
                        nc.vector.tensor_copy(ktm[:, a:b], gb[c][:, 0:b - a]).then_inc(bank_free[c], 1)
                return run
            steps_dve(v, S.A, spread([job(j, c) for j, c in FOX_JOBS]))

        def fox_step_pool(pool, S):
            fox_setup_pool(pool, S)
            for j in range(4):
                if S.last and j in (1, 3):
                    if j == 1:
                        pool.wait_ge(tab_in, 32)
                    for c in range(3):
                        rope_pool(pool, S.new[j], c, j // 3 * 3 + c, kbT if j == 1 else nA)
                lo(pool, ahead(S.new[j]))

        def fox_step_sp(sp, S):
            if S.last:
                parts = [cols_of(I["w_in"], COL_KB), cols_of(I["w_in"], COL_VB), cols_qb(0)]
            else:
                parts = [cols_of(I["w_in"], c0 + P, S.p, P) for c0 in (COL_QA, COL_KA, COL_VA)]
            load(sp, S.new[1], parts[0])
            fox_store_kv(sp, S.A)
            if S.last:
                sp.wait_ge(cur_copied, 4 * 6)
                sp.wait_ge(tp_full, S.A.round(6).n)
                sp.dma_start(nB[:, :], I["cos"]).then_inc(tab_in, 16)
                sp.dma_start(nC[:, :], I["sin"]).then_inc(tab_in, 16)
            load(sp, S.new[2], parts[1])
            gate_store(sp, S.p)
            load(sp, S.new[3], parts[2])
            load(sp, ahead(S.new[2]), cols_gate(1, S.p, 1) if not S.last else cols_gate(4))
            if S.last:
                load(sp, ahead(S.new[3]), cols_qb(1))
            fox_store_o(sp, S.p)

        def swa_pre_pe(pe):
            unit_read(pe, Unit(U_PEEL + 2))
            pe.wait_ge(rope_b, 3)
            vcols = [0] + [META + P * t for t in range(8)] + [S0]
            src = [ktm[:, c:c + P] for c in vcols] + [kbT[:, S0 - P:S0], kbT[:, S0:S0 + P]]
            for j in range(3):
                round_fill(pe, Count(SWA_RB - 4 + j), src[4 * j:4 * j + 4])
            R = Count(SWA_RB - 1)
            pe.wait_ge(tp_free[R.slot], R.half)
            for j, c0 in enumerate(KVB):
                last = nc.tensor.transpose(tp[R.slot][:, 8 * j:8 * j + 8], lfq[:, c0:c0 + P], ident[0:8, 0:8])
            last.then_inc(tp_full, 1)

        def swa_pre_act(act):
            for j in range(3):
                R = Count(SWA_RB - 4 + j)
                act.wait_ge(tp_full, R.n + 1)
                nc.scalar.activation(vball[:, 512 * j:512 * j + 512], tp[R.slot][:, :], ACT.Copy).then_inc(tp_free[R.slot], 1)
            R = Count(SWA_RB - 1)
            act.wait_ge(tp_full, R.n + 1)
            act.wait_ge(kv_out, 4 * 96)
            act.wait_ge(pv_done, 4 * SIDE)
            nc.scalar.activation(vcur[:, 0:80], tp[R.slot][:, 0:80], ACT.Copy).then_inc(tp_free[R.slot], 1)

        def swa_pre_pool(pool):
            unit_read(pool, Unit(U_PEEL + 2))
            nc.gpsimd.tensor_copy(vbs[:, :], ktm[:, S0:S0 + P]).then_inc(vb_done, 1)

        def swa_pre_sp(sp):
            for j in range(4):
                round_read(sp, Count(SWA_RB - 4 + j))
            for name, b in (("swa_v_p", 8), ("swa_v_s", 9), ("swa_k_p", 10), ("swa_k_s", 11)):
                sp.dma_start(O[name], vball[:, P * b:P * b + P]).then_inc(kb_out, 16)
            sp.dma_start(O["fox_f_p"][0:SEQ, :].rearrange("(j t) h -> t j h", t=P),
                         vcur[:, 0:64].rearrange("t (j h) -> t j h", j=8)).then_inc(kb_out, 16)
            sp.dma_start(O["fox_f_p"][SEQ:KEYS, :], vcur[0:META, 64:72]).then_inc(kb_out, 16)
            sp.dma_start(O["fox_f_s"], vcur[:, 72:80]).then_inc(kb_out, 16)

        class SwaStep:

            def __init__(self, r, it=None):
                self.A = Swa(r, it)
                self.p = self.A.p
                b = U_SWA if it is not None else U_SWA + 2 * r
                self.new = [Unit(b + j, 2, it) if it is not None else Unit(b + j) for j in range(2)]
                self.last, self.first = it is None and r == 3, it is None and r == 0
                self.jobs = [(j, c) for j in range(1 if self.last else 2) for c in range(3)]

        def swa_setup_pool(pool, S):
            r = S.p
            ropes, scores, items = at(pool, r * 3 + 6), at(pool, S.A.chunk(0).n), at(pool, S.A.N)
            apart(pool)
            pool.wait_ge(rope_b, ropes)
            pool.wait_ge(sc_full, scores)
            pool.wait_ge(sc_free, scores)
            pool.wait_ge(o_done, items)
            nc.gpsimd.tensor_copy(qcur[:, :], nA[:, :]).then_inc(swa_cur, 1)
            rr = slice(r, r + 1) if isinstance(r, int) else bass.ds(r, 1)
            nc.gpsimd.tensor_copy(sinkcur.rearrange("p (o g) -> p o g", o=1),
                                  sinkb.rearrange("p (g r) -> p r g", g=2)[:, rr, :]).then_inc(swa_cur, 1)
            nc.gpsimd.tensor_copy(part(qbs, r, P), nA[:, S0:S0 + P]).then_inc(swa_cur, 1)

        def swa_step_pe(pe, S):
            pe.wait_ge(swa_cur, S.p * 3 + 3)
            steps_pe(pe, S.A, spread([lambda e, j=j, c=c: gemm(e, S.new[j], c, CHUNK_ALL[c] if j else CHUNK_TOK[c])
                                      for j, c in S.jobs]))

        def swa_step_act(act, S):
            def job(j, c):
                def run(e):
                    if j == 0:
                        gate_act(e, S.new[0], c, S.p + 4)
                    else:
                        rope_act(e, S.new[1], c, S.p * 3 + (6 + c), SCALE)
                    if c == 2:
                        hi(e, ahead(S.new[j]))
                return run
            steps_act(act, S.A, spread([job(j, c) for j, c in S.jobs]))

        def swa_step_dve(v, S):
            def job(j, c):
                def run(e):
                    if j == 0:
                        gate_dve(e, S.new[0], c, S.p + 4)
                    else:
                        e.wait_ge(swa_cur, S.p * 3 + 3)
                        rope_dve(e, S.new[1], c, S.p * 3 + (6 + c), SCALE, nA)
                return run
            steps_dve(v, S.A, spread([job(j, c) for j, c in S.jobs]))

        def swa_step_pool(pool, S):
            swa_setup_pool(pool, S)
            lo(pool, ahead(S.new[0]))
            if not S.last:
                for c in range(3):
                    rope_pool(pool, S.new[1], c, S.p * 3 + (6 + c), nA)
                lo(pool, ahead(S.new[1]))

        def swa_step_sp(sp, S):
            if S.last:
                load(sp, S.new[1], cols_gate(8))
            elif S.first:
                pass
            else:
                load(sp, S.new[1], cols_qb(S.p + 1))
            gate_store(sp, S.p + 4)
            load(sp, ahead(S.new[0]), cols_gate(9) if S.last else cols_gate(5, S.p, 1))
            swa_store_o(sp, S.p)

        SAM_ROUNDS = 10
        cfk = I["cache_fox_k"].rearrange("o b (t p) h d -> (o b) p t (h d)", p=P)
        cfv = I["cache_fox_v"].rearrange("o b (t p) h d -> (o b) p t (h d)", p=P)
        csk = I["cache_swa_k"].rearrange("o b p g d -> (o b) p (g d)")
        csv = I["cache_swa_v"].rearrange("o b p g d -> (o b) p (g d)")
        clg = I["cache_fox_logf"].rearrange("o b (t p) h -> (o b) p t h", p=P)
        clf4 = clf[:, :].rearrange("p (b t h) -> p b t h", b=STREAMS, t=4)
        osT3 = osT.rearrange("p (k n) -> p k n", k=8)

        class Sam:

            def __init__(self, it, e):
                self.b = it * 2 + e
                self.e, self.it = e, it

            def round(self, d):
                return Count(SAM_RB + SAM_ROUNDS * self.e + d, 2 * SAM_ROUNDS, self.it)

            def chunk(self, d):
                return Count(SAM_CB + 2 * self.e + d, 4, self.it)

        def b_cols(t, blocks, b):
            v = t.rearrange("p (k n) -> p k n", k=blocks)
            return v[:, :, bass.ds(b * NEW, NEW)]

        def sam_caches(sp, S):
            e = S.e
            sp.wait_ge(sam_free, S.b + 1)
            for dst, src in ((kc, cfk), (vc, cfv)):
                sp.dma_start(dst[e][:, :].rearrange("p (t n) -> p t n", t=4),
                             src[bass.ds(S.b, 1), :, :, :].rearrange("o p t n -> p (o t) n")).then_inc(c_in[e], 16)
            for dst, src in ((kw, csk), (vw, csv)):
                sp.dma_start(dst[e][:, :], src[bass.ds(S.b, 1), :, :].rearrange("o p n -> p (o n)")
                             ).then_inc(c_in[e], 16)
            sp.dma_start(clf[:, 32 * e:32 * e + 32].rearrange("p (t h) -> p t h", t=4),
                         clg[bass.ds(S.b, 1), :, :, :].rearrange("o p t h -> p (o t) h")).then_inc(c_in[e], 16)

        def sam_sp(sp, it):
            for e in range(2):
                S = Sam(it, e)
                last = isinstance(it, int)
                load(sp, ahead(Unit(U_SAM + e, 2, it)), mix_parts(e) if last else cols_gate(10 + e, it, 2))
                if not (last and e):
                    sam_caches(sp, Sam(it, 1) if e == 0 else Sam(it + 1, 0))
                gate_store(sp, S.b + 8)

        def sam_pool(pool, it):
            for e in range(2):
                S = Sam(it, e)
                used = at(pool, S.b + 2)
                apart(pool)
                pool.wait_ge(sam_free, used)
                kv3 = kvn[:, :].rearrange("p (k n) -> p k n", n=NEW)
                for dst, src in ((kv3[:, 0:4, :], b_cols(kTs[:, :], 4, S.b)), (kv3[:, 4:8, :], b_cols(vTs[:, :], 4, S.b)),
                                 (kv3[:, 8:9, :], b_cols(kbT[:, S0:S0 + P], 1, S.b)), (kv3[:, 9:10, :], b_cols(vbs[:, :], 1, S.b))):
                    nc.gpsimd.tensor_copy(dst, src).then_inc(s_stage, 1)
                qz3 = qz[:, :].rearrange("p (j n) -> p j n", j=4)
                qzs4 = qzs[:, :].rearrange("p (r g q) -> p r g q", r=4, g=2)
                for h in range(2):
                    hp = slice(DH * h, DH * h + DH)
                    if h:
                        staged = at(pool, S.b * 8 + 6)
                        apart(pool)
                        pool.wait_ge(s_stage, staged)
                    nc.gpsimd.tensor_copy(qz3[hp, :, NEW * h:NEW * h + NEW], b_cols(qTs[hp, :], 4, S.b)).then_inc(s_stage, 1)
                    nc.gpsimd.tensor_copy(qzs4[hp, :, h, :], b_cols(qbs[hp, :], 4, S.b)).then_inc(s_stage, 1)
                pool.wait_ge(s_stage, S.b * 8 + 8)
                lo(pool, ahead(Unit(U_SAM + e, 2, it)))

        def sam_pe(pe, it):
            for e in range(2):
                S = Sam(it, e)
                U = Unit(U_SAM + e, 2, it)
                gemm(pe, U, 0, CHUNK_TOK[0])
                pe.wait_ge(c_in[e], it * 80 + 80)
                for j in range(4):
                    round_fill(pe, S.round(j), [kc[e][:, 512 * t + P * j:512 * t + P * j + P] for t in range(4)])
                round_fill(pe, S.round(4), [kw[e][:, :]])
                R = S.round(5)
                pe.wait_ge(tp_free[R.slot], R.half)
                for t in range(4):
                    last = nc.tensor.transpose(tp[R.slot][0:8, P * t:P * t + P], clf[:, 32 * e + 8 * t:32 * e + 8 * t + 8], ident[:, :])
                last.then_inc(tp_full, 1)
                pe.wait_ge(s_stage, S.b * 8 + 8)
                for R, ks in ((S.round(6), range(4, 8)), (S.round(7), (9,))):
                    pe.wait_ge(tp_free[R.slot], R.half)
                    for t, k in enumerate(ks):
                        last = nc.tensor.transpose(tp[R.slot][0:NEW, P * t:P * t + P], kvn[:, NEW * k:NEW * k + NEW], ident[:, :])
                    last.then_inc(tp_full, 1)
                gemm(pe, U, 1, CHUNK_TOK[1])
                rounds_read(pe, [S.round(j) for j in range(5)])
                pe.wait_ge(s_cs, S.b * 2 + 2)
                bank = chunk_slot(pe, S.chunk(0))
                nsel = cst[0:8, C_NSEL:C_NSEL + P]
                nc.tensor.matmul(bank[:, :], nsel, cs[:, 0:512], start=True, stop=False)
                for j in range(4):
                    last = nc.tensor.matmul(bank[:, :], qz[:, P * j:P * j + P], KcT[:, 512 * j:512 * j + 512],
                                            start=False, stop=(j == 3))
                last.then_inc(sc_full, 1)
                bank = chunk_slot(pe, S.chunk(1))
                nc.tensor.matmul(bank[:, 0:NEW], nsel, cs[:, 512:528], start=True, stop=False)
                nc.tensor.matmul(bank[:, 0:NEW], ident[:, :], cst[:, C_NEW:C_NEW + NEW], start=False, stop=False)
                for j in range(4):
                    nc.tensor.matmul(bank[:, 0:NEW], qz[:, P * j:P * j + P], kvn[:, NEW * j:NEW * j + NEW],
                                     start=False, stop=(j == 3))
                for a, keys in ((32, kbT[:, 0:META]), (48, KwT[:, :]), (176, kvn[:, 8 * NEW:9 * NEW])):
                    last = nc.tensor.matmul(bank[:, a:a + keys.shape[1]], qzs[:, :], keys, start=True, stop=True)
                last.then_inc(sc_full, 1)
                gemm(pe, U, 2, CHUNK_TOK[2])
                pe.wait_ge(s_scl, S.b * 2 + 2)
                round_fill(pe, S.round(8), [Ps[:, P * t:P * t + P] for t in range(4)])
                round_fill(pe, S.round(9), [Ps[:, 512:640], Pw[:, 0:P], Pw[:, META:META + P], Pw[:, META + P:META + 2 * P]])
                rounds_read(pe, [S.round(j) for j in (6, 7, 8, 9)])
                pe.wait_ge(o_done, S.b * 6 + 8 * SIDE)
                for j in range(4):
                    for t in range(4):
                        nc.tensor.matmul(po[:, 32 * j:32 * j + 32], vc[e][:, 512 * t + P * j:512 * t + P * j + P],
                                         PTs[:, P * t + 32 * j:P * t + 32 * j + 32], start=(t == 0), stop=False)
                    nc.tensor.matmul(po[:, 32 * j:32 * j + 32], vn[:, P * j:P * j + P],
                                     PTs[0:NEW, 512 + 32 * j:512 + 32 * j + 32], start=False, stop=True)
                nc.tensor.matmul(po[:, P:2 * P], vball[0:META, 0:P], PTs[0:META, 5 * P:6 * P], start=True, stop=False)
                nc.tensor.matmul(po[:, P:2 * P], vw[e][:, :], PTs[:, 6 * P:7 * P], start=False, stop=False)
                nc.tensor.matmul(po[:, P:2 * P], vn[:, 4 * P:5 * P], PTs[0:NEW, 7 * P:8 * P],
                                 start=False, stop=True).then_inc(sam_free, 1)

        mxs, nms, sms, tots, invs = (small[:, a:b] for a, b in ((140, 143), (143, 145), (145, 149), (149, 151), (151, 153)))

        def sam_act(act, it):
            for e in range(2):
                S = Sam(it, e)
                U = Unit(U_SAM + e, 2, it)
                gate_act(act, U, 0, S.b + 8)
                for j, dst in ((0, KcT[:, 0:512]), (2, KcT[:, 1024:1536]), (4, KwT[:, :])):
                    R = S.round(j)
                    act.wait_ge(tp_full, R.n + 1)
                    nc.scalar.activation(dst, tp[R.slot][:, 0:dst.shape[1]], ACT.Copy).then_inc(tp_free[R.slot], 1)
                R = S.round(6)
                act.wait_ge(tp_full, R.n + 1)
                nc.scalar.activation(vn[:, 0:512], tp[R.slot][0:NEW, :], ACT.Copy).then_inc(tp_free[R.slot], 1)
                gate_act(act, U, 1, S.b + 8)
                act.wait_ge(s_red, S.b * 5 + 5)
                nc.scalar.activation(Ps[:, 0:512], sc[0][:, :], ACT.Exp, bias=nms[:, 0:1], accum_out=sms[:, 0:1]).then_inc(sc_free, 1)
                nc.scalar.activation(Ps[:, 512:528], sc[1][:, 0:NEW], ACT.Exp, bias=nms[:, 0:1], accum_out=sms[:, 1:2]).then_inc(s_exp, 1)
                nc.scalar.activation(Pw[:, 0:160], sc[1][:, 32:192], ACT.Exp, bias=nms[:, 1:2], accum_out=sms[:, 2:3]).then_inc(sc_free, 1)
                nc.scalar.activation(sms[:, 3:4], sinkrow, ACT.Exp, bias=nms[:, 1:2]).then_inc(s_exp, 1)
                gate_act(act, U, 2, S.b + 8)
                hi(act, ahead(U))
                R = S.round(8)
                act.wait_ge(tp_full, R.n + 1)
                nc.scalar.activation(PTs[:, 0:512], tp[R.slot][:, :], ACT.Copy).then_inc(tp_free[R.slot], 1)

        def sam_dve(v, it):
            for e in range(2):
                S = Sam(it, e)
                U = Unit(U_SAM + e, 2, it)
                gate_dve(v, U, 0, S.b + 8)
                for j in (1, 3):
                    R = S.round(j)
                    v.wait_ge(tp_full, R.n + 1)
                    nc.vector.tensor_copy(KcT[:, 512 * j:512 * j + 512], tp[R.slot][:, :]).then_inc(tp_free[R.slot], 1)
                R = S.round(5)
                v.wait_ge(tp_full, R.n + 1)
                nc.vector.tensor_tensor_scan(cs[:, 0:512], one8[:, :], tp[R.slot][0:8, :], 0.0,
                                             ALU.mult, ALU.add).then_inc(tp_free[R.slot], 1)
                round_read(v, R)
                nc.vector.tensor_copy(lf16[:, :], lfq[:, bass.ds(S.b * NEW + S0, NEW)]).then_inc(s_cs, 1)
                v.wait_ge(s_cs, S.b * 2 + 1)
                nc.vector.tensor_tensor_scan(cs[:, 512:528], one8[:, 0:NEW], lf16[:, :], cs[:, 511:512],
                                             ALU.mult, ALU.add).then_inc(s_cs, 1)
                R = S.round(7)
                v.wait_ge(tp_full, R.n + 1)
                nc.vector.tensor_copy(vn[:, 512:640], tp[R.slot][0:NEW, 0:P]).then_inc(tp_free[R.slot], 1)
                gate_dve(v, U, 1, S.b + 8)
                v.wait_ge(sc_full, S.chunk(0).n + 1)
                nc.vector.tensor_reduce(mxs[:, 0:1], sc[0][:, :], AX_X, ALU.max).then_inc(s_red, 1)
                v.wait_ge(sc_full, S.chunk(1).n + 1)
                nc.vector.tensor_reduce(mxs[:, 1:2], sc[1][:, 0:NEW], AX_X, ALU.max).then_inc(s_red, 1)
                nc.vector.tensor_reduce(mxs[:, 2:3], sc[1][:, 32:192], AX_X, ALU.max).then_inc(s_red, 1)
                v.wait_ge(s_red, S.b * 5 + 3)
                nc.vector.tensor_reduce(nms[:, 0:1], mxs[:, 0:2], AX_X, ALU.max, negate=True).then_inc(s_red, 1)
                nc.vector.tensor_scalar(nms[:, 1:2], mxs[:, 2:3], sinkrow, -1.0, ALU.max, ALU.mult).then_inc(s_red, 1)
                v.wait_ge(sc_free, S.chunk(1).n + 1)
                v.wait_ge(s_exp, S.b * 2 + 2)
                nc.vector.tensor_tensor(tots[:, 0:1], sms[:, 0:1], sms[:, 1:2], ALU.add).then_inc(s_sum, 1)
                nc.vector.tensor_tensor(tots[:, 1:2], sms[:, 2:3], sms[:, 3:4], ALU.add).then_inc(s_sum, 1)
                v.wait_ge(s_sum, S.b * 3 + 2)
                nc.vector.reciprocal(invs, tots).then_inc(s_sum, 1)
                v.wait_ge(s_sum, S.b * 3 + 3)
                nc.vector.tensor_scalar(Ps[:, 0:528], Ps[:, 0:528], invs[:, 0:1], None, ALU.mult).then_inc(s_scl, 1)
                nc.vector.tensor_scalar(Pw[:, 0:160], Pw[:, 0:160], invs[:, 1:2], None, ALU.mult).then_inc(s_scl, 1)
                gate_dve(v, U, 2, S.b + 8)
                R = S.round(9)
                v.wait_ge(tp_full, R.n + 1)
                nc.vector.tensor_copy(PTs[:, 512:1024], tp[R.slot][:, :]).then_inc(tp_free[R.slot], 1)
                v.wait_ge(sam_free, S.b + 3)
                pf = po[:, 0:P].rearrange("p (j h q) -> p j h q", j=4, h=2)
                pw = po[:, P:2 * P].rearrange("p (a s g q) -> p a s g q", a=2, s=2, g=2)
                for h in range(2):
                    hp = slice(DH * h, DH * h + DH)
                    nc.vector.tensor_copy(osT3[hp, 0:4, bass.ds(S.b * NEW, NEW)], pf[hp, :, h, :]).then_inc(o_done, 1)
                for g in range(2):
                    for s in range(2):
                        nc.vector.tensor_copy(osT3[DH * s:DH * s + DH, 4 + 2 * g:6 + 2 * g, bass.ds(S.b * NEW, NEW)],
                                              pw[DH * g:DH * g + DH, :, s, g, :]).then_inc(o_done, 1)

        MIX_RB = SAM_RB + 8 * SAM_ROUNDS
        MIX_G = 3 * U_MIX
        OREADY = 8 * SIDE + 6 * STREAMS

        def mix_parts(f, reg=None):
            out = []
            for j, w in enumerate(("w_o_fox", "w_o_swa")):
                v = I[w].rearrange("(k p) n -> p k n", p=P)
                cs_ = slice(f * P, f * P + P) if reg is None else bass.ds(reg * (2 * P) + f * P, P)
                out.append((lambda d, j=j: d[:, 4 * j:4 * j + 4, :], v[:, :, cs_]))
            return out

        def enter_mix(eng):
            eng.wait_ge(gemm_done, MIX_G)
            eng.wait_ge(o_done, OREADY)

        def mix_load(sp, f):
            if f >= 2:
                sp.wait_ge(tp_full, MIX_RB + 2 * (f - 1))
            sp.dma_start(ot[f % 2][:, :], o_scr[P * f:P * f + P, :]).then_inc(o_in[f % 2], 16)

        def sg_load(sp, s, f, reg=None):
            for dst, base in ((sga, 0), (sgb, D)):
                rows = slice(base + f * P, base + f * P + P) if reg is None else bass.ds(reg * (2 * P) + (base + f * P), P)
                sp.dma_start(dst[s][:, :], sig_scr[rows, :]).then_inc(sg_in[s], 16)

        def split_o_pe(pe, t):
            pe.wait_ge(o_in[t % 2], 16 * (t // 2 + 1))
            for h in range(2):
                round_fill(pe, Count(MIX_RB + 2 * t + h), [ot[t % 2][:, P * (4 * h + j):P * (4 * h + j) + P] for j in range(4)])

        def split_act(act, t, H3, rb, banks, sem_full, sem_hi, n0):
            for h in range(2):
                act.wait_ge(sem_full, rb + 2 * t + h + 1)
                nc.scalar.activation(H3[:, 4 * h:4 * h + 4, P * t:P * t + P], four(banks[h]), ACT.Copy).then_inc(sem_hi, 1)

        def split_dve(v, t, H3, L3, banks, sem_hi, free):
            for h in range(2):
                v.wait_ge(sem_hi, 2 * t + h + 1)
                nc.vector.tensor_tensor(L3[:, 4 * h:4 * h + 4, P * t:P * t + P], four(banks[h]),
                                        H3[:, 4 * h:4 * h + 4, P * t:P * t + P].bitcast(F32), ALU.subtract).then_inc(free[h], 1)

        class Mix:

            def __init__(self, it, s):
                self.s, self.f, self.it = s, it * 2 + s, it
                self.U = Unit(U_MIX + s, 2, it)
                self.g = it * 12 + (MIX_G + 6 * s)
                self.used = it * 4 + (U_MIX + 2 * s)

        def mix_pe(pe, M, y, c):
            if y == 0 and c == 0:
                pe.wait_ge(w_lo, M.U.n + 1)
                for h in range(2):
                    pe.wait_ge(tp_free[h], MIX_RB // 2 + 8)
                pe.wait_ge(o_lo, 1)
            pe.wait_ge(bank_free[c], M.used + y)
            a, b = 384 * c, 384 * c + 384
            for k in range(4):
                ws = slice((4 * y + k) * P, (4 * y + k + 1) * P)
                for j, (w_, x_) in enumerate(((wh, Oh3), (wl, Oh3), (wh, Ol3))):
                    last = nc.tensor.matmul(gb[c][:, 0:384], w_[M.U.slot][:, ws], x_[:, 4 * y + k, a:b],
                                            start=(k == 0 and j == 0), stop=(k == 3 and j == 2))
            last.then_inc(gemm_done, 1)

        def mix_dve(v, M, y, c):
            s_ = (sga, sgb)[y][M.s][:, 384 * c:384 * c + 384]
            if y == 0 and c == 0:
                v.wait_ge(sg_in[M.s], M.it * 32 + 32)
            v.wait_ge(gemm_done, M.g + (3 * y + c + 1))
            nc.vector.tensor_tensor(s_, gb[c][:, 0:384], s_, ALU.mult).then_inc(bank_free[c], 1)

        def mix_split(v, M, c):
            s_ = sga[M.s][:, 384 * c:384 * c + 384]
            v.wait_ge(m_hi, M.f * 3 + (c + 1))
            d_ = mslice(Ml, M, c)
            nc.vector.tensor_tensor(d_, s_, mslice(Mh, M, c).bitcast(F32), ALU.subtract).then_inc(m_lo, 1)

        def mslice(T, M, c):
            return T[:, bass.ds(M.f * TOK + 384 * c, 384)]

        def mix_pool(pool, M, c):
            pool.wait_ge(bank_free[c], M.used + 2)
            s_ = sga[M.s][:, 384 * c:384 * c + 384]
            nc.gpsimd.tensor_tensor(s_, s_, sgb[M.s][:, 384 * c:384 * c + 384], ALU.add).then_inc(m_sum, 1)

        def mix_act(act, M, c):
            act.wait_ge(m_sum, M.f * 3 + (c + 1))
            nc.scalar.activation(mslice(Mh, M, c), sga[M.s][:, 384 * c:384 * c + 384], ACT.Copy).then_inc(m_hi, 1)

        def mix_tile_pe(pe, M):
            for y in range(2):
                for c in range(3):
                    mix_pe(pe, M, y, c)

        def mix_tile_dve(v, M):
            for y in range(2):
                for c in range(3):
                    mix_dve(v, M, y, c)
            for c in range(3):
                mix_split(v, M, c)

        U_OUT = U_MIX + 8
        U_MLP = U_OUT + 8
        OUT_G = MIX_G + 48
        xrows = [I["x_prompt"][0, P * t:P * t + P, :] for t in range(8)] + [XSRC[9]]
        yrows = [O["y_prompt"][P * t:P * t + P, :] for t in range(8)] + [O["y_sample"]]

        def row_parts(rows):
            return [(lambda d, j=j: d[:, 4 * j:4 * j + 4, :], rows[:, 512 * j:512 * j + 512].rearrange("p (k n) -> p k n", k=4))
                    for j in range(2)]

        def out_sp(sp):
            for k in range(8):
                U = Unit(U_OUT + k)
                if k < 2:
                    sp.wait_ge(w_lo, U.n - 1)
                else:
                    sp.wait_ge(wo_lo[k % 2], k // 2)
                dst = raw[U.slot][:, :].rearrange("p (k n) -> p k n", k=KT)
                for part_, src in row_parts(I["w_out"][P * k:P * k + P, :]):
                    sp.dma_start(part_(dst), src).then_inc(raw_full[U.slot], 16)
            sp.wait_ge(gemm_done, OUT_G)
            sp.wait_ge(m_lo, 24)
            sp.dma_start(gpost[:, :], I["g_post_mix"].to_broadcast([P, D])).then_inc(g2_in, 16)
            sp.dma_start(gmlp[:, :], I["g_pre_mlp"].to_broadcast([P, D])).then_inc(g2_in, 16)
            for t in range(TT + 2):
                if t < TT:
                    if t >= 2:
                        sp.wait_ge(hT_full, 2 * (t - 1))
                    sp.dma_start(xr[t % 2][:, :], xrows[t]).then_inc(xr_in[t % 2], 16)
                if 0 <= t - 1 < TT:
                    sp.wait_ge(h_done, t)
                    sp.dma_start(h_scr[P * (t - 1):P * t, :], tb[(t - 1) % 2][:, :]).then_inc(h_out[(t - 1) % 2], 16)

        def out_hi(act, k):
            U = Unit(U_OUT + k)
            act.wait_ge(raw_full[U.slot], U.nth * 32 + 32)
            act.wait_ge(gemm_done, OUT_G)
            nc.scalar.activation(woh[:, D * k:D * k + D], raw[U.slot][:, :], ACT.Copy).then_inc(wo_hi, 1)

        def out_lo(eng, tt, k):
            U = Unit(U_OUT + k)
            eng.wait_ge(wo_hi, k + 1)
            tt(wol[:, D * k:D * k + D], raw[U.slot][:, :], woh[:, D * k:D * k + D].bitcast(F32),
               ALU.subtract).then_inc(wo_lo[k % 2], 1)

        def out_pe(pe, tiles):
            pe.wait_ge(m_lo, 24)
            for t in tiles:
                if t >= 2:
                    pe.wait_ge(dn_free, 2 * (t - 1))
            for k in range(KT):
                if 0 in tiles:
                    pe.wait_ge(wo_lo[k % 2], k // 2 + 1)
                for t in tiles:
                    ts = slice(P * t, P * t + P)
                    for h in range(2):
                        bank = dn[(2 * t + h) % 4]
                        hs = slice(D * k + 512 * h, D * k + 512 * h + 512)
                        for j, (m_, w_) in enumerate(((Mh3, woh), (Mh3, wol), (Ml3, woh))):
                            last = nc.tensor.matmul(bank[:, :], m_[:, k, ts], w_[:, hs],
                                                    start=(k == 0 and j == 0), stop=(k == KT - 1 and j == 2))
                        if k == KT - 1:
                            last.then_inc(dn_full, 1)

        def out_turn(pe, t):
            pe.wait_ge(hn_done, t + 1)
            for h in range(2):
                if t:
                    pe.wait_ge(hT_free[h], t)
                for j in range(4):
                    last = nc.tensor.transpose(four(hb[h])[:, j, :], xr[t % 2][:, P * (4 * h + j):P * (4 * h + j) + P], ident[:, :])
                last.then_inc(hT_full, 1)

        stat = small[:, 48:160]

        class Link:

            def __init__(self, at):
                self.at = at

            def do(self, v, ins):
                ins.then_inc(x_chain, 1)
                self.at += 1
                v.wait_ge(x_chain, self.at)

        link = Link(6)

        def norm_var(v, ss, w, r, add=None):
            if add is not None:
                link.do(v, nc.vector.tensor_tensor(ss, ss, add, ALU.add))
            link.do(v, nc.vector.tensor_scalar(w, ss, 1.0 / D, EPS, ALU.mult, ALU.add))
            nc.vector.reciprocal(r, w).then_inc(rv_done, 1)

        def norm_newton(v, y, w, t1):
            link.do(v, nc.vector.tensor_tensor(t1, y, y, ALU.mult))
            link.do(v, nc.vector.tensor_tensor(t1, t1, w, ALU.mult))
            link.do(v, nc.vector.tensor_scalar(t1, t1, -0.5, 1.5, ALU.mult, ALU.add))
            link.do(v, nc.vector.tensor_tensor(y, y, t1, ALU.mult))

        def st(c, t, n=1):
            return stat[:, 16 * (t % 2) + c:16 * (t % 2) + c + n]

        def out_act_a(act, t):
            for h in range(2):
                act.wait_ge(dn_full, 2 * t + h + 1)
                if t:
                    act.wait_ge(sq_b, t)
                nc.scalar.activation(jk[:, 512 * h:512 * h + 512], dn[(2 * t + h) % 4][:, :], ACT.Square,
                                     accum_out=st(h, t)).then_inc(sq_a, 1)
            act.wait_ge(rv_done, 2 * t + 1)
            nc.scalar.activation(st(4, t), st(3, t), ACT.Sqrt).then_inc(sq_done, 1)

        def out_act_b(act, t):
            act.wait_ge(h_done, t + 1)
            act.wait_ge(sq_a, 2 * t + 2)
            nc.scalar.activation(jk[:, :], tb[t % 2][:, :], ACT.Square, accum_out=st(8, t)).then_inc(sq_b, 1)
            act.wait_ge(rv_done, 2 * t + 2)
            nc.scalar.activation(st(11, t), st(10, t), ACT.Sqrt).then_inc(sq_done, 1)

        def stored(eng):
            eng.wait_ge(h_out[0], 16 * (TT // 2 + 1))
            eng.wait_ge(h_out[1], 16 * (TT // 2))

        def out_dve_a(v, t):
            v.wait_ge(sq_a, 2 * t + 2)
            norm_var(v, st(0, t), st(2, t), st(3, t), st(1, t))
            v.wait_ge(sq_done, 2 * t + 2)
            norm_newton(v, st(4, t), st(2, t), st(5, t))
            if t >= 2:
                v.wait_ge(h_out[t % 2], 16 * (t // 2))
            for h in range(2):
                hs = slice(512 * h, 512 * h + 512)
                nc.vector.scalar_tensor_tensor(tb[t % 2][:, hs], dn[(2 * t + h) % 4][:, :], st(4, t), gpost[:, hs],
                                               ALU.mult, ALU.mult).then_inc(dn_free, 1)

        def out_pool(pool, t):
            pool.wait_ge(dn_free, 2 * t + 2)
            pool.wait_ge(xr_in[t % 2], 16 * (t // 2 + 1))
            nc.gpsimd.tensor_tensor(tb[t % 2][:, :], tb[t % 2][:, :], xr[t % 2][:, :], ALU.add).then_inc(h_done, 1)

        def out_dve_b(v, t):
            v.wait_ge(sq_b, t + 1)
            norm_var(v, st(8, t), st(9, t), st(10, t))
            v.wait_ge(sq_done, 2 * t + 3)
            norm_newton(v, st(11, t), st(9, t), st(12, t))
            nc.vector.scalar_tensor_tensor(xr[t % 2][:, :], tb[t % 2][:, :], st(11, t), gmlp[:, :],
                                           ALU.mult, ALU.mult).then_inc(hn_done, 1)

        UP_B = U_MIX + 16
        DB = 2 * TT
        WB = U_OUT

        def mlp_unit(g, j, down):
            return Unit(U_MLP + 2 * j + down, 2 * GRP, g)

        def mlp_sp(sp, g):
            for j in range(GRP):
                for down in (0, 1):
                    U = mlp_unit(g, j, down)
                    if down:
                        sp.wait_ge(d_lo, g * GRP + (j + 1))
                        rows = I["w_down"][bass.ds(g * (GRP * P) + P * j, P), :]
                        parts = row_parts(rows)
                    else:
                        sp.wait_ge(w_lo, g * GRP + (WB + j))
                        v = I["w_up"].rearrange("(k p) n -> p k n", p=P)
                        cs_ = bass.ds(g * (GRP * P) + P * j, P)
                        parts = [(lambda d, i=i: d[:, 4 * i:4 * i + 4, :], v[:, 4 * i:4 * i + 4, cs_]) for i in range(2)]
                    dst = raw[U.slot][:, :].rearrange("p (k n) -> p k n", k=KT)
                    for part_, src in parts:
                        sp.dma_start(part_(dst), src).then_inc(raw_full[U.slot], 16)

        def mlp_hi(act, g, j, down):
            U = mlp_unit(g, j, down)
            act.wait_ge(raw_full[U.slot], U.nth * 32 + 32)
            if down:
                act.wait_ge(dn_full, g * 18 + DB)
                act.wait_ge(hT_full, 2 * TT)
                nc.scalar.activation(dh[:, D * j:D * j + D], raw[U.slot][:, :], ACT.Copy).then_inc(d_hi, 1)
            else:
                act.wait_ge(gemm_done, g * 12 + (OUT_G + 3 * j - 3))
                act.wait_ge(gemm_done, OUT_G)
                nc.scalar.activation(wh[j % 2][:, :], raw[U.slot][:, :], ACT.Copy).then_inc(w_hi, 1)

        def mlp_lo(pool, g, j, down):
            U = mlp_unit(g, j, down)
            if down:
                pool.wait_ge(d_hi, g * GRP + (j + 1))
                hi_, lo_, done = dh[:, D * j:D * j + D], dl[:, D * j:D * j + D], d_lo
            else:
                pool.wait_ge(w_hi, g * GRP + (WB + j + 1))
                hi_, lo_, done = wh[j % 2][:, :], wl[j % 2][:, :], w_lo
            nc.gpsimd.tensor_tensor(lo_, raw[U.slot][:, :], hi_.bitcast(F32), ALU.subtract).then_inc(done, 1)

        def mlp_up_pe(pe, g, j, c):
            if c == 0:
                pe.wait_ge(w_lo, g * GRP + (WB + j + 1))
            if j == 0:
                for h in range(2):
                    pe.wait_ge(hT_free[h], 3 * c + 3)
            pe.wait_ge(bank_free[c], g * 4 + (UP_B + j))
            a = 384 * c
            for k in range(KT):
                ws = slice(P * k, P * k + P)
                for i, (w_, x_) in enumerate(((wh, Mh3), (wl, Mh3), (wh, Ml3))):
                    last = nc.tensor.matmul(gb[c][:, 0:384], w_[j % 2][:, ws], x_[:, k, a:a + 384],
                                            start=(k == 0 and i == 0), stop=(k == KT - 1 and i == 2))
            last.then_inc(gemm_done, 1)


        def mlp_up_act(act, g, j, c):
            m = 3 * j + c
            act.wait_ge(gemm_done, g * 12 + (OUT_G + m + 1))
            act.wait_ge(u_lo, g * 12 + (U_B + m - 1))
            act.wait_ge(dn_full, g * 18 + DB)
            nc.scalar.activation(rl[m % 2], gb[c][:, 0:384], ACT.Relu).then_inc(bank_free[c], 1)
            act.wait_ge(bank_free[c], g * 4 + (UP_B + j + 1))
            us = slice(TOK * j + 384 * c, TOK * j + 384 * c + 384)
            nc.scalar.activation(Uh[:, us], rl[m % 2], ACT.Square).then_inc(u_hi, 1)

        def mlp_up_dve(v, g, j, c):
            m = 3 * j + c
            us = slice(TOK * j + 384 * c, TOK * j + 384 * c + 384)
            v.wait_ge(bank_free[c], g * 4 + (UP_B + j + 1))
            v.wait_ge(u_lo, g * 12 + (U_B + m))
            nc.vector.tensor_tensor(rl2, rl[m % 2], rl[m % 2], ALU.mult).then_inc(u_sq, 1)
            v.wait_ge(u_sq, g * 12 + (m + 1))
            v.wait_ge(u_hi, g * 12 + (m + 1))
            nc.vector.tensor_tensor(Ul[:, us], rl2, Uh[:, us].bitcast(F32), ALU.subtract).then_inc(u_lo, 1)

        U_B = 2

        def mlp_down_pe(pe, g, t, h):
            q = 2 * t + h
            pe.wait_ge(dn_free, g * 18 + (DB + q - 2))
            if q < 3:
                pe.wait_ge(dn_free, DB)
            if h == 0 and t % 3 == 0:
                pe.wait_ge(u_lo, g * 12 + (U_B + 10 + t // 3))
            if q == 0:
                pe.wait_ge(d_lo, g * GRP + (GRP + 1))
            for j in range(GRP):
                us = slice(TOK * j + P * t, TOK * j + P * t + P)
                ds_ = slice(D * j + 512 * h, D * j + 512 * h + 512)
                for i, (u_, d_) in enumerate(((Uh, dh), (Uh, dl), (Ul, dh))):
                    last = nc.tensor.matmul(dn[q % 3][:, :], u_[:, us], d_[:, ds_],
                                            start=(j == 0 and i == 0), stop=(j == GRP - 1 and i == 2))
            last.then_inc(dn_full, 1)

        def mlp_down_dve(v, g, t, h):
            q = 2 * t + h
            ys = yacc[:, D * t + 512 * h:D * t + 512 * h + 512]
            v.wait_ge(dn_full, g * 18 + (DB + q + 1))
            if q == 0:
                v.wait_ge(dn_free, g * 18 + DB)
            nc.vector.tensor_tensor(ys, dn[q % 3][:, :], ys, ALU.add).then_inc(dn_free, 1)

        def end_sp(sp):
            sp.wait_ge(gemm_done, OUT_G + 12 * NGRP)
            stored(sp)
            sp.dma_start(gend[:, :], I["g_post_mlp"].to_broadcast([P, D])).then_inc(g3_in, 16)
            for t in range(TT):
                sp.dma_start(hend[:, D * t:D * t + D], h_scr[P * t:P * t + P, :]).then_inc(x_in[t], 16)
            for t in range(TT):
                sp.wait_ge(y_done[t % 2], t // 2 + 1)
                sp.dma_start(yrows[t], yacc[:, D * t:D * t + D]).then_inc(y_out, 16)
            sp.wait_ge(y_out, 16 * TT)

        def end_act(act):
            for t in range(TT):
                act.wait_ge(dn_free, DB + 18 * (NGRP - 1) + 2 * t + 2)
                if t:
                    act.wait_ge(sq_b, TT + t)
                nc.scalar.activation(jend[:, :], yacc[:, D * t:D * t + D], ACT.Square,
                                     accum_out=stat[:, 32 + t:33 + t]).then_inc(sq_b, 1)
            act.wait_ge(rv_done, 2 * TT + 1)
            nc.scalar.activation(stat[:, 62:71], stat[:, 52:61], ACT.Sqrt).then_inc(sq_done, 1)

        def end_dve(v):
            v.wait_ge(sq_b, 2 * TT)
            norm_var(v, stat[:, 32:41], stat[:, 42:51], stat[:, 52:61])
            v.wait_ge(sq_done, 2 * TT + 2)
            norm_newton(v, stat[:, 62:71], stat[:, 42:51], stat[:, 72:81])
            v.wait_ge(g3_in, 16)
            for t in range(TT):
                yt, ht = yacc[:, D * t:D * t + D], hend[:, D * t:D * t + D]
                nc.vector.scalar_tensor_tensor(yt, yt, stat[:, 62 + t:63 + t], gend[:, :], ALU.mult, ALU.mult).then_inc(yn_done, 1)
                if t % 2:
                    v.wait_ge(yn_done, t + 1)
                    v.wait_ge(x_in[t], 32)
                    nc.vector.tensor_tensor(yt, yt, ht, ALU.add).then_inc(y_done[1], 1)

        def end_pool(pool):
            for t in range(0, TT, 2):
                yt, ht = yacc[:, D * t:D * t + D], hend[:, D * t:D * t + D]
                pool.wait_ge(yn_done, t + 1)
                pool.wait_ge(x_in[t], 32)
                nc.gpsimd.tensor_tensor(yt, yt, ht, ALU.add).then_inc(y_done[0], 1)

        block = keep.enter_context(nc.Block())

        def attention_done(eng):
            eng.wait_ge(kb_out, 16 * 7)
            eng.wait_ge(o_out, 16 * 12)
            eng.wait_ge(swa_cur, 12)

        @block.sync
        def _(sp):
            norm_sp(sp)
            load(sp, Unit(2), cols_of(I["w_in"], COL_KA))
            load(sp, Unit(3), cols_of(I["w_in"], COL_VA))
            load(sp, Unit(4), cols_gate(0))
            fox_step_sp(sp, FoxStep(0))
            with sp.Fori(1, 3) as it:
                fox_step_sp(sp, FoxStep(None, it))
            fox_step_sp(sp, FoxStep(3))
            swa_pre_sp(sp)
            swa_step_sp(sp, SwaStep(0))
            with sp.Fori(1, 3) as it:
                swa_step_sp(sp, SwaStep(None, it))
            swa_step_sp(sp, SwaStep(3))
            attention_done(sp)
            sam_caches(sp, Sam(0, 0))
            with sp.Fori(0, 3) as it:
                sam_sp(sp, it)
            sam_sp(sp, 3)
            sp.wait_ge(sig_out, 16 * 16)
            enter_mix(sp)
            for f in range(8):
                mix_load(sp, f)
                if f < 2:
                    sg_load(sp, f, f)
            with sp.Fori(0, 3) as it:
                for s in range(2):
                    M = Mix(it, s)
                    load(sp, ahead(M.U), mix_parts(2 + s, it))
                    sp.wait_ge(m_lo, M.f * 3 + 3)
                    sg_load(sp, s, 2 + s, it)
            out_sp(sp)
            with sp.Fori(0, NGRP) as g:
                mlp_sp(sp, g)
            end_sp(sp)

        @block.scalar
        def _(act):
            norm_act(act)
            hi(act, Unit(2))
            lf_act_(act)
            for c in range(3):
                q_read(act, Unit(1), c, 0)
            for n in (3, 4, 5):
                hi(act, Unit(n))
            fox_step_act(act, FoxStep(0))
            with act.Fori(1, 3) as it:
                fox_step_act(act, FoxStep(None, it))
            fox_step_act(act, FoxStep(3))
            swa_pre_act(act)
            with act.Fori(0, 3) as it:
                swa_step_act(act, SwaStep(None, it))
            swa_step_act(act, SwaStep(3))
            attention_done(act)
            with act.Fori(0, 4) as it:
                sam_act(act, it)
            enter_mix(act)
            for t in range(8):
                split_act(act, t, Oh3, MIX_RB, tp, tp_full, o_hi, 0)
            nc.scalar.activation(Oh3[:, :, SEQ:TOK], osT3[:, :, :], ACT.Copy).then_inc(o_hi, 1)

            def mix_step(M, more):
                for c in range(3):
                    mix_act(act, M, c)
                if more:
                    hi(act, ahead(M.U), used=M.g + 6)
            with act.Fori(0, 3) as it:
                for s in range(2):
                    mix_step(Mix(it, s), True)
            for s in range(2):
                mix_step(Mix(3, s), False)
            for k in range(8):
                out_hi(act, k)
            act.wait_ge(m_lo, 24)
            for t in range(TT + 1):
                if t < TT:
                    out_act_a(act, t)
                    out_act_b(act, t)
                if t >= 1:
                    split_act(act, t - 1, Mh3, 0, hb, hT_full, h_hi, 0)
            with act.Fori(0, NGRP) as g:
                mlp_hi(act, g, 0, 0)
                mlp_hi(act, g, 1, 0)
                mlp_hi(act, g, 0, 1)
                for j in range(GRP):
                    for c in range(3):
                        mlp_up_act(act, g, j, c)
                    if j + 2 < GRP:
                        mlp_hi(act, g, j + 2, 0)
                    if j + 1 < GRP:
                        mlp_hi(act, g, j + 1, 1)
            end_act(act)

        @block.vector
        def _(v):
            norm_dve(v)
            for c in range(3):
                lf_dve_z(v, c)
            lf_dve(v)
            for n, dst, r in ((2, nB, 3), (3, nC, 0)):
                for c in range(3):
                    kv_read(v, Unit(n), c, 0, dst, r)
            fox_step_dve(v, FoxStep(0))
            with v.Fori(1, 3) as it:
                fox_step_dve(v, FoxStep(None, it))
            fox_step_dve(v, FoxStep(3))
            with v.Fori(0, 3) as it:
                swa_step_dve(v, SwaStep(None, it))
            swa_step_dve(v, SwaStep(3))
            attention_done(v)
            nc.vector.memset(one8[:, :], 1.0).then_inc(one_set, 1)
            v.wait_ge(one_set, 1)
            with v.Fori(0, 4) as it:
                sam_dve(v, it)
            enter_mix(v)
            for t in range(8):
                split_dve(v, t, Oh3, Ol3, tp, o_hi, tp_free)
            v.wait_ge(o_hi, 17)
            nc.vector.tensor_tensor(Ol3[:, :, SEQ:TOK], osT3[:, :, :], Oh3[:, :, SEQ:TOK].bitcast(F32),
                                    ALU.subtract).then_inc(o_lo, 1)
            with v.Fori(0, 4) as it:
                for s in range(2):
                    mix_tile_dve(v, Mix(it, s))
            for k in range(1, 8, 2):
                out_lo(v, nc.vector.tensor_tensor, k)
            v.wait_ge(g2_in, 32)
            for t in range(TT + 1):
                if t < TT:
                    out_dve_a(v, t)
                    out_dve_b(v, t)
                if t >= 1:
                    split_dve(v, t - 1, Mh3, Ml3, hb, h_hi, hT_free)
            stored(v)
            v.wait_ge(hT_full, 2 * TT)
            nc.vector.memset(yacc[:, :], 0.0).then_inc(y_zero, 1)
            v.wait_ge(y_zero, 1)
            v.sem_inc(u_lo, U_B)
            with v.Fori(0, NGRP) as g:
                for j in range(GRP):
                    for c in range(3):
                        mlp_up_dve(v, g, j, c)
                for t in range(TT):
                    for h in range(2):
                        mlp_down_dve(v, g, t, h)
            end_dve(v)

        @block.gpsimd
        def _(pool):
            for n in range(2):
                lo(pool, Unit(n))
            pool.wait_ge(tp_full, NORM_R)
            pool.wait_ge(tp_free[1], NORM_R // 2)
            for s in range(2):
                nc.gpsimd.memset(u[s][:, :], 0.0).then_inc(zero_u, 1)
            for n in range(2, 6):
                lo(pool, Unit(n))
            fox_step_pool(pool, FoxStep(0))
            with pool.Fori(1, 3) as it:
                fox_step_pool(pool, FoxStep(None, it))
            fox_step_pool(pool, FoxStep(3))
            swa_pre_pool(pool)
            with pool.Fori(0, 3) as it:
                swa_step_pool(pool, SwaStep(None, it))
            swa_step_pool(pool, SwaStep(3))
            attention_done(pool)
            for t_ in (qz, qzs, Ps, Pw):
                nc.gpsimd.memset(t_[:, :], 0.0).then_inc(zero_s, 1)
            pool.wait_ge(zero_s, 4)
            with pool.Fori(0, 4) as it:
                sam_pool(pool, it)

            def mix_step(M, more):
                for c in range(3):
                    mix_pool(pool, M, c)
                if more:
                    lo(pool, ahead(M.U))
            with pool.Fori(0, 3) as it:
                for s in range(2):
                    mix_step(Mix(it, s), True)
            for s in range(2):
                mix_step(Mix(3, s), False)
            for k in range(0, 8, 2):
                out_lo(pool, nc.gpsimd.tensor_tensor, k)
            for t in range(TT):
                out_pool(pool, t)
            pool.sem_inc(d_lo, 1)
            with pool.Fori(0, NGRP) as g:
                mlp_lo(pool, g, 0, 0)
                mlp_lo(pool, g, 1, 0)
                mlp_lo(pool, g, 0, 1)
                for j in range(GRP):
                    if j + 2 < GRP:
                        mlp_lo(pool, g, j + 2, 0)
                    if j + 1 < GRP:
                        mlp_lo(pool, g, j + 1, 1)
            end_pool(pool)

        @block.tensor
        def _(pe):
            norm_pe(pe)
            for n in (1, 2, 3):
                for c in range(3):
                    gemm(pe, Unit(n), c, CHUNK_ALL[c])
            pe.wait_ge(cst_r, 2)
            pe.wait_ge(zero_u, 2)
            fox_step_pe(pe, FoxStep(0))
            with pe.Fori(1, 3) as it:
                fox_step_pe(pe, FoxStep(None, it))
            fox_step_pe(pe, FoxStep(3))
            swa_pre_pe(pe)
            with pe.Fori(0, 3) as it:
                swa_step_pe(pe, SwaStep(None, it))
            swa_step_pe(pe, SwaStep(3))
            pe.sem_inc(sam_free, 2)
            with pe.Fori(0, 4) as it:
                sam_pe(pe, it)
            for t in range(8):
                split_o_pe(pe, t)
            with pe.Fori(0, 4) as it:
                for s in range(2):
                    mix_tile_pe(pe, Mix(it, s))
            out_pe(pe, (0, 1))
            for t in range(2, TT):
                out_pe(pe, (t,))
                out_turn(pe, t - 2)
            out_turn(pe, TT - 2)
            out_turn(pe, TT - 1)
            with pe.Fori(0, NGRP) as g:
                for j in range(GRP):
                    for c in range(3):
                        mlp_up_pe(pe, g, j, c)
                for t in range(TT):
                    for h in range(2):
                        mlp_down_pe(pe, g, t, h)


def tables():
    import numpy as np

    cst = np.zeros((P, C_ALL), np.float32)
    row = np.arange(P)
    cst[:, C_ID:C_ID + P] = np.eye(P, dtype=np.float32)
    cst[:, C_MASK:C_MASK + P] = np.where(row[None, :] <= row[:, None], 0.0, -BIG)
    band = np.zeros((P, META + 2 * P), np.float32)
    band[P // 2:, META:META + 64] = BIG
    band[:P // 2, META + 192:META + 256] = BIG
    cst[:, C_BAND:C_BAND + META + 2 * P] = band
    cst[:P // 2, C_BAND0 + META + 64:C_BAND0 + META + P] = BIG
    cst[:, C_NEW:C_NEW + NEW] = np.where(np.arange(NEW)[None, :] <= row[:, None] % NEW, 0.0, -BIG)
    for h in range(HEADS):
        cst[h, C_SEL + P * h:C_SEL + P * h + P] = 1.0
        cst[h, C_NSEL + NEW * h:C_NSEL + NEW * h + NEW] = -1.0
    half = DH // 2
    inv_freq = np.float32(10000.0) ** (-np.arange(half, dtype=np.float32) / np.float32(half))
    pos = np.concatenate([np.arange(-META, SEQ), np.tile(PAST + np.arange(NEW), STREAMS)]).astype(np.float32)
    ang = (pos[None, :] * inv_freq[:, None]).astype(np.float32).astype(np.float64)
    cos = np.tile(np.cos(ang), (4, 1)).astype(np.float32)
    sin = np.tile(np.concatenate([-np.sin(ang), np.sin(ang)]), (2, 1)).astype(np.float32)
    return {"cst": cst, "cos": cos, "sin": sin}


_INS = ["x_prompt", "x_sample", "cache_fox_k", "cache_fox_v", "cache_fox_logf", "cache_swa_k", "cache_swa_v",
        "meta_tokens", "w_in", "b_forget", "attn_sinks", "w_o_fox", "w_o_swa", "w_out", "g_pre_mix", "g_post_mix",
        "g_pre_mlp", "g_post_mlp", "w_up", "w_down"]
_OUTS = [("y_prompt", (1, SEQ, D)), ("y_sample", (STREAMS, NEW, D)),
         ("fox_k_p", (1, 1, KEYS, HEADS, DH)), ("fox_v_p", (1, 1, KEYS, HEADS, DH)), ("fox_f_p", (1, 1, KEYS, HEADS)),
         ("swa_k_p", (1, 1, P, 2, DH)), ("swa_v_p", (1, 1, P, 2, DH)),
         ("fox_k_s", (1, STREAMS, NEW, HEADS, DH)), ("fox_v_s", (1, STREAMS, NEW, HEADS, DH)),
         ("fox_f_s", (1, STREAMS, NEW, HEADS)),
         ("swa_k_s", (1, STREAMS, NEW, 2, DH)), ("swa_v_s", (1, STREAMS, NEW, 2, DH))]


def kernel(**inputs):
    import numpy as np
    import concourse.bacc as bacc
    from concourse.bass_utils import run_bass_kernel_spmd as run

    nc = bacc.Bacc("TRN2", target_bir_lowering=False, num_devices=1)
    arrays, I = {}, {}
    for name, a in [(n, inputs[n]) for n in _INS] + list(tables().items()):
        a = np.ascontiguousarray(a)
        arrays[f"in_{name}"] = a
        I[name] = nc.dram_tensor(f"in_{name}", a.shape, F32, kind="ExternalInput").ap()
    for name in ("w_in", "w_o_fox", "w_o_swa", "w_out", "w_up", "w_down"):
        I[name] = I[name].rearrange("o k n -> (o k) n")
    rows2 = {4: "a b c d -> (a b) (c d)", 3: "a b c -> (a b) c"}
    O = {}
    for name, shape in _OUTS:
        ap = nc.dram_tensor(f"out_{name}", shape, F32, kind="ExternalOutput").ap()
        O[name] = ap.rearrange({3: "a b c -> (a b) c", 4: "o a b c -> (o a b) c", 5: "o a b c d -> (o a b) (c d)"}[len(shape)])
    scratch = [nc.dram_tensor(n, s, F32, kind="Internal").ap()
               for n, s in (("o_scr", (SEQ, D)), ("sig_scr", (2 * D, TOK)), ("h_scr", (TOK, D)))]
    layer(nc, I, O, scratch)
    r = run(nc, [arrays], core_ids=[0])
    return tuple(r.results[0][f"out_{name}"] for name, _ in _OUTS)
```

```python
from contextlib import ExitStack

import concourse.bass as bass
from concourse import mybir

P = 128
F32 = mybir.dt.float32
F32R = mybir.dt.float32r
ALU = mybir.AluOpType
ACT = mybir.ActivationFunctionType
AX_X = mybir.AxisListType.X

D = 1024
KT = D // P
META, SEQ, STREAMS, NEW = 16, 1024, 8, 16
PAST, SBUF_WIN = 512, 128
SAMPLE = STREAMS * NEW
TOK = SEQ + SAMPLE
NT = META + TOK
KEYS = META + SEQ
S0 = KEYS
HEADS, DH = 8, 64
FOX_W = HEADS * DH
DFF = 4 * D
EPS = 1e-6
SCALE = DH ** -0.5
BIG = 1e30
COL_QA, COL_KA, COL_VA, COL_F = 0, FOX_W, 2 * FOX_W, 3 * FOX_W
COL_QB = COL_F + HEADS
COL_KB, COL_VB = COL_QB + FOX_W, COL_QB + FOX_W + P
COL_GA = COL_VB + P
COL_GB = COL_GA + D
CHUNK_ALL = [(0, 400), (400, 784), (784, 1168)]
CHUNK_TOK = [(META + 384 * c, META + 384 * c + 384) for c in range(3)]
TT = TOK // P
GRP = 4
NGRP = DFF // (GRP * P)

C_ID, C_MASK, C_BAND, C_BAND0, C_NEW, C_SEL, C_NSEL = 0, 128, 256, 528, 672, 688, 1712
C_ALL = 1840

U_F, U_QA = 0, 1
U_FOX = 4
U_PEEL = U_FOX + 12
U_SWA = U_PEEL + 4
U_SPEEL = U_SWA + 6
U_SAM = U_SPEEL + 1
U_MIX = U_SAM + 8
SIDE = 16


def fox_chunks(i):
    w = META + P * (i + 1)
    if w <= 512:
        return [(0, w)]
    return [(0, 400), (400, w)] if w <= 912 else [(0, 400), (400, 912), (912, w)]


def fox_rounds(i):
    n = i + 2
    return [(a, min(a + 4, n)) for a in range(0, n, 4)]


FOX_C = [6 + sum(len(fox_chunks(m % 8)) for m in range(n)) for n in range(SIDE + 1)]
FOX_R = [6 + sum(len(fox_rounds(m % 8)) for m in range(n)) for n in range(SIDE + 1)]
FC, FR = FOX_C[SIDE], FOX_R[SIDE]
assert FC % 2 == 0 and FR % 2 == 0


class Unit:

    def __init__(self, b, per=0, it=0):
        self.n = b + per * it if per else b
        self.slot = b % 2
        self.nth = b // 2 + (per // 2) * it if per else b // 2


def layer(nc, I, O, scratch):
    o_scr, sig_scr, h_scr = scratch
    keep = ExitStack()
    with keep:
        def sb(name, shape, dt=F32, ctx=keep):
            return ctx.enter_context(nc.sbuf_tensor(name, shape, dt))

        def sem(name):
            return keep.enter_context(nc.semaphore(name))

        gb = [keep.enter_context(nc.psum_tensor(f"gb{c}", [P, 512], F32)) for c in range(3)]
        sc = [keep.enter_context(nc.psum_tensor(f"sc{c}", [P, 512], F32)) for c in range(2)]
        tp = [keep.enter_context(nc.psum_tensor(f"tp{c}", [P, 512], F32)) for c in range(2)]
        po = keep.enter_context(nc.psum_tensor("po", [P, 512], F32))
        dn = [sc[0], sc[1], tp[0], tp[1]]
        hb = [po, gb[2]]

        raw = [sb(f"raw{s}", [P, 1024]) for s in range(2)]
        wh = [sb(f"wh{s}", [P, 1024], F32R) for s in range(2)]
        wl = [sb(f"wl{s}", [P, 1024], F32R) for s in range(2)]
        ident = sb("ident", [P, P])
        ident_r = sb("ident_r", [P, P], F32R)
        mask_r = sb("mask_r", [P, P], F32R)
        osT_rl = sb("osT_rl", [P, 3 * 384])
        osT = osT_rl[:, 0:8 * SAMPLE]
        rl, rl2 = [osT_rl[:, 0:384], osT_rl[:, 384:768]], osT_rl[:, 768:1152]
        small = sb("small", [P, 160])
        mx, nm, ssum, rinv = small[:, 0:12], small[:, 12:16], small[:, 16:24], small[:, 24:28]
        esink, sinkcur, bf = small[:, 28:32], small[:, 32:34], small[0:8, 34:35]
        sinkb, sinkrow = small[:, 36:44], small[:, 44:45]
        ssq, var, rv, rstd = small[:, 48:60], small[:, 60:72], small[:, 72:84], small[:, 84:96]
        nt1, nt2 = small[:, 96:108], small[:, 108:120]

        A = ExitStack()
        cst = sb("cst", [P, C_ALL], ctx=A)
        Xh = sb("Xh", [P, KT * NT], F32R, A)
        Xl = sb("Xl", [P, KT * NT], F32R, A)
        A1 = ExitStack()
        xt = [sb(f"xt{t}", [P, D], ctx=A1) for t in range(10)]
        gpre = sb("gpre", [P, D], ctx=A1)
        junk = sb("junk", [P, D], ctx=A1)
        A1.close()
        A2k = ExitStack()
        qTs = sb("qTs", [P, 4 * P], ctx=A2k)
        kTs = sb("kTs", [P, 4 * P], ctx=A2k)
        vTs = sb("vTs", [P, 4 * P], ctx=A2k)
        qbs = sb("qbs", [P, 4 * P], ctx=A2k)
        kbT = sb("kbT", [P, NT], ctx=A2k)
        vball = sb("vball", [P, 12 * P], ctx=A2k)
        vbs = sb("vbs", [P, P], ctx=A2k)
        lfq = sb("lfq", [8, NT], ctx=A2k)
        cum_lf = sb("cum_lf", [8, KEYS], ctx=A2k)
        sig = sb("sig", [P, TOK], ctx=A2k)
        A2 = ExitStack()
        ckb = [sb(f"ckb{h}", [P, KEYS], ctx=A2) for h in range(2)]
        kcur = sb("kcur", [P, NT], ctx=A2)
        vcur = sb("vcur", [P, 10 * P], ctx=A2)
        ktm = sb("ktm", [P, 10 * P], ctx=A2)
        nA = sb("nA", [P, NT], ctx=A2)
        nB = sb("nB", [P, NT], ctx=A2)
        nC = sb("nC", [P, NT], ctx=A2)
        qcur = sb("qcur", [P, NT], ctx=A2)
        u = [sb(f"u{s}", [P, 9 * P], ctx=A2) for s in range(2)]
        PT = [sb(f"PT{s}", [P, 9 * P], ctx=A2) for s in range(2)]
        opair = sb("opair", [P, SEQ], ctx=A2)
        selcur = sb("selcur", [8, 2 * P], ctx=A2)
        sh = osT_rl[:, 0:400]
        A2.close()
        A3 = ExitStack()
        kc, vc, kw, vw = ([None, None] for _ in range(4))
        for e in range(2):
            kc[e], vc[e] = sb(f"kc{e}", [P, 4 * 512], ctx=A3), sb(f"vc{e}", [P, 4 * 512], ctx=A3)
            kw[e], vw[e] = sb(f"kw{e}", [P, P], ctx=A3), sb(f"vw{e}", [P, P], ctx=A3)
            if e == 0:
                clf = sb("clf", [P, 2 * 32], ctx=A3)
                qz = sb("qz", [P, 640], ctx=A3)
                qzs = sb("qzs", [P, P], ctx=A3)
        KcT = sb("KcT", [P, 4 * 512], ctx=A3)
        KwT = sb("KwT", [P, P], ctx=A3)
        kvn = sb("kvn", [P, 10 * NEW], ctx=A3)
        vn = sb("vn", [NEW, 5 * P], ctx=A3)
        Ps = sb("Ps", [P, 5 * P], ctx=A3)
        Pw = sb("Pw", [P, 272], ctx=A3)
        PTs = sb("PTs", [P, 8 * P], ctx=A3)
        one8 = sb("one8", [8, 512], ctx=A3)
        lf16 = sb("lf16", [8, NEW], ctx=A3)
        cs = sb("cs", [8, 528], ctx=A3)
        A3.close()
        A2k.close()
        A.close()
        Mk = ExitStack()
        Mh = sb("Mh", [P, KT * TOK], F32R, Mk)
        Ml = sb("Ml", [P, KT * TOK], F32R, Mk)
        B1 = ExitStack()
        Oh = sb("Oh", [P, KT * TOK], F32R, B1)
        Ol = sb("Ol", [P, KT * TOK], F32R, B1)
        sga = [sb(f"sga{s}", [P, TOK], ctx=B1) for s in range(2)]
        sgb = [sb(f"sgb{s}", [P, TOK], ctx=B1) for s in range(2)]
        ot = [None] + [sb(f"ot{s}", [P, D], ctx=B1) for s in (1, 2)]
        sb("beyond_sample", [P, 800], ctx=B1)
        ot[0] = sb("ot0", [P, D], ctx=B1)
        B1.close()
        B2 = ExitStack()
        woh = sb("woh", [P, 8 * D], F32R, B2)
        wol = sb("wol", [P, 8 * D], F32R, B2)
        gpost = sb("gpost", [P, D], ctx=B2)
        gmlp = sb("gmlp", [P, D], ctx=B2)
        xr = [sb(f"xr{s}", [P, D], ctx=B2) for s in range(2)]
        tb = [sb(f"tb{s}", [P, D], ctx=B2) for s in range(2)]
        jk = sb("jk", [P, D], ctx=B2)
        B2.close()
        B3 = ExitStack()
        Uh = sb("Uh", [P, GRP * TOK], F32R, B3)
        Ul = sb("Ul", [P, GRP * TOK], F32R, B3)
        yacc = sb("yacc", [P, TT * D], ctx=B3)
        dh = sb("dh", [P, GRP * D], F32R, B3)
        dl = sb("dl", [P, GRP * D], F32R, B3)
        B3.close()
        Mk.close()
        E1 = ExitStack()
        hend = sb("hend", [P, TT * D], ctx=E1)
        gend = sb("gend", [P, D], ctx=E1)
        jend = sb("jend", [P, D], ctx=E1)
        E1.close()

        Xh3 = Xh[:, :].rearrange("p (k n) -> p k n", k=KT)
        Xl3 = Xl[:, :].rearrange("p (k n) -> p k n", k=KT)
        Mh3 = Mh[:, :].rearrange("p (k n) -> p k n", k=KT)
        Ml3 = Ml[:, :].rearrange("p (k n) -> p k n", k=KT)
        Oh3 = Oh[:, :].rearrange("p (k n) -> p k n", k=KT)
        Ol3 = Ol[:, :].rearrange("p (k n) -> p k n", k=KT)

        raw_full = [sem(f"raw_full{s}") for s in range(2)]
        w_hi, w_lo = sem("w_hi"), sem("w_lo")
        gemm_done = sem("gemm_done")
        bank_free = [sem(f"bank_free{c}") for c in range(3)]
        tp_full = sem("tp_full")
        tp_free = [sem(f"tp_free{s}") for s in range(2)]
        sc_full, sc_free = sem("sc_full"), sem("sc_free")
        cst_in, cst_r, id_in, gpre_in = sem("cst_in"), sem("cst_r"), sem("id_in"), sem("gpre_in")
        x_in = [sem(f"x_in{t}") for t in range(10)]
        g_in, ssq_done, rstd_done, x_chain = sem("g_in"), sem("ssq_done"), sem("rstd_done"), sem("x_chain")
        sq_done, xs_done, x_hi = sem("sq_done"), sem("xs_done"), sem("x_hi")
        lf_chain, lf_act, lf_done = sem("lf_chain"), sem("lf_act"), sem("lf_done")
        zero_u, zero_s, one_set = sem("zero_u"), sem("zero_s"), sem("one_set")
        cur_copied, kv_out, tab_in = sem("cur_copied"), sem("kv_out"), sem("tab_in")
        nm_done, p_done, sum_inv = sem("nm_done"), sem("p_done"), sem("sum_inv")
        pv_done, o_done, o_out = sem("pv_done"), sem("o_done"), sem("o_out")
        es_done, tot_done = sem("es_done"), sem("tot_done")
        gate_1, sig_done, sig_out = sem("gate_1"), sem("sig_done"), sem("sig_out")
        rope_sh, rope_a, rope_b = sem("rope_sh"), sem("rope_a"), sem("rope_b")
        vb_done, kb_out = sem("vb_done"), sem("kb_out")
        swa_cur, q_moved, qk_moved = sem("swa_cur"), sem("q_moved"), sem("qk_moved")
        c_in = [sem(f"c_in{e}") for e in range(2)]
        sam_free, s_stage, s_cs, s_red = sem("sam_free"), sem("s_stage"), sem("s_cs"), sem("s_red")
        s_exp, s_sum, s_scl = sem("s_exp"), sem("s_sum"), sem("s_scl")
        sg_in = [sem(f"sg_in{e}") for e in range(2)]
        o_hi, o_lo, m_sum, m_hi, m_lo = sem("o_hi"), sem("o_lo"), sem("m_sum"), sem("m_hi"), sem("m_lo")
        wo_hi, wo_lo = sem("wo_hi"), [sem(f"wo_lo{e}") for e in range(2)]
        g2_in, g3_in, rv_done = sem("g2_in"), sem("g3_in"), sem("rv_done")
        xr_in = [sem(f"xr_in{e}") for e in range(2)]
        dn_full, dn_free = sem("dn_full"), sem("dn_free")
        hT_full, hT_free, h_hi = sem("hT_full"), [sem(f"hT_free{e}") for e in range(2)], sem("h_hi")
        h_done, hn_done, sq_a, sq_b = sem("h_done"), sem("hn_done"), sem("sq_a"), sem("sq_b")
        h_out = [sem(f"h_out{e}") for e in range(2)]
        u_hi, u_sq, u_lo, d_hi, d_lo = sem("u_hi"), sem("u_sq"), sem("u_lo"), sem("d_hi"), sem("d_lo")
        yn_done, y_done, y_out = sem("yn_done"), [sem(f"y_done{e}") for e in range(2)], sem("y_out")

        def cols_of(w, c0, reg=None, step=0):
            v = w.rearrange("(k p) n -> p k n", p=P)
            cs_ = bass.ds(reg * step + c0, P) if step else slice(c0, c0 + P)
            return [(lambda d: d[:, 0:4, :], v[:, 0:4, cs_]), (lambda d: d[:, 4:8, :], v[:, 4:8, cs_])]

        def cols_qb(reg):
            v = I["w_in"].rearrange("(k p) n -> p k n", p=P)
            return [(lambda d, g=g: d[:, :, g * DH:(g + 1) * DH],
                     v[:, :, bass.ds(reg * DH + (COL_QB + g * 4 * DH), DH)]) for g in range(2)]

        def cols_gate(g0, reg=None, step=0):
            return cols_of(I["w_in"], COL_GA + g0 * P, reg, step * P)

        def load(sp, U, parts):
            if not isinstance(U.n, int) or U.n >= 2:
                sp.wait_ge(w_lo, U.n - 1)
            dst = raw[U.slot][:, :].rearrange("p (k n) -> p k n", k=KT)
            for part, src in parts:
                sp.dma_start(part(dst), src).then_inc(raw_full[U.slot], 16)

        def hi(act, U, used=None):
            act.wait_ge(raw_full[U.slot], U.nth * 32 + 32)
            if not isinstance(U.n, int) or U.n >= 2:
                act.wait_ge(gemm_done, U.n * 3 - 3 if used is None else used)
            nc.scalar.activation(wh[U.slot][:, :], raw[U.slot][:, :], ACT.Copy).then_inc(w_hi, 1)

        def lo(pool, U):
            pool.wait_ge(w_hi, U.n + 1)
            nc.gpsimd.tensor_tensor(wl[U.slot][:, :], raw[U.slot][:, :], wh[U.slot][:, :].bitcast(F32),
                                    ALU.subtract).then_inc(w_lo, 1)

        def gemm(pe, U, c, cols, between=()):
            if c == 0:
                pe.wait_ge(w_lo, U.n + 1)
            if not isinstance(U.n, int) or U.n > 0:
                pe.wait_ge(bank_free[c], U.n)
            a, b = cols
            for k in range(KT):
                ws = slice(k * P, (k + 1) * P)
                for j, (w_, x_) in enumerate(((wh, Xh3), (wl, Xh3), (wh, Xl3))):
                    last = nc.tensor.matmul(gb[c][:, 0:b - a], w_[U.slot][:, ws], x_[:, k, a:b],
                                            start=(k == 0 and j == 0), stop=(k == KT - 1 and j == 2))
                if k % 2 and k // 2 < len(between) and k < KT - 1:
                    between[k // 2]()
            last.then_inc(gemm_done, 1)
            for f in between[KT // 2 - 1:]:
                f()

        def apart(eng):
            eng.wait_ge(cst_in, 16)

        def at(eng, x):
            return x if isinstance(x, int) else eng.snap(eng.to_reg(x))

        def gemm_wait(eng, U, c):
            eng.wait_ge(gemm_done, U.n * 3 + (c + 1))

        def four(bank):
            return bank[:, :].rearrange("p (j n) -> p j n", j=4)

        XROWS = [META] + [P] * 9
        XCOL = [0] + [META + P * t for t in range(9)]
        XSRC = [I["meta_tokens"]] + [I["x_prompt"][0, P * t:P * t + P, :] for t in range(8)] + [
            I["x_sample"].rearrange("b l d -> (b l) d")]

        def norm_sp(sp):
            sp.dma_start(ident[:, :], I["cst"][:, C_ID:C_ID + P]).then_inc(id_in, 16)
            for t in range(10):
                sp.dma_start(xt[t][0:XROWS[t], :], XSRC[t]).then_inc(x_in[t], 16)
                if t == FIRST - 1:
                    sp.dma_start(gpre[:, :], I["g_pre_mix"].to_broadcast([P, D])).then_inc(gpre_in, 16)
                    load(sp, Unit(0), cols_of(I["w_in"], COL_F))
            load(sp, Unit(1), cols_of(I["w_in"], COL_QA))
            sp.dma_start(cst[:, :], I["cst"]).then_inc(cst_in, 16)
            sp.wait_ge(x_chain, 1)
            sp.dma_start(sinkb, I["attn_sinks"].to_broadcast([P, HEADS])).then_inc(g_in, 16)
            sp.dma_start(bf, I["b_forget"].rearrange("o h -> h o")).then_inc(g_in, 16)
            for h in range(HEADS):
                row = (h % 4) * 32 + (h // 4) * 16
                sp.dma_start(sinkrow[row:row + 16, :], I["attn_sinks"][:, h:h + 1].to_broadcast([16, 1])).then_inc(g_in, 16)

        FIRST = 4

        def norm_act(act):
            def square(t):
                act.wait_ge(x_in[t], 16)
                if t:
                    act.wait_ge(ssq_done, t)
                nc.scalar.activation(junk[0:XROWS[t], :], xt[t][0:XROWS[t], :], ACT.Square,
                                     accum_out=ssq[0:XROWS[t], t:t + 1]).then_inc(ssq_done, 1)

            def root(a, b):
                act.wait_ge(rstd_done, 1 if a == 0 else 2)
                nc.scalar.activation(rstd[:, a:b], rv[:, a:b], ACT.Sqrt).then_inc(sq_done, 1)

            act.wait_ge(x_chain, 1)
            for t in range(FIRST):
                square(t)
            root(0, FIRST)
            between = {0: (4, 5), 1: (6, 7), 2: (8,), 3: (9,)}
            for t in range(10):
                for later_ in between.get(t, ()):
                    square(later_)
                n, c0 = XROWS[t], XCOL[t]
                for h in range(2):
                    act.wait_ge(tp_full, 2 * t + h + 1)
                    nc.scalar.activation(Xh3[:, 4 * h:4 * h + 4, c0:c0 + n], four(tp[h])[:, :, 0:n],
                                         ACT.Copy).then_inc(x_hi, 1)
                if t == 1:
                    hi(act, Unit(0))
                if t == 3:
                    root(FIRST, 10)
                if t == 5:
                    hi(act, Unit(1))

        def rsqrt_dve(v, n, base, y0_ready, y0_count):
            a, b = n
            v.wait_ge(y0_ready, y0_count)
            y, t1, t2, w = rstd[:, a:b], nt1[:, a:b], nt2[:, a:b], var[:, a:b]
            nc.vector.tensor_tensor(t1, y, y, ALU.mult).then_inc(x_chain, 1)
            v.wait_ge(x_chain, base + 1)
            nc.vector.tensor_tensor(t2, t1, w, ALU.mult).then_inc(x_chain, 1)
            v.wait_ge(x_chain, base + 2)
            nc.vector.tensor_scalar(t1, t2, -0.5, 1.5, ALU.mult, ALU.add).then_inc(x_chain, 1)
            v.wait_ge(x_chain, base + 3)
            nc.vector.tensor_tensor(y, y, t1, ALU.mult).then_inc(x_chain, 1)
            v.wait_ge(x_chain, base + 4)

        def norm_dve(v):
            nc.vector.memset(small[:, :], 1.0).then_inc(x_chain, 1)
            v.wait_ge(id_in, 16)
            nc.vector.tensor_copy(ident_r[:, :], ident[:, :]).then_inc(cst_r, 1)
            for t in range(11):
                if t in (0, FIRST):
                    a, b, at_ = (0, FIRST, 1) if t == 0 else (FIRST, 10, 6)
                    v.wait_ge(ssq_done, b)
                    nc.vector.tensor_scalar(var[:, a:b], ssq[:, a:b], 1.0 / D, EPS, ALU.mult, ALU.add).then_inc(x_chain, 1)
                    v.wait_ge(x_chain, at_ + 1)
                    nc.vector.reciprocal(rv[:, a:b], var[:, a:b]).then_inc(rstd_done, 1)
                    rsqrt_dve(v, (a, b), at_ + 1, sq_done, 1 if t == 0 else 2)
                    v.wait_ge(gpre_in, 16)
                if t < 10:
                    n = XROWS[t]
                    nc.vector.scalar_tensor_tensor(xt[t][0:n, :], xt[t][0:n, :], rstd[0:n, t:t + 1], gpre[0:n, :],
                                                   ALU.mult, ALU.mult).then_inc(xs_done, 1)
                if t >= 1:
                    s, n, c0 = t - 1, XROWS[t - 1], XCOL[t - 1]
                    for h in range(2):
                        v.wait_ge(x_hi, 2 * s + h + 1)
                        nc.vector.tensor_tensor(Xl3[:, 4 * h:4 * h + 4, c0:c0 + n], four(tp[h])[:, :, 0:n],
                                                Xh3[:, 4 * h:4 * h + 4, c0:c0 + n].bitcast(F32),
                                                ALU.subtract).then_inc(tp_free[h], 1)
            v.wait_ge(cst_in, 16)
            nc.vector.tensor_copy(mask_r[:, :], cst[:, C_MASK:C_MASK + P]).then_inc(cst_r, 1)
            v.wait_ge(g_in, 16 * 10)

        def norm_pe(pe):
            pe.wait_ge(id_in, 16)

            def turn(t):
                n = XROWS[t]
                pe.wait_ge(xs_done, t + 1)
                for h in range(2):
                    if t:
                        pe.wait_ge(tp_free[h], t)
                    for j in range(4):
                        k = 4 * h + j
                        last = nc.tensor.transpose(four(tp[h])[:, j, 0:n], xt[t][0:n, k * P:(k + 1) * P], ident[0:n, 0:n])
                    last.then_inc(tp_full, 1)
            for t in range(4):
                turn(t)
            for c in range(3):
                for h in range(2):
                    pe.wait_ge(tp_free[h], 3 * c + 4)
                gemm(pe, Unit(0), c, CHUNK_ALL[c], [lambda t=t: turn(t) for t in range(3 * c + 4, 3 * c + 7) if t < 10])

        NORM_R = 20

        class Count:

            def __init__(self, b, per=0, it=0):
                self.slot = b % 2
                self.n = b + per * it if per else b
                self.half = b // 2 + (per // 2) * it if per else b // 2

        def positive(x):
            return not isinstance(x, int) or x > 0

        def round_fill(pe, R, blocks, n=P, m=P):
            if positive(R.half):
                pe.wait_ge(tp_free[R.slot], R.half)
            for j, src in enumerate(blocks):
                last = nc.tensor.transpose(four(tp[R.slot])[0:n, j, 0:m], src, ident[0:m, 0:m])
            last.then_inc(tp_full, 1)

        def round_read(eng, R):
            eng.wait_ge(tp_free[R.slot], R.half + 1)

        def rounds_read(eng, Rs):
            last = [(R.slot, at(eng, R.half + 1)) for R in list({R.slot: R for R in Rs}.values())]
            apart(eng)
            for slot, n in last:
                eng.wait_ge(tp_free[slot], n)

        def chunk_slot(pe, C):
            if positive(C.n) and not (isinstance(C.n, int) and C.n < 2):
                pe.wait_ge(sc_free, C.n - 1)
            return sc[C.slot]

        lz, le, lw_, ll, ld = (t[0:8, 0:NT] for t in (qcur, kcur, nB, nC, ktm))

        def lf_dve_z(v, c):
            a, b = CHUNK_ALL[c]
            gemm_wait(v, Unit(U_F), c)
            nc.vector.tensor_scalar(lz[:, a:b], gb[c][0:8, 0:b - a], bf, None, ALU.add).then_inc(bank_free[c], 1)

        def lf_dve(v):
            for c in range(3):
                v.wait_ge(bank_free[c], 1)
            nc.vector.scalar_tensor_tensor(le, lz, -1.0, lz, ALU.mult, ALU.min).then_inc(lf_chain, 1)
            v.wait_ge(lf_act, 1)
            nc.vector.tensor_scalar(lw_, le, 1.0, None, ALU.add).then_inc(lf_chain, 1)
            v.wait_ge(lf_chain, 2)
            nc.vector.scalar_tensor_tensor(ld, lw_, -1.0, le, ALU.add, ALU.subtract).then_inc(lf_chain, 1)
            v.wait_ge(lf_act, 2)
            v.wait_ge(lf_chain, 3)
            nc.vector.reciprocal(le, lw_).then_inc(lf_chain, 1)
            v.wait_ge(lf_chain, 4)
            nc.vector.tensor_tensor(ld, ld, le, ALU.mult).then_inc(lf_chain, 1)
            nc.vector.scalar_tensor_tensor(lz, lz, 0.0, ll, ALU.min, ALU.subtract).then_inc(lf_chain, 1)
            v.wait_ge(lf_chain, 6)
            nc.vector.tensor_tensor(lfq[:, :], lz, ld, ALU.add).then_inc(lf_chain, 1)
            v.wait_ge(lf_chain, 7)
            nc.vector.memset(PT[0][0:8, 0:KEYS], 1.0).then_inc(lf_chain, 1)
            v.wait_ge(lf_chain, 8)
            nc.vector.tensor_tensor_scan(cum_lf[:, 0:KEYS], PT[0][0:8, 0:KEYS], lfq[:, 0:KEYS], 0.0,
                                         ALU.mult, ALU.add).then_inc(lf_done, 1)


        def lf_act_(act):
            act.wait_ge(lf_chain, 1)
            nc.scalar.activation(le, le, ACT.Exp).then_inc(lf_act, 1)
            act.wait_ge(lf_chain, 2)
            nc.scalar.activation(ll, lw_, ACT.Ln).then_inc(lf_act, 1)

        def unit_read(eng, U):
            n = at(eng, U.n + 1)
            apart(eng)
            for c in range(3):
                eng.wait_ge(bank_free[c], n)

        def q_read(act, U, c, p):
            if c == 0 and positive(p):
                act.wait_ge(cur_copied, p * 4)
                act.wait_ge(qk_moved, p * 2)
            a, b = CHUNK_ALL[c]
            gemm_wait(act, U, c)
            nc.scalar.activation(nA[:, a:b], gb[c][:, 0:b - a], ACT.Copy, scale=SCALE).then_inc(bank_free[c], 1)

        def kv_read(v, U, c, p, dst, first_round):
            if c == 0 and positive(p):
                v.wait_ge(cur_copied, p * 4)
                v.wait_ge(qk_moved, p * 2)
                v.wait_ge(tp_full, p * FR + (FOX_RB - FR + first_round + 3))
            a, b = CHUNK_ALL[c]
            gemm_wait(v, U, c)
            nc.vector.tensor_copy(dst[:, a:b], gb[c][:, 0:b - a]).then_inc(bank_free[c], 1)

        def gate_act(act, U, c, g):
            if c == 0 and positive(g):
                act.wait_ge(sig_out, g * 16)
            gemm_wait(act, U, c)
            nc.scalar.activation(sig[:, 384 * c:384 * c + 384], gb[c][:, 0:384], ACT.Exp,
                                 scale=-1.0).then_inc(bank_free[c], 1)

        def gate_piece(v, U, n, g):
            c = n // 3
            if n % 3 == 0:
                s_ = sig[:, 384 * c:384 * c + 384]
                v.wait_ge(bank_free[c], U.n + 1)
                nc.vector.tensor_scalar(s_, s_, 1.0, None, ALU.add).then_inc(gate_1, 1)
                v.wait_ge(gate_1, g * 3 + (c + 1))
            s_ = sig[:, P * n:P * n + P]
            nc.vector.reciprocal(s_, s_).then_inc(sig_done, 1)

        def gate_dve(v, U, c, g):
            for n in range(3 * c, 3 * c + 3):
                gate_piece(v, U, n, g)

        def gate_store(sp, g):
            sp.wait_ge(sig_done, g * 9 + 9)
            dst = sig_scr[g * P:g * P + P, :] if isinstance(g, int) else sig_scr[bass.ds(g * P, P), :]
            sp.dma_start(dst, sig[:, :]).then_inc(sig_out, 16)

        def rope_act(act, U, c, m, scale):
            a, b = CHUNK_ALL[c]
            gemm_wait(act, U, c)
            if positive(m):
                act.wait_ge(rope_b, m)
            for h in range(4):
                o = h ^ 1
                nc.scalar.activation(sh[32 * h:32 * h + 32, 0:b - a], gb[c][32 * o:32 * o + 32, 0:b - a],
                                     ACT.Copy, scale=scale).then_inc(rope_sh, 1)

        def rope_dve(v, U, c, m, scale, dst):
            a, b = CHUNK_ALL[c]
            v.wait_ge(rope_sh, m * 4 + 4)
            nc.vector.scalar_tensor_tensor(dst[:, a:b], gb[c][:, 0:b - a], scale, nB[:, a:b],
                                           ALU.mult, ALU.mult).then_inc(bank_free[c], 1)

        def rope_pool(pool, U, c, m, dst):
            a, b = CHUNK_ALL[c]
            pool.wait_ge(rope_sh, m * 4 + 4)
            nc.gpsimd.tensor_tensor(sh[:, 0:b - a], sh[:, 0:b - a], nC[:, a:b], ALU.mult).then_inc(rope_a, 1)
            pool.wait_ge(rope_a, m + 1)
            pool.wait_ge(bank_free[c], U.n + 1)
            nc.gpsimd.tensor_tensor(dst[:, a:b], dst[:, a:b], sh[:, 0:b - a], ALU.add).then_inc(rope_b, 1)

        FOX_RB = NORM_R
        SWA_RB = FOX_RB + 4 * FR + 4
        SWA_CB = 4 * FC
        SAM_RB, SAM_CB = SWA_RB + 4 * SIDE, SWA_CB + 4 * SIDE

        class Fox:

            fox = True

            def __init__(self, p, it=None):
                self.p = p if it is None else it
                self.it = it
                self.N = self.p * SIDE

            def chunk(self, d):
                return Count(d, FC, self.it) if self.it is not None else Count(FC * self.p + d)

            def round(self, d):
                return Count(FOX_RB + d, FR, self.it) if self.it is not None else Count(FOX_RB + FR * self.p + d)

            def chunks(self, n):
                return [(self.chunk(FOX_C[n] + j), a, b) for j, (a, b) in enumerate(fox_chunks(n % 8))]

            def rounds(self, n):
                return [(self.round(FOX_R[n] + j), a, b) for j, (a, b) in enumerate(fox_rounds(n % 8))]

            def blocks(self, n):
                h, i = divmod(n, 8)
                return [(k, P * j, vcur[0:k, P * j + DH * h:P * j + DH * h + DH])
                        for j, k in enumerate([P] * (i + 1) + [META])]

        class Swa:

            fox = False

            def __init__(self, r, it=None):
                self.p = r if it is None else it
                self.it = it
                self.N = self.p * SIDE + 4 * SIDE

            def chunk(self, d):
                return Count(SWA_CB + d, SIDE, self.it) if self.it is not None else Count(SWA_CB + SIDE * self.p + d)

            def round(self, d):
                return Count(SWA_RB + d, SIDE, self.it) if self.it is not None else Count(SWA_RB + SIDE * self.p + d)

            def chunks(self, n):
                return [(self.chunk(n), 0, META + P if n % 8 == 0 else META + 2 * P)]

            def rounds(self, n):
                return [(self.round(n), 0, 2 if n % 8 == 0 else 3)]

            def blocks(self, n):
                h, i = divmod(n, 8)
                c0 = DH * h
                out = [(META, 0, vball[0:META, c0:c0 + DH])]
                for j, t in enumerate([0] if i == 0 else [i - 1, i]):
                    out.append((P, META + P * j, vball[:, P * (t + 1) + c0:P * (t + 1) + c0 + DH]))
                return out

        def item_scores(pe, A_, n):
            h, i = divmod(n, 8)
            hp = slice(DH * h, DH * h + DH)
            q_ = qcur[hp, META + P * i:META + P * i + P]
            for C, a, b in A_.chunks(n):
                bank = chunk_slot(pe, C)
                if A_.fox:
                    diag = b == META + P * (i + 1)
                    last = nc.tensor.matmul(bank[:, 0:b - a], q_, kcur[hp, a:b], start=True, stop=not diag)
                    if diag:
                        last = nc.tensor.matmul(bank[:, b - a - P:b - a], ident_r[:, :], mask_r[:, :],
                                                start=False, stop=True)
                elif i == 0:
                    last = nc.tensor.matmul(bank[:, 0:b], q_, kbT[hp, 0:b], start=True, stop=True)
                else:
                    nc.tensor.matmul(bank[:, 0:META], q_, kbT[hp, 0:META], start=True, stop=True)
                    s0 = META + P * (i - 1)
                    last = nc.tensor.matmul(bank[:, META:b], q_, kbT[hp, s0:s0 + 2 * P], start=True, stop=True)
                last.then_inc(sc_full, 1)

        def item_max(v, A_, n):
            h, i = divmod(n, 8)
            ms, us, parts = 3 * (n % 4), u[n % 2], A_.chunks(n)
            full = [at(v, C.n + 1) for C, _, _ in parts]
            turned = at(v, A_.round(0).n if n < 2 else A_.rounds(n - 2)[-1][0].n + 1)
            if n == 0:
                ready = at(v, A_.chunk(6).n if A_.fox else A_.p * 2 + 2)
            apart(v)
            v.wait_ge(tp_full, turned)
            if n == 0 and A_.fox:
                v.wait_ge(sc_free, ready)
            if n == 0 and not A_.fox:
                v.wait_ge(swa_cur, ready)
            for j, (C, a, b) in enumerate(parts):
                if j:
                    apart(v)
                v.wait_ge(sc_full, full[j])
                bias = ckb[h][:, a:b] if A_.fox else cst[:, C_BAND0:C_BAND0 + b] if i == 0 else cst[:, C_BAND:C_BAND + b]
                init = -3e38 if A_.fox else sinkcur[:, h:h + 1]
                nc.vector.tensor_tensor_reduce(us[:, a:b], sc[C.slot][:, 0:b - a], bias, 1.0, init, ALU.subtract,
                                               ALU.max, mx[:, ms + j:ms + j + 1]).then_inc(sc_free, 1)
            v.wait_ge(sc_free, parts[-1][0].n + 1)
            nc.vector.tensor_reduce(nm[:, n % 4:n % 4 + 1], mx[:, ms:ms + len(parts)], AX_X, ALU.max,
                                    negate=True).then_inc(nm_done, 1)

        def item_exp(act, A_, n):
            w = A_.chunks(n)[-1][2]
            us, m = u[n % 2][:, 0:w], nm[:, n % 4:n % 4 + 1]
            act.wait_ge(nm_done, A_.N + (n + 1))
            nc.scalar.activation(us, us, ACT.Exp, bias=m, accum_out=ssum[:, n % 4:n % 4 + 1]).then_inc(p_done, 1)
            if not A_.fox:
                h = n // 8
                nc.scalar.activation(esink[:, n % 4:n % 4 + 1], sinkcur[:, h:h + 1], ACT.Exp, bias=m).then_inc(es_done, 1)

        def item_inv(v, A_, n):
            s_ = slice(n % 4, n % 4 + 1)
            v.wait_ge(p_done, A_.N + (n + 1))
            if not A_.fox:
                t_ = slice(4 + n % 4, 5 + n % 4)
                v.wait_ge(es_done, A_.p * SIDE + (n + 1))
                nc.vector.tensor_tensor(ssum[:, t_], ssum[:, s_], esink[:, s_], ALU.add).then_inc(tot_done, 1)
                v.wait_ge(tot_done, A_.p * SIDE + (n + 1))
                s_ = t_
            nc.vector.reciprocal(rinv[:, n % 4:n % 4 + 1], ssum[:, s_]).then_inc(sum_inv, 1)

        def item_turn(pe, A_, n):
            pe.wait_ge(p_done, A_.N + (n + 1))
            bl = A_.blocks(n)
            for R, a, b in A_.rounds(n):
                round_fill(pe, R, [u[n % 2][:, c0:c0 + P] for _, c0, _ in bl[a:b]])

        def item_turned(act, A_, n):
            if positive(A_.N) or n >= 2:
                act.wait_ge(pv_done, A_.N + (n - 1))
            for R, a, b in A_.rounds(n):
                act.wait_ge(tp_full, R.n + 1)
                nc.scalar.activation(PT[n % 2][:, P * a:P * b], tp[R.slot][:, 0:P * (b - a)],
                                     ACT.Copy).then_inc(tp_free[R.slot], 1)

        def item_values(pe, A_, n):
            rounds_read(pe, [R for R, _, _ in A_.rounds(n)])
            if positive(A_.N) or n >= 1:
                pe.wait_ge(o_done, A_.N + n)
            bl = A_.blocks(n)
            for j, (k, _, val) in enumerate(bl):
                last = nc.tensor.matmul(po[:, 0:DH], PT[n % 2][0:k, P * j:P * j + P], val,
                                        start=(j == 0), stop=(j == len(bl) - 1))
            last.then_inc(pv_done, 1)

        def item_out(v, A_, n):
            h, i = divmod(n, 8)
            v.wait_ge(pv_done, A_.N + (n + 1))
            v.wait_ge(sum_inv, A_.N + (n + 1))
            if n == 0:
                if not A_.fox:
                    v.wait_ge(o_out, A_.p * 32 + 64)
                elif positive(A_.p):
                    v.wait_ge(o_out, A_.p * 16)
            nc.vector.tensor_scalar(opair[:, P * i + DH * h:P * i + DH * h + DH], po[:, 0:DH],
                                    rinv[:, n % 4:n % 4 + 1], None, ALU.mult).then_inc(o_done, 1)

        STEPS = SIDE + 3

        def spread(jobs):
            at = {11: [0, 1, 3, 5, 6, 8, 10, 12, 14, 16, 17], 5: [3, 6, 10, 13, 17], 2: [3, 6]}[len(jobs)]
            return dict(zip(at, jobs))

        def steps_pe(pe, A_, jobs):
            for s in range(STEPS):
                if 0 <= s - 2 < SIDE:
                    item_turn(pe, A_, s - 2)
                if s < SIDE:
                    item_scores(pe, A_, s)
                if s in jobs:
                    jobs[s](pe)
                if 0 <= s - 3 < SIDE:
                    item_values(pe, A_, s - 3)

        def steps_act(act, A_, jobs):
            for s in range(STEPS):
                if 0 <= s - 2 < SIDE:
                    item_turned(act, A_, s - 2)
                if s < SIDE:
                    item_exp(act, A_, s)
                if s in jobs:
                    jobs[s](act)

        def steps_dve(v, A_, jobs, gate, g):
            for s in range(STEPS):
                if s < SIDE:
                    item_max(v, A_, s)
                if 0 <= s - 1 < SIDE:
                    item_inv(v, A_, s - 1)
                if 0 <= s - 3 < SIDE:
                    item_out(v, A_, s - 3)
                if s in jobs:
                    jobs[s](v)
                if s < 9:
                    gate_piece(v, gate, s, g)

        CKB = [(h, a, b) for h in range(2) for a, b in ((0, 400), (400, 912), (912, KEYS))]
        KVB = [P * j for j in range(9)] + [S0]

        def part(t, reg, size, c0=0):
            if isinstance(reg, int):
                return t[:, c0 + reg * size:c0 + reg * size + size]
            return t[:, bass.ds(reg * size + c0, size)]

        def ahead(U):
            V = Unit(0)
            V.n, V.slot, V.nth = U.n + 2, U.slot, U.nth + 1
            return V

        class FoxStep:

            def __init__(self, p, it=None):
                self.A = Fox(p, it)
                b = U_FOX if it is not None else U_FOX + 4 * p
                mk = (lambda n: Unit(n, 4, it)) if it is not None else Unit
                self.new = [mk(b + j) for j in range(4)]
                self.own = [mk(b - 3 + j) for j in range(3)]
                self.p = self.A.p
                self.last = it is None and p == 3

        FOX_JOBS = [(0, 1), (0, 2)] + [(j, c) for j in range(1, 4) for c in range(3)]

        def fox_setup_pe(pe, S):
            A_ = S.A
            pe.wait_ge(cur_copied, A_.p * 4 + 1)
            pe.wait_ge(lf_done, 1)
            for m, (h, a, b) in enumerate(CKB):
                bank = chunk_slot(pe, A_.chunk(m))
                nc.tensor.matmul(bank[:, 0:b - a], selcur[:, P * h:P * h + P], cum_lf[:, a:b],
                                 start=True, stop=True).then_inc(sc_full, 1)
                if m in (1, 3):
                    fox_turn_kv(pe, S, 4 + m // 2)
            pe.wait_ge(qk_moved, A_.p * 2 + 2)

        def fox_turn_kv(pe, S, j):
            src, U = (nC, S.own[2]) if j < 3 else (nB, S.own[1])
            if j % 3 == 0:
                unit_read(pe, U)
            round_fill(pe, S.A.round(j), [src[:, c0:c0 + P] for c0 in KVB[4 * (j % 3):4 * (j % 3) + 4]])

        def fox_setup_dve(v, S):
            A_ = S.A
            for U, src, dst in ((S.own[0], nA, qcur), (S.own[1], nB, kcur)):
                unit_read(v, U)
                nc.vector.tensor_copy(dst[:, :], src[:, :]).then_inc(qk_moved, 1)
            for m, (h, a, b) in enumerate(CKB):
                C = A_.chunk(m)
                v.wait_ge(sc_full, C.n + 1)
                nc.vector.tensor_copy(ckb[h][:, a:b], sc[C.slot][:, 0:b - a]).then_inc(sc_free, 1)

        def fox_setup_act(act, S):
            A_ = S.A
            if positive(A_.p):
                act.wait_ge(kv_out, A_.p * 96)
                act.wait_ge(pv_done, A_.N)
            act.wait_ge(lf_done, 1)
            for j in range(6):
                R = A_.round(j)
                dst = vcur if j < 3 else ktm
                w = P * len(KVB[4 * (j % 3):4 * (j % 3) + 4])
                act.wait_ge(tp_full, R.n + 1)
                nc.scalar.activation(dst[:, 512 * (j % 3):512 * (j % 3) + w], tp[R.slot][:, 0:w],
                                     ACT.Copy).then_inc(tp_free[R.slot], 1)
                if j == 3:
                    gate_act(act, S.new[0], 0, S.p)

        def fox_setup_pool(pool, S):
            A_ = S.A
            if positive(A_.p):
                pool.wait_ge(sc_full, A_.chunk(0).n)
            pool.wait_ge(lf_done, 1)
            nc.gpsimd.tensor_copy(selcur[:, :], part(cst[0:8, :], A_.p, 2 * P, C_SEL)).then_inc(cur_copied, 1)
            for U in S.own:
                unit_read(pool, U)
            for src, dst in ((nA, qTs), (nB, kTs), (nC, vTs)):
                nc.gpsimd.tensor_copy(part(dst, A_.p, P), src[:, S0:S0 + P]).then_inc(cur_copied, 1)

        def fox_store_kv(sp, A_):
            for tm, first, p_out, s_out in ((vcur, 0, "fox_v_p", "fox_v_s"), (ktm, 3, "fox_k_p", "fox_k_s")):
                rounds_read(sp, [A_.round(first + j) for j in range(3)])
                full = part(O[p_out][0:SEQ, :], A_.p, P).rearrange("(j t) n -> t j n", t=P)
                sp.dma_start(full, tm[:, 0:SEQ].rearrange("t (j n) -> t j n", j=8)).then_inc(kv_out, 16)
                sp.dma_start(part(O[p_out][SEQ:KEYS, :], A_.p, P), tm[0:META, SEQ:SEQ + P]).then_inc(kv_out, 16)
                sp.dma_start(part(O[s_out], A_.p, P), tm[:, 9 * P:10 * P]).then_inc(kv_out, 16)

        opair3 = opair[:, :].rearrange("t (i n) -> t i n", i=8)

        def fox_store_o(sp, p):
            sp.wait_ge(o_done, p * SIDE + SIDE)
            sp.dma_start(part(o_scr, p, P).rearrange("(i t) n -> t i n", t=P), opair3).then_inc(o_out, 16)

        def swa_store_o(sp, r):
            sp.wait_ge(o_done, r * SIDE + 5 * SIDE)
            for g in range(2):
                sp.dma_start(part(o_scr, r, DH, FOX_W + g * 4 * DH).rearrange("(i t) n -> t i n", t=P),
                             opair3[:, :, DH * g:DH * g + DH]).then_inc(o_out, 16)

        def fox_step_pe(pe, S):
            gemm(pe, S.new[0], 0, CHUNK_TOK[0], [lambda j=j: fox_turn_kv(pe, S, j) for j in range(4)])
            fox_setup_pe(pe, S)
            steps_pe(pe, S.A, spread([lambda e, j=j, c=c: gemm(e, S.new[j], c, CHUNK_ALL[c] if j else CHUNK_TOK[c])
                                      for j, c in FOX_JOBS]))

        def fox_step_act(act, S):
            fox_setup_act(act, S)

            def job(j, c):
                def run(e):
                    if j == 0:
                        gate_act(e, S.new[0], c, S.p)
                    elif j == 1 and not S.last:
                        q_read(e, S.new[1], c, S.p + 1)
                    elif j == 1:
                        rope_act(e, S.new[1], c, c, 1.0)
                    elif j == 3 and S.last:
                        rope_act(e, S.new[3], c, 3 + c, SCALE)
                    if c == 2:
                        hi(e, ahead(S.new[j]))
                return run
            steps_act(act, S.A, spread([job(j, c) for j, c in FOX_JOBS]))

        def q_move(v, A_, r):
            ropes, scores = at(v, r * 3 + 5), at(v, A_.chunks(SIDE - 1)[-1][0].n + 1)
            apart(v)
            v.wait_ge(rope_b, ropes)
            v.wait_ge(sc_full, scores)
            nc.vector.tensor_copy(qcur[:, 0:CHUNK_ALL[1][1]], nA[:, 0:CHUNK_ALL[1][1]]).then_inc(q_moved, 1)

        def fox_step_dve(v, S):
            fox_setup_dve(v, S)

            def job(j, c):
                def run(e):
                    if j == 0:
                        return
                    if not S.last:
                        if j > 1:
                            kv_read(e, S.new[j], c, S.p + 1, (nB, nC)[j - 2], (3, 0)[j - 2])
                    elif j == 1:
                        e.wait_ge(tab_in, 32)
                        rope_dve(e, S.new[1], c, c, 1.0, kbT)
                    elif j == 3:
                        if c == 0:
                            e.wait_ge(cur_copied, 4 * 4)
                            e.wait_ge(qk_moved, 4 * 2)
                        if c == 2:
                            q_move(e, S.A, 0)
                        rope_dve(e, S.new[3], c, 3 + c, SCALE, qcur if c == 2 else nA)
                    else:
                        a, b = CHUNK_ALL[c]
                        e.wait_ge(kv_out, 4 * 96)
                        gemm_wait(e, S.new[2], c)
                        nc.vector.tensor_copy(ktm[:, a:b], gb[c][:, 0:b - a]).then_inc(bank_free[c], 1)
                return run
            steps_dve(v, S.A, spread([job(j, c) for j, c in FOX_JOBS]), S.new[0], S.p)

        def fox_step_pool(pool, S):
            fox_setup_pool(pool, S)
            for j in range(4):
                if S.last and j in (1, 3):
                    if j == 1:
                        pool.wait_ge(tab_in, 32)
                    for c in range(3):
                        rope_pool(pool, S.new[j], c, j // 3 * 3 + c, kbT if j == 1 else qcur if c == 2 else nA)
                lo(pool, ahead(S.new[j]))

        def fox_step_sp(sp, S, qb=None):
            w, n = I["w_in"], S.new
            load(sp, n[2], cols_of(w, COL_VB) if S.last else cols_of(w, COL_KA + P, S.p, P))
            load(sp, n[3], cols_qb(0) if S.last else cols_of(w, COL_VA + P, S.p, P))
            fox_store_kv(sp, S.A)
            if S.last:
                sp.wait_ge(cur_copied, 4 * 4)
                sp.wait_ge(qk_moved, 4 * 2)
                sp.wait_ge(tp_full, S.A.round(6).n)
                sp.dma_start(nB[:, :], I["cos"]).then_inc(tab_in, 16)
                sp.dma_start(nC[:, :], I["sin"]).then_inc(tab_in, 16)
            gate_store(sp, S.p)
            load(sp, ahead(n[2]), cols_gate(1, S.p, 1))
            load(sp, ahead(n[3]), cols_of(w, COL_QA + 2 * P, S.p, P) if qb is None else qb)
            fox_store_o(sp, S.p)

        def swa_pre_pe(pe):
            unit_read(pe, Unit(U_PEEL + 2))
            pe.wait_ge(rope_b, 3)
            vcols = [0] + [META + P * t for t in range(8)] + [S0]
            src = [ktm[:, c:c + P] for c in vcols] + [kbT[:, S0 - P:S0], kbT[:, S0:S0 + P]]
            for j in range(3):
                round_fill(pe, Count(SWA_RB - 4 + j), src[4 * j:4 * j + 4])
            R = Count(SWA_RB - 1)
            pe.wait_ge(tp_free[R.slot], R.half)
            for j, c0 in enumerate(KVB):
                last = nc.tensor.transpose(tp[R.slot][:, 8 * j:8 * j + 8], lfq[:, c0:c0 + P], ident[0:8, 0:8])
            last.then_inc(tp_full, 1)

        def swa_pre_act(act):
            for j in range(3):
                R = Count(SWA_RB - 4 + j)
                act.wait_ge(tp_full, R.n + 1)
                nc.scalar.activation(vball[:, 512 * j:512 * j + 512], tp[R.slot][:, :], ACT.Copy).then_inc(tp_free[R.slot], 1)
            R = Count(SWA_RB - 1)
            act.wait_ge(tp_full, R.n + 1)
            act.wait_ge(kv_out, 4 * 96)
            act.wait_ge(pv_done, 4 * SIDE)
            nc.scalar.activation(vcur[:, 0:80], tp[R.slot][:, 0:80], ACT.Copy).then_inc(tp_free[R.slot], 1)

        def swa_pre_pool(pool):
            unit_read(pool, Unit(U_PEEL + 2))
            nc.gpsimd.tensor_copy(vbs[:, :], ktm[:, S0:S0 + P]).then_inc(vb_done, 1)

        def swa_pre_sp(sp):
            for j in range(4):
                round_read(sp, Count(SWA_RB - 4 + j))
            for name, b in (("swa_v_p", 8), ("swa_v_s", 9), ("swa_k_p", 10), ("swa_k_s", 11)):
                sp.dma_start(O[name], vball[:, P * b:P * b + P]).then_inc(kb_out, 16)
            sp.dma_start(O["fox_f_p"][0:SEQ, :].rearrange("(j t) h -> t j h", t=P),
                         vcur[:, 0:64].rearrange("t (j h) -> t j h", j=8)).then_inc(kb_out, 16)
            sp.dma_start(O["fox_f_p"][SEQ:KEYS, :], vcur[0:META, 64:72]).then_inc(kb_out, 16)
            sp.dma_start(O["fox_f_s"], vcur[:, 72:80]).then_inc(kb_out, 16)

        class SwaStep:

            def __init__(self, r, it=None):
                self.A = Swa(r, it)
                self.p = self.A.p
                b = U_SWA if it is not None else U_SWA + 2 * r
                self.new = [Unit(b + j, 2, it) if it is not None else Unit(b + j) for j in range(2)]
                self.last = it is None and r == 3
                self.jobs = [(j, c) for j in range(1 if self.last else 2) for c in range(3)][1:]

        def swa_setup_pool(pool, S):
            r = S.p
            ropes, items = at(pool, r * 3 + 6), at(pool, S.A.N)
            apart(pool)
            pool.wait_ge(rope_b, ropes)
            pool.wait_ge(o_done, items)
            rr = slice(r, r + 1) if isinstance(r, int) else bass.ds(r, 1)
            nc.gpsimd.tensor_copy(sinkcur.rearrange("p (o g) -> p o g", o=1),
                                  sinkb.rearrange("p (g r) -> p r g", g=2)[:, rr, :]).then_inc(swa_cur, 1)
            nc.gpsimd.tensor_copy(part(qbs, r, P), qcur[:, S0:S0 + P]).then_inc(swa_cur, 1)

        def swa_step_pe(pe, S):
            gemm(pe, S.new[0], 0, CHUNK_TOK[0])
            pe.wait_ge(rope_b, S.p * 3 + 6)
            pe.wait_ge(q_moved, S.p + 1)
            steps_pe(pe, S.A, spread([lambda e, j=j, c=c: gemm(e, S.new[j], c, CHUNK_ALL[c] if j else CHUNK_TOK[c])
                                      for j, c in S.jobs]))

        def swa_step_act(act, S):
            def job(j, c):
                def run(e):
                    if j == 0:
                        gate_act(e, S.new[0], c, S.p + 4)
                    else:
                        rope_act(e, S.new[1], c, S.p * 3 + (6 + c), SCALE)
                    if c == 2:
                        hi(e, ahead(S.new[j]))
                return run
            gate_act(act, S.new[0], 0, S.p + 4)
            steps_act(act, S.A, spread([job(j, c) for j, c in S.jobs]))

        def swa_step_dve(v, S):
            def job(j, c):
                def run(e):
                    if j:
                        if c == 0:
                            e.wait_ge(q_moved, S.p + 1)
                        if c == 2:
                            e.wait_ge(swa_cur, S.p * 2 + 2)
                            q_move(e, S.A, S.p + 1)
                        rope_dve(e, S.new[1], c, S.p * 3 + (6 + c), SCALE, qcur if c == 2 else nA)
                return run
            steps_dve(v, S.A, spread([job(j, c) for j, c in S.jobs]), S.new[0], S.p + 4)

        def swa_step_pool(pool, S):
            swa_setup_pool(pool, S)
            lo(pool, ahead(S.new[0]))
            if not S.last:
                for c in range(3):
                    rope_pool(pool, S.new[1], c, S.p * 3 + (6 + c), qcur if c == 2 else nA)
                lo(pool, ahead(S.new[1]))

        def swa_step_sp(sp, S, after=None):
            load(sp, ahead(S.new[0]), cols_gate(5, S.p, 1) if not S.last else cols_gate(9))
            if not S.last:
                load(sp, ahead(S.new[1]), cols_qb(S.p + 2) if after is None else after)
            gate_store(sp, S.p + 4)
            swa_store_o(sp, S.p)

        SAM_ROUNDS = 10
        cfk = I["cache_fox_k"].rearrange("o b (t p) h d -> (o b) p t (h d)", p=P)
        cfv = I["cache_fox_v"].rearrange("o b (t p) h d -> (o b) p t (h d)", p=P)
        csk = I["cache_swa_k"].rearrange("o b p g d -> (o b) p (g d)")
        csv = I["cache_swa_v"].rearrange("o b p g d -> (o b) p (g d)")
        clg = I["cache_fox_logf"].rearrange("o b (t p) h -> (o b) p t h", p=P)
        osT3 = osT.rearrange("p (k n) -> p k n", k=8)

        class Sam:

            def __init__(self, it, e):
                self.b = it * 2 + e
                self.e, self.it = e, it
                self.U = Unit(U_SAM + e, 2, it)
                self.U = Unit(U_SAM + e, 2, it)

            def round(self, d):
                return Count(SAM_RB + SAM_ROUNDS * self.e + d, 2 * SAM_ROUNDS, self.it)

            def chunk(self, d):
                return Count(SAM_CB + 2 * self.e + d, 4, self.it)

        def b_cols(t, blocks, b):
            v = t.rearrange("p (k n) -> p k n", k=blocks)
            return v[:, :, bass.ds(b * NEW, NEW)]

        def sam_caches(sp, S):
            e = S.e
            sp.wait_ge(sam_free, S.b + 1)
            for dst, src in ((kc, cfk), (vc, cfv)):
                sp.dma_start(dst[e][:, :].rearrange("p (t n) -> p t n", t=4),
                             src[bass.ds(S.b, 1), :, :, :].rearrange("o p t n -> p (o t) n")).then_inc(c_in[e], 16)
            for dst, src in ((kw, csk), (vw, csv)):
                sp.dma_start(dst[e][:, :], src[bass.ds(S.b, 1), :, :].rearrange("o p n -> p (o n)")
                             ).then_inc(c_in[e], 16)
            sp.dma_start(clf[:, 32 * e:32 * e + 32].rearrange("p (t h) -> p t h", t=4),
                         clg[bass.ds(S.b, 1), :, :, :].rearrange("o p t h -> p (o t) h")).then_inc(c_in[e], 16)

        def sam_sp(sp, it):
            for e in range(2):
                S = Sam(it, e)
                last = isinstance(it, int)
                load(sp, ahead(Unit(U_SAM + e, 2, it)), mix_parts(e) if last else cols_gate(10 + e, it, 2))
                if not (last and e):
                    sam_caches(sp, Sam(it, 1) if e == 0 else Sam(it + 1, 0))
                gate_store(sp, S.b + 8)

        def sam_pool(pool, it):
            for e in range(2):
                S = Sam(it, e)
                used = at(pool, S.chunk(0).n)
                apart(pool)
                pool.wait_ge(sc_full, used)
                kv3 = kvn[:, :].rearrange("p (k n) -> p k n", n=NEW)
                for dst, src in ((kv3[:, 0:4, :], b_cols(kTs[:, :], 4, S.b)), (kv3[:, 4:8, :], b_cols(vTs[:, :], 4, S.b)),
                                 (kv3[:, 8:9, :], b_cols(kbT[:, S0:S0 + P], 1, S.b)), (kv3[:, 9:10, :], b_cols(vbs[:, :], 1, S.b))):
                    nc.gpsimd.tensor_copy(dst, src).then_inc(s_stage, 1)
                qz3 = qz[:, :].rearrange("p (j n) -> p j n", j=4)
                qzs4 = qzs[:, :].rearrange("p (r g q) -> p r g q", r=4, g=2)
                for h in range(2):
                    hp = slice(DH * h, DH * h + DH)
                    if h:
                        staged = at(pool, S.b * 8 + 6)
                        apart(pool)
                        pool.wait_ge(s_stage, staged)
                    nc.gpsimd.tensor_copy(qz3[hp, :, NEW * h:NEW * h + NEW], b_cols(qTs[hp, :], 4, S.b)).then_inc(s_stage, 1)
                    nc.gpsimd.tensor_copy(qzs4[hp, :, h, :], b_cols(qbs[hp, :], 4, S.b)).then_inc(s_stage, 1)
                pool.wait_ge(s_stage, S.b * 8 + 8)
                lo(pool, ahead(Unit(U_SAM + e, 2, it)))

        def sam_first_pe(pe, S):
            def turn_k(j):
                if j == 0:
                    pe.wait_ge(c_in[S.e], S.it * 80 + 80)
                round_fill(pe, S.round(j), [kc[S.e][:, 512 * t + P * j:512 * t + P * j + P] for t in range(4)])
            gemm(pe, S.U, 0, CHUNK_TOK[0], [lambda j=j: turn_k(j) for j in range(4)])

        def sam_rest_pe(pe, S, following):
            e, U = S.e, S.U

            def turn_f():
                R = S.round(5)
                pe.wait_ge(tp_free[R.slot], R.half)
                for t in range(4):
                    last = nc.tensor.transpose(tp[R.slot][0:8, P * t:P * t + P], clf[:, 32 * e + 8 * t:32 * e + 8 * t + 8], ident[:, :])
                last.then_inc(tp_full, 1)

            def turn_new(R, ks):
                pe.wait_ge(s_stage, S.b * 8 + 8)
                pe.wait_ge(tp_free[R.slot], R.half)
                for t, k in enumerate(ks):
                    last = nc.tensor.transpose(tp[R.slot][0:NEW, P * t:P * t + P], kvn[:, NEW * k:NEW * k + NEW], ident[:, :])
                last.then_inc(tp_full, 1)
            gemm(pe, U, 1, CHUNK_TOK[1], [lambda: round_fill(pe, S.round(4), [kw[e][:, :]]), turn_f,
                                          lambda: turn_new(S.round(6), range(4, 8)), lambda: turn_new(S.round(7), (9,))])
            rounds_read(pe, [S.round(j) for j in range(5)])
            pe.wait_ge(s_cs, S.b * 2 + 2)
            bank = chunk_slot(pe, S.chunk(0))
            nsel = cst[0:8, C_NSEL:C_NSEL + P]
            nc.tensor.matmul(bank[:, :], nsel, cs[:, 0:512], start=True, stop=False)
            for j in range(4):
                last = nc.tensor.matmul(bank[:, :], qz[:, P * j:P * j + P], KcT[:, 512 * j:512 * j + 512],
                                        start=False, stop=(j == 3))
            last.then_inc(sc_full, 1)
            bank = chunk_slot(pe, S.chunk(1))
            nc.tensor.matmul(bank[:, 0:NEW], nsel, cs[:, 512:528], start=True, stop=False)
            nc.tensor.matmul(bank[:, 0:NEW], ident[:, :], cst[:, C_NEW:C_NEW + NEW], start=False, stop=False)
            for j in range(4):
                nc.tensor.matmul(bank[:, 0:NEW], qz[:, P * j:P * j + P], kvn[:, NEW * j:NEW * j + NEW],
                                 start=False, stop=(j == 3))
            for a, keys in ((32, kbT[:, 0:META]), (48, KwT[:, :]), (176, kvn[:, 8 * NEW:9 * NEW])):
                last = nc.tensor.matmul(bank[:, a:a + keys.shape[1]], qzs[:, :], keys, start=True, stop=True)
            last.then_inc(sc_full, 1)
            gemm(pe, U, 2, CHUNK_TOK[2])
            pe.wait_ge(s_scl, S.b * 2 + 2)
            round_fill(pe, S.round(8), [Ps[:, P * t:P * t + P] for t in range(4)])
            round_fill(pe, S.round(9), [Ps[:, 512:640], Pw[:, 0:P], Pw[:, META:META + P], Pw[:, META + P:META + 2 * P]])
            if following is not None:
                sam_first_pe(pe, following)
            rounds_read(pe, [S.round(j) for j in (6, 7, 8, 9)])
            pe.wait_ge(o_done, S.b * 6 + 8 * SIDE)
            for j in range(4):
                for t in range(4):
                    nc.tensor.matmul(po[:, 32 * j:32 * j + 32], vc[e][:, 512 * t + P * j:512 * t + P * j + P],
                                     PTs[:, P * t + 32 * j:P * t + 32 * j + 32], start=(t == 0), stop=False)
                nc.tensor.matmul(po[:, 32 * j:32 * j + 32], vn[:, P * j:P * j + P],
                                 PTs[0:NEW, 512 + 32 * j:512 + 32 * j + 32], start=False, stop=True)
            nc.tensor.matmul(po[:, P:2 * P], vball[0:META, 0:P], PTs[0:META, 5 * P:6 * P], start=True, stop=False)
            nc.tensor.matmul(po[:, P:2 * P], vw[e][:, :], PTs[:, 6 * P:7 * P], start=False, stop=False)
            nc.tensor.matmul(po[:, P:2 * P], vn[:, 4 * P:5 * P], PTs[0:NEW, 7 * P:8 * P],
                             start=False, stop=True).then_inc(sam_free, 1)

        mxs, nms, sms, tots, invs = (small[:, a:b] for a, b in ((140, 143), (143, 145), (145, 149), (149, 151), (151, 153)))

        def sam_first_act(act, S):
            for j in range(4):
                R = S.round(j)
                act.wait_ge(tp_full, R.n + 1)
                nc.scalar.activation(KcT[:, 512 * j:512 * j + 512], tp[R.slot][:, :], ACT.Copy).then_inc(tp_free[R.slot], 1)
            gate_act(act, S.U, 0, S.b + 8)

        def sam_rest_act(act, S, following):
            for j, dst, src in ((4, KwT[:, :], slice(0, P)), (6, vn[:, 0:512], slice(0, NEW))):
                R = S.round(j)
                act.wait_ge(tp_full, R.n + 1)
                nc.scalar.activation(dst, tp[R.slot][src, 0:dst.shape[1]], ACT.Copy).then_inc(tp_free[R.slot], 1)
            gate_act(act, S.U, 1, S.b + 8)
            act.wait_ge(s_red, S.b * 5 + 5)
            nc.scalar.activation(Ps[:, 0:512], sc[0][:, :], ACT.Exp, bias=nms[:, 0:1], accum_out=sms[:, 0:1]).then_inc(sc_free, 1)
            nc.scalar.activation(Ps[:, 512:528], sc[1][:, 0:NEW], ACT.Exp, bias=nms[:, 0:1], accum_out=sms[:, 1:2]).then_inc(s_exp, 1)
            nc.scalar.activation(Pw[:, 0:160], sc[1][:, 32:192], ACT.Exp, bias=nms[:, 1:2], accum_out=sms[:, 2:3]).then_inc(sc_free, 1)
            nc.scalar.activation(sms[:, 3:4], sinkrow, ACT.Exp, bias=nms[:, 1:2]).then_inc(s_exp, 1)
            gate_act(act, S.U, 2, S.b + 8)
            R = S.round(8)
            act.wait_ge(tp_full, R.n + 1)
            nc.scalar.activation(PTs[:, 0:512], tp[R.slot][:, :], ACT.Copy).then_inc(tp_free[R.slot], 1)
            hi(act, ahead(S.U))
            if following is not None:
                sam_first_act(act, following)

        def sam_rest_dve(v, S, following):
            R = S.round(5)
            v.wait_ge(tp_full, R.n + 1)
            nc.vector.tensor_tensor_scan(cs[:, 0:512], one8[:, :], tp[R.slot][0:8, :], 0.0,
                                         ALU.mult, ALU.add).then_inc(tp_free[R.slot], 1)
            round_read(v, R)
            nc.vector.tensor_copy(lf16[:, :], lfq[:, bass.ds(S.b * NEW + S0, NEW)]).then_inc(s_cs, 1)
            v.wait_ge(s_cs, S.b * 2 + 1)
            nc.vector.tensor_tensor_scan(cs[:, 512:528], one8[:, 0:NEW], lf16[:, :], cs[:, 511:512],
                                         ALU.mult, ALU.add).then_inc(s_cs, 1)
            R = S.round(7)
            v.wait_ge(tp_full, R.n + 1)
            nc.vector.tensor_copy(vn[:, 512:640], tp[R.slot][0:NEW, 0:P]).then_inc(tp_free[R.slot], 1)
            v.wait_ge(sc_full, S.chunk(0).n + 1)
            nc.vector.tensor_reduce(mxs[:, 0:1], sc[0][:, :], AX_X, ALU.max).then_inc(s_red, 1)
            v.wait_ge(sc_full, S.chunk(1).n + 1)
            nc.vector.tensor_reduce(mxs[:, 1:2], sc[1][:, 0:NEW], AX_X, ALU.max).then_inc(s_red, 1)
            nc.vector.tensor_reduce(mxs[:, 2:3], sc[1][:, 32:192], AX_X, ALU.max).then_inc(s_red, 1)
            v.wait_ge(s_red, S.b * 5 + 3)
            nc.vector.tensor_reduce(nms[:, 0:1], mxs[:, 0:2], AX_X, ALU.max, negate=True).then_inc(s_red, 1)
            nc.vector.tensor_scalar(nms[:, 1:2], mxs[:, 2:3], sinkrow, -1.0, ALU.max, ALU.mult).then_inc(s_red, 1)
            v.wait_ge(sc_free, S.chunk(1).n + 1)
            v.wait_ge(s_exp, S.b * 2 + 2)
            nc.vector.tensor_tensor(tots[:, 0:1], sms[:, 0:1], sms[:, 1:2], ALU.add).then_inc(s_sum, 1)
            nc.vector.tensor_tensor(tots[:, 1:2], sms[:, 2:3], sms[:, 3:4], ALU.add).then_inc(s_sum, 1)
            v.wait_ge(s_sum, S.b * 3 + 2)
            nc.vector.reciprocal(invs, tots).then_inc(s_sum, 1)
            v.wait_ge(s_sum, S.b * 3 + 3)
            nc.vector.tensor_scalar(Ps[:, 0:528], Ps[:, 0:528], invs[:, 0:1], None, ALU.mult).then_inc(s_scl, 1)
            nc.vector.tensor_scalar(Pw[:, 0:160], Pw[:, 0:160], invs[:, 1:2], None, ALU.mult).then_inc(s_scl, 1)
            gate_dve(v, S.U, 1, S.b + 8)
            R = S.round(9)
            v.wait_ge(tp_full, R.n + 1)
            nc.vector.tensor_copy(PTs[:, 512:1024], tp[R.slot][:, :]).then_inc(tp_free[R.slot], 1)
            gate_dve(v, S.U, 2, S.b + 8)
            if following is not None:
                gate_dve(v, following.U, 0, following.b + 8)
            v.wait_ge(sam_free, S.b + 3)
            pf = po[:, 0:P].rearrange("p (j h q) -> p j h q", j=4, h=2)
            pw = po[:, P:2 * P].rearrange("p (a s g q) -> p a s g q", a=2, s=2, g=2)
            for h in range(2):
                hp = slice(DH * h, DH * h + DH)
                nc.vector.tensor_copy(osT3[hp, 0:4, bass.ds(S.b * NEW, NEW)], pf[hp, :, h, :]).then_inc(o_done, 1)
            for g in range(2):
                for s in range(2):
                    nc.vector.tensor_copy(osT3[DH * s:DH * s + DH, 4 + 2 * g:6 + 2 * g, bass.ds(S.b * NEW, NEW)],
                                          pw[DH * g:DH * g + DH, :, s, g, :]).then_inc(o_done, 1)

        def sam_dve_gate0(v, S):
            gate_dve(v, S.U, 0, S.b + 8)

        def streams(eng, first, rest):
            first(eng, Sam(0, 0))
            with eng.Fori(0, 3) as it:
                rest(eng, Sam(it, 0), Sam(it, 1))
                rest(eng, Sam(it, 1), Sam(it + 1, 0))
            rest(eng, Sam(3, 0), Sam(3, 1))
            rest(eng, Sam(3, 1), None)

        MIX_RB = SAM_RB + 8 * SAM_ROUNDS
        MIX_G = 3 * U_MIX
        OREADY = 8 * SIDE + 6 * STREAMS

        def mix_parts(f, reg=None):
            out = []
            for j, w in enumerate(("w_o_fox", "w_o_swa")):
                v = I[w].rearrange("(k p) n -> p k n", p=P)
                cs_ = slice(f * P, f * P + P) if reg is None else bass.ds(reg * (2 * P) + f * P, P)
                out.append((lambda d, j=j: d[:, 4 * j:4 * j + 4, :], v[:, :, cs_]))
            return out

        def enter_mix(eng):
            eng.wait_ge(gemm_done, MIX_G)
            eng.wait_ge(o_done, OREADY)
            eng.wait_ge(sig_out, 16 * 16)

        def mix_load(sp, f):
            if f >= 3:
                sp.wait_ge(tp_full, MIX_RB + 2 * (f - 2))
            sp.dma_start(ot[f % 3][:, :], o_scr[P * f:P * f + P, :]).then_inc(x_in[f], 16)

        def sg_load(sp, s, f, reg=None):
            for dst, base in ((sga, 0), (sgb, D)):
                rows = slice(base + f * P, base + f * P + P) if reg is None else bass.ds(reg * (2 * P) + (base + f * P), P)
                sp.dma_start(dst[s][:, :], sig_scr[rows, :]).then_inc(sg_in[s], 16)

        def split_o_pe(pe, t):
            pe.wait_ge(x_in[t], 32)
            for h in range(2):
                round_fill(pe, Count(MIX_RB + 2 * t + h), [ot[t % 3][:, P * (4 * h + j):P * (4 * h + j) + P] for j in range(4)])

        def split_act(act, t, H3, rb, banks, sem_full, sem_hi):
            for h in range(2):
                act.wait_ge(sem_full, rb + 2 * t + h + 1)
                nc.scalar.activation(H3[:, 4 * h:4 * h + 4, P * t:P * t + P], four(banks[h]), ACT.Copy).then_inc(sem_hi, 1)

        def split_dve(v, t, H3, L3, banks, sem_hi, free):
            for h in range(2):
                v.wait_ge(sem_hi, 2 * t + h + 1)
                nc.vector.tensor_tensor(L3[:, 4 * h:4 * h + 4, P * t:P * t + P], four(banks[h]),
                                        H3[:, 4 * h:4 * h + 4, P * t:P * t + P].bitcast(F32), ALU.subtract).then_inc(free[h], 1)

        class Mix:

            def __init__(self, it, s):
                self.s, self.f, self.it = s, it * 2 + s, it
                self.U = Unit(U_MIX + s, 2, it)
                self.g = it * 12 + (MIX_G + 6 * s)
                self.used = it * 4 + (U_MIX + 2 * s)
                self.first = isinstance(it, int) and it == 0 and s == 0

            def product(self, y, c):
                return self.g + (2 * c + y + 1 if self.first else 3 * y + c + 1)

        def mix_pe(pe, M, y, c):
            if y == 0 and c == 0:
                pe.wait_ge(w_lo, M.U.n + 1)
            if y == 0 and M.first:
                for h in range(2):
                    pe.wait_ge(tp_free[h], MIX_RB // 2 + min(3 * c + 3, 8))
                if c == 2:
                    pe.wait_ge(o_lo, 1)
            pe.wait_ge(bank_free[c], M.used + y)
            a, b = 384 * c, 384 * c + 384
            for k in range(4):
                ws = slice((4 * y + k) * P, (4 * y + k + 1) * P)
                for j, (w_, x_) in enumerate(((wh, Oh3), (wl, Oh3), (wh, Ol3))):
                    last = nc.tensor.matmul(gb[c][:, 0:384], w_[M.U.slot][:, ws], x_[:, 4 * y + k, a:b],
                                            start=(k == 0 and j == 0), stop=(k == 3 and j == 2))
            last.then_inc(gemm_done, 1)

        def mix_dve(v, M, y, c):
            s_ = (sga, sgb)[y][M.s][:, 384 * c:384 * c + 384]
            if c == 0 and (y == 0 or M.first):
                v.wait_ge(sg_in[M.s], M.it * 32 + 32)
            v.wait_ge(gemm_done, M.product(y, c))
            nc.vector.tensor_tensor(s_, gb[c][:, 0:384], s_, ALU.mult).then_inc(bank_free[c], 1)

        def mix_split(v, M, c):
            s_ = sga[M.s][:, 384 * c:384 * c + 384]
            v.wait_ge(m_hi, M.f * 3 + (c + 1))
            d_ = mslice(Ml, M, c)
            nc.vector.tensor_tensor(d_, s_, mslice(Mh, M, c).bitcast(F32), ALU.subtract).then_inc(m_lo, 1)

        def mslice(T, M, c):
            return T[:, bass.ds(M.f * TOK + 384 * c, 384)]

        def mix_pool(pool, M, c):
            pool.wait_ge(bank_free[c], M.used + 2)
            s_ = sga[M.s][:, 384 * c:384 * c + 384]
            nc.gpsimd.tensor_tensor(s_, s_, sgb[M.s][:, 384 * c:384 * c + 384], ALU.add).then_inc(m_sum, 1)

        def mix_act(act, M, c):
            act.wait_ge(m_sum, M.f * 3 + (c + 1))
            nc.scalar.activation(mslice(Mh, M, c), sga[M.s][:, 384 * c:384 * c + 384], ACT.Copy).then_inc(m_hi, 1)

        def mix_tile_pe(pe, M):
            for y in range(2):
                for c in range(3):
                    mix_pe(pe, M, y, c)

        def mix_tile_dve(v, M, between=None):
            for y in range(2):
                for c in range(3):
                    mix_dve(v, M, y, c)
            if between is not None:
                between()
            for c in range(3):
                mix_split(v, M, c)

        U_OUT = U_MIX + 8
        U_MLP = U_OUT + 8
        OUT_G = MIX_G + 48
        xrows = [I["x_prompt"][0, P * t:P * t + P, :] for t in range(8)] + [XSRC[9]]
        yrows = [O["y_prompt"][P * t:P * t + P, :] for t in range(8)] + [O["y_sample"]]

        def row_parts(rows):
            return [(lambda d, j=j: d[:, 4 * j:4 * j + 4, :], rows[:, 512 * j:512 * j + 512].rearrange("p (k n) -> p k n", k=4))
                    for j in range(2)]

        def out_sp(sp):
            for k in range(8):
                U = Unit(U_OUT + k)
                if k < 2:
                    sp.wait_ge(w_lo, U.n - 1)
                else:
                    sp.wait_ge(wo_lo[k % 2], k // 2)
                dst = raw[U.slot][:, :].rearrange("p (k n) -> p k n", k=KT)
                for part_, src in row_parts(I["w_out"][P * k:P * k + P, :]):
                    sp.dma_start(part_(dst), src).then_inc(raw_full[U.slot], 16)
            sp.wait_ge(gemm_done, OUT_G)
            sp.wait_ge(m_lo, 24)
            sp.dma_start(gpost[:, :], I["g_post_mix"].to_broadcast([P, D])).then_inc(g2_in, 16)
            sp.dma_start(gmlp[:, :], I["g_pre_mlp"].to_broadcast([P, D])).then_inc(g2_in, 16)
            for t in range(TT + 2):
                if t < TT:
                    if t >= 2:
                        sp.wait_ge(hT_full, 2 * (t - 1))
                    sp.dma_start(xr[t % 2][:, :], xrows[t]).then_inc(xr_in[t % 2], 16)
                if t in (3, 5):
                    mlp_sp_early(sp, t // 4)
                if 0 <= t - 1 < TT:
                    sp.wait_ge(h_done, t)
                    sp.dma_start(h_scr[P * (t - 1):P * t, :], tb[(t - 1) % 2][:, :]).then_inc(h_out[(t - 1) % 2], 16)

        def out_hi(act, k):
            U = Unit(U_OUT + k)
            act.wait_ge(raw_full[U.slot], U.nth * 32 + 32)
            act.wait_ge(gemm_done, OUT_G)
            nc.scalar.activation(woh[:, D * k:D * k + D], raw[U.slot][:, :], ACT.Copy).then_inc(wo_hi, 1)

        def out_lo(eng, tt, k):
            U = Unit(U_OUT + k)
            eng.wait_ge(wo_hi, k + 1)
            tt(wol[:, D * k:D * k + D], raw[U.slot][:, :], woh[:, D * k:D * k + D].bitcast(F32),
               ALU.subtract).then_inc(wo_lo[k % 2], 1)

        def out_pe(pe, tiles):
            for t in tiles:
                if t >= 2:
                    pe.wait_ge(dn_free, 2 * (t - 1))
            for k in range(KT):
                if 0 in tiles:
                    pe.wait_ge(wo_lo[k % 2], k // 2 + 1)
                    pe.wait_ge(m_lo, 3 * k + 3)
                for t in tiles:
                    ts = slice(P * t, P * t + P)
                    for h in range(2):
                        bank = dn[(2 * t + h) % 4]
                        hs = slice(D * k + 512 * h, D * k + 512 * h + 512)
                        for j, (m_, w_) in enumerate(((Mh3, woh), (Mh3, wol), (Ml3, woh))):
                            last = nc.tensor.matmul(bank[:, :], m_[:, k, ts], w_[:, hs],
                                                    start=(k == 0 and j == 0), stop=(k == KT - 1 and j == 2))
                        if k == KT - 1:
                            last.then_inc(dn_full, 1)

        def out_turn(pe, t):
            pe.wait_ge(hn_done, t + 1)
            for h in range(2):
                if t:
                    pe.wait_ge(hT_free[h], t)
                for j in range(4):
                    last = nc.tensor.transpose(four(hb[h])[:, j, :], xr[t % 2][:, P * (4 * h + j):P * (4 * h + j) + P], ident[:, :])
                last.then_inc(hT_full, 1)

        stat = small[:, 48:160]

        class Link:

            def __init__(self, at):
                self.at = at

            def do(self, v, ins):
                ins.then_inc(x_chain, 1)
                self.at += 1
                v.wait_ge(x_chain, self.at)

        link = Link(11)

        def norm_var(v, ss, w, r, add=None):
            if add is not None:
                link.do(v, nc.vector.tensor_tensor(ss, ss, add, ALU.add))
            link.do(v, nc.vector.tensor_scalar(w, ss, 1.0 / D, EPS, ALU.mult, ALU.add))
            nc.vector.reciprocal(r, w).then_inc(rv_done, 1)

        def norm_newton(v, y, w, t1):
            link.do(v, nc.vector.tensor_tensor(t1, y, y, ALU.mult))
            link.do(v, nc.vector.tensor_tensor(t1, t1, w, ALU.mult))
            link.do(v, nc.vector.tensor_scalar(t1, t1, -0.5, 1.5, ALU.mult, ALU.add))
            link.do(v, nc.vector.tensor_tensor(y, y, t1, ALU.mult))

        def st(c, t, n=1):
            return stat[:, 16 * (t % 2) + c:16 * (t % 2) + c + n]

        def out_act_a(act, t):
            for h in range(2):
                act.wait_ge(dn_full, 2 * t + h + 1)
                if t:
                    act.wait_ge(sq_b, t)
                nc.scalar.activation(jk[:, 512 * h:512 * h + 512], dn[(2 * t + h) % 4][:, :], ACT.Square,
                                     accum_out=st(h, t)).then_inc(sq_a, 1)
            act.wait_ge(rv_done, 2 * t + 1)
            nc.scalar.activation(st(4, t), st(3, t), ACT.Sqrt).then_inc(sq_done, 1)

        def out_act_b(act, t):
            act.wait_ge(h_done, t + 1)
            act.wait_ge(sq_a, 2 * t + 2)
            nc.scalar.activation(jk[:, :], tb[t % 2][:, :], ACT.Square, accum_out=st(8, t)).then_inc(sq_b, 1)
            act.wait_ge(rv_done, 2 * t + 2)
            nc.scalar.activation(st(11, t), st(10, t), ACT.Sqrt).then_inc(sq_done, 1)

        def stored(eng):
            eng.wait_ge(h_out[0], 16 * (TT // 2 + 1))
            eng.wait_ge(h_out[1], 16 * (TT // 2))

        def out_dve_a(v, t):
            v.wait_ge(sq_a, 2 * t + 2)
            norm_var(v, st(0, t), st(2, t), st(3, t), st(1, t))
            v.wait_ge(sq_done, 2 * t + 3)
            norm_newton(v, st(4, t), st(2, t), st(5, t))
            if t >= 2:
                v.wait_ge(h_out[t % 2], 16 * (t // 2))
            for h in range(2):
                hs = slice(512 * h, 512 * h + 512)
                nc.vector.scalar_tensor_tensor(tb[t % 2][:, hs], dn[(2 * t + h) % 4][:, :], st(4, t), gpost[:, hs],
                                               ALU.mult, ALU.mult).then_inc(dn_free, 1)

        def out_pool(pool, t):
            pool.wait_ge(dn_free, 2 * t + 2)
            pool.wait_ge(xr_in[t % 2], 16 * (t // 2 + 1))
            nc.gpsimd.tensor_tensor(tb[t % 2][:, :], tb[t % 2][:, :], xr[t % 2][:, :], ALU.add).then_inc(h_done, 1)

        def out_dve_b(v, t):
            v.wait_ge(sq_b, t + 1)
            norm_var(v, st(8, t), st(9, t), st(10, t))
            v.wait_ge(sq_done, 2 * t + 4)
            norm_newton(v, st(11, t), st(9, t), st(12, t))
            nc.vector.scalar_tensor_tensor(xr[t % 2][:, :], tb[t % 2][:, :], st(11, t), gmlp[:, :],
                                           ALU.mult, ALU.mult).then_inc(hn_done, 1)

        UP_B = U_MIX + 16
        DB = 2 * TT
        WB = U_OUT

        def mlp_unit(g, j, down):
            return Unit(U_MLP + 2 * j + down, 2 * GRP, g)

        def early(g, j, down):
            return isinstance(g, int) and g == 0 and j < 2 and not down

        def mlp_sp_early(sp, j):
            if j == 0:
                sp.wait_ge(wo_lo[1], 4)
            else:
                sp.wait_ge(w_lo, WB + 1)
            U = mlp_unit(0, j, 0)
            dst = raw[U.slot][:, :].rearrange("p (k n) -> p k n", k=KT)
            for part_, src in cols_of(I["w_up"], P * j):
                sp.dma_start(part_(dst), src).then_inc(raw_full[U.slot], 16)

        def mlp_sp(sp, g):
            for j in range(GRP):
                for down in (0, 1):
                    if early(g, j, down):
                        continue
                    U = mlp_unit(g, j, down)
                    if down:
                        sp.wait_ge(d_lo, g * GRP + (j + 1))
                        rows = I["w_down"][bass.ds(g * (GRP * P) + P * j, P), :]
                        parts = row_parts(rows)
                    else:
                        sp.wait_ge(w_lo, g * GRP + (WB + j))
                        v = I["w_up"].rearrange("(k p) n -> p k n", p=P)
                        cs_ = bass.ds(g * (GRP * P) + P * j, P)
                        parts = [(lambda d, i=i: d[:, 4 * i:4 * i + 4, :], v[:, 4 * i:4 * i + 4, cs_]) for i in range(2)]
                    dst = raw[U.slot][:, :].rearrange("p (k n) -> p k n", k=KT)
                    for part_, src in parts:
                        sp.dma_start(part_(dst), src).then_inc(raw_full[U.slot], 16)

        def begun(g, j, c):
            return isinstance(g, int) and g == 0 and j == 0 and c < 2

        def groups(eng, group):
            group(0)
            with eng.Fori(1, NGRP - 1) as g:
                group(g)
            group(NGRP - 1)

        def mlp_hi(act, g, j, down):
            U = mlp_unit(g, j, down)
            act.wait_ge(raw_full[U.slot], U.nth * 32 + 32)
            if down:
                act.wait_ge(dn_full, g * 18 + DB)
                act.wait_ge(hT_full, 2 * TT)
                if isinstance(g, int) and g == 0:
                    stored(act)
                nc.scalar.activation(dh[:, D * j:D * j + D], raw[U.slot][:, :], ACT.Copy).then_inc(d_hi, 1)
            else:
                if j >= 2 or not isinstance(g, int) or g > 0:
                    act.wait_ge(gemm_done, g * 12 + (OUT_G + 3 * j - 3))
                nc.scalar.activation(wh[j % 2][:, :], raw[U.slot][:, :], ACT.Copy).then_inc(w_hi, 1)

        def mlp_lo(pool, g, j, down):
            U = mlp_unit(g, j, down)
            if down:
                pool.wait_ge(d_hi, g * GRP + (j + 1))
                hi_, lo_, done = dh[:, D * j:D * j + D], dl[:, D * j:D * j + D], d_lo
            else:
                pool.wait_ge(w_hi, g * GRP + (WB + j + 1))
                hi_, lo_, done = wh[j % 2][:, :], wl[j % 2][:, :], w_lo
            nc.gpsimd.tensor_tensor(lo_, raw[U.slot][:, :], hi_.bitcast(F32), ALU.subtract).then_inc(done, 1)

        def mlp_up_pe(pe, g, j, c):
            if c == 0:
                pe.wait_ge(w_lo, g * GRP + (WB + j + 1))
            if j == 0:
                for h in range(2):
                    pe.wait_ge(hT_free[h], 3 * c + 3)
            pe.wait_ge(bank_free[c], g * 4 + (UP_B + j))
            a = 384 * c
            for k in range(KT):
                ws = slice(P * k, P * k + P)
                for i, (w_, x_) in enumerate(((wh, Mh3), (wl, Mh3), (wh, Ml3))):
                    last = nc.tensor.matmul(gb[c][:, 0:384], w_[j % 2][:, ws], x_[:, k, a:a + 384],
                                            start=(k == 0 and i == 0), stop=(k == KT - 1 and i == 2))
            last.then_inc(gemm_done, 1)


        def mlp_up_act(act, g, j, c):
            m = 3 * j + c
            act.wait_ge(gemm_done, g * 12 + (OUT_G + m + 1))
            act.wait_ge(u_lo, g * 12 + (U_B + m - 1))
            act.wait_ge(dn_full, g * 18 + DB)
            nc.scalar.activation(rl[m % 2], gb[c][:, 0:384], ACT.Relu).then_inc(bank_free[c], 1)
            act.wait_ge(bank_free[c], g * 4 + (UP_B + j + 1))
            us = slice(TOK * j + 384 * c, TOK * j + 384 * c + 384)
            nc.scalar.activation(Uh[:, us], rl[m % 2], ACT.Square).then_inc(u_hi, 1)

        def mlp_up_dve(v, g, j, c):
            m = 3 * j + c
            us = slice(TOK * j + 384 * c, TOK * j + 384 * c + 384)
            v.wait_ge(bank_free[c], g * 4 + (UP_B + j + 1))
            v.wait_ge(u_lo, g * 12 + (U_B + m))
            nc.vector.tensor_tensor(rl2, rl[m % 2], rl[m % 2], ALU.mult).then_inc(u_sq, 1)
            v.wait_ge(u_sq, g * 12 + (m + 1))
            v.wait_ge(u_hi, g * 12 + (m + 1))
            nc.vector.tensor_tensor(Ul[:, us], rl2, Uh[:, us].bitcast(F32), ALU.subtract).then_inc(u_lo, 1)

        U_B = 2

        def mlp_down_pe(pe, g, t, h):
            q = 2 * t + h
            pe.wait_ge(dn_free, g * 18 + (DB + q - 2))
            if q < 3:
                pe.wait_ge(dn_free, DB)
            if h == 0 and t % 3 == 0:
                pe.wait_ge(u_lo, g * 12 + (U_B + 10 + t // 3))
            if q == 0:
                pe.wait_ge(d_lo, g * GRP + (GRP + 1))
            for j in range(GRP):
                us = slice(TOK * j + P * t, TOK * j + P * t + P)
                ds_ = slice(D * j + 512 * h, D * j + 512 * h + 512)
                for i, (u_, d_) in enumerate(((Uh, dh), (Uh, dl), (Ul, dh))):
                    last = nc.tensor.matmul(dn[q % 3][:, :], u_[:, us], d_[:, ds_],
                                            start=(j == 0 and i == 0), stop=(j == GRP - 1 and i == 2))
            last.then_inc(dn_full, 1)

        def mlp_down_dve(v, g, t, h):
            q = 2 * t + h
            ys = yacc[:, D * t + 512 * h:D * t + 512 * h + 512]
            v.wait_ge(dn_full, g * 18 + (DB + q + 1))
            if isinstance(g, int) and g == 0:
                if q == 0:
                    stored(v)
                nc.vector.tensor_copy(ys, dn[q % 3][:, :]).then_inc(dn_free, 1)
                return
            if q == 0:
                v.wait_ge(dn_free, g * 18 + DB)
            nc.vector.tensor_tensor(ys, dn[q % 3][:, :], ys, ALU.add).then_inc(dn_free, 1)

        def end_sp(sp):
            sp.wait_ge(gemm_done, OUT_G + 12 * NGRP)
            stored(sp)
            sp.dma_start(gend[:, :], I["g_post_mlp"].to_broadcast([P, D])).then_inc(g3_in, 16)
            for t in range(TT):
                sp.dma_start(hend[:, D * t:D * t + D], h_scr[P * t:P * t + P, :]).then_inc(x_in[t], 16)
            for t in range(TT):
                sp.wait_ge(y_done[t % 2], t // 2 + 1)
                sp.dma_start(yrows[t], yacc[:, D * t:D * t + D]).then_inc(y_out, 16)
            sp.wait_ge(y_out, 16 * TT)

        def end_act(act, t):
            if t == 0:
                act.wait_ge(gemm_done, OUT_G + 12 * NGRP)
            else:
                act.wait_ge(sq_b, TT + t)
            act.wait_ge(dn_free, DB + 18 * (NGRP - 1) + 2 * t + 2)
            nc.scalar.activation(jend[:, :], yacc[:, D * t:D * t + D], ACT.Square,
                                 accum_out=stat[:, 32 + t:33 + t]).then_inc(sq_b, 1)
            act.wait_ge(rv_done, 2 * TT + t + 1)
            nc.scalar.activation(stat[:, 62 + t:63 + t], stat[:, 52 + t:53 + t], ACT.Sqrt).then_inc(sq_done, 1)

        def end_dve(v, t):
            one = lambda c: stat[:, c + t:c + t + 1]
            v.wait_ge(sq_b, TT + t + 1)
            norm_var(v, one(32), one(42), one(52))
            v.wait_ge(sq_done, 2 * TT + 3 + t)
            norm_newton(v, one(62), one(42), one(72))
            v.wait_ge(g3_in, 16)
            yt, ht = yacc[:, D * t:D * t + D], hend[:, D * t:D * t + D]
            nc.vector.scalar_tensor_tensor(yt, yt, one(62), gend[:, :], ALU.mult, ALU.mult).then_inc(yn_done, 1)
            if t % 2:
                v.wait_ge(yn_done, t + 1)
                v.wait_ge(x_in[t], 48 if t < 8 else 32)
                nc.vector.tensor_tensor(yt, yt, ht, ALU.add).then_inc(y_done[1], 1)

        def end_pool(pool):
            for t in range(0, TT, 2):
                yt, ht = yacc[:, D * t:D * t + D], hend[:, D * t:D * t + D]
                pool.wait_ge(yn_done, t + 1)
                pool.wait_ge(x_in[t], 48 if t < 8 else 32)
                nc.gpsimd.tensor_tensor(yt, yt, ht, ALU.add).then_inc(y_done[0], 1)

        block = keep.enter_context(nc.Block())

        def attention_done(eng):
            eng.wait_ge(kb_out, 16 * 7)
            eng.wait_ge(o_out, 16 * 12)
            eng.wait_ge(swa_cur, 8)

        def fox_buffers_free(eng):
            eng.wait_ge(kb_out, 16 * 7)
            eng.wait_ge(kv_out, 16 * 24)
            eng.wait_ge(vb_done, 1)
            eng.wait_ge(tp_full, SWA_RB)
            eng.wait_ge(pv_done, 4 * SIDE)
            eng.wait_ge(sc_free, SWA_CB)

        @block.sync
        def _(sp):
            norm_sp(sp)
            load(sp, Unit(2), cols_of(I["w_in"], COL_KA))
            load(sp, Unit(3), cols_of(I["w_in"], COL_VA))
            load(sp, Unit(4), cols_gate(0))
            load(sp, Unit(5), cols_of(I["w_in"], COL_QA + P))
            fox_step_sp(sp, FoxStep(0))
            fox_step_sp(sp, FoxStep(1))
            fox_step_sp(sp, FoxStep(2), cols_of(I["w_in"], COL_KB))
            fox_step_sp(sp, FoxStep(3), cols_qb(1))
            swa_pre_sp(sp)
            swa_step_sp(sp, SwaStep(0))
            swa_step_sp(sp, SwaStep(1))
            fox_buffers_free(sp)
            sam_caches(sp, Sam(0, 0))
            swa_step_sp(sp, SwaStep(2), cols_gate(8))
            swa_step_sp(sp, SwaStep(3))
            attention_done(sp)
            mix_load(sp, 0)
            with sp.Fori(0, 3) as it:
                sam_sp(sp, it)
            sam_sp(sp, 3)
            enter_mix(sp)
            for f in range(1, 8):
                mix_load(sp, f)
                if f == 2:
                    sg_load(sp, 0, 0)
            sg_load(sp, 1, 1)
            with sp.Fori(0, 3) as it:
                for s in range(2):
                    M = Mix(it, s)
                    load(sp, ahead(M.U), mix_parts(2 + s, it))
                    sp.wait_ge(m_lo, M.f * 3 + 3)
                    sg_load(sp, s, 2 + s, it)
            out_sp(sp)
            mlp_sp(sp, 0)
            with sp.Fori(1, NGRP) as g:
                mlp_sp(sp, g)
            end_sp(sp)

        @block.scalar
        def _(act):
            norm_act(act)
            hi(act, Unit(2))
            lf_act_(act)
            for c in range(3):
                q_read(act, Unit(1), c, 0)
            for n in (3, 4, 5):
                hi(act, Unit(n))
            fox_step_act(act, FoxStep(0))
            with act.Fori(1, 3) as it:
                fox_step_act(act, FoxStep(None, it))
            fox_step_act(act, FoxStep(3))
            swa_pre_act(act)
            with act.Fori(0, 3) as it:
                swa_step_act(act, SwaStep(None, it))
            swa_step_act(act, SwaStep(3))
            attention_done(act)
            streams(act, sam_first_act, sam_rest_act)
            enter_mix(act)
            for t in range(8):
                split_act(act, t, Oh3, MIX_RB, tp, tp_full, o_hi)
            nc.scalar.activation(Oh3[:, :, SEQ:TOK], osT3[:, :, :], ACT.Copy).then_inc(o_hi, 1)

            def mix_step(M, more):
                for c in range(3):
                    mix_act(act, M, c)
                if more:
                    hi(act, ahead(M.U), used=M.g + 6)
            with act.Fori(0, 3) as it:
                for s in range(2):
                    mix_step(Mix(it, s), True)
            mix_step(Mix(3, 0), False)
            out_hi(act, 0)
            mix_step(Mix(3, 1), False)
            for k in range(1, 8):
                out_hi(act, k)
            act.wait_ge(m_lo, 24)
            for t in range(TT):
                out_act_a(act, t)
                out_act_b(act, t)
                if t >= 1:
                    split_act(act, t - 1, Mh3, 0, hb, hT_full, h_hi)
                if t in (3, 5):
                    mlp_hi(act, 0, t // 4, 0)
            mlp_up_act(act, 0, 0, 0)
            mlp_up_act(act, 0, 0, 1)
            split_act(act, TT - 1, Mh3, 0, hb, hT_full, h_hi)

            def group(g):
                if not isinstance(g, int) or g > 0:
                    mlp_hi(act, g, 0, 0)
                    mlp_hi(act, g, 1, 0)
                mlp_hi(act, g, 0, 1)
                for j in range(GRP):
                    for c in range(3):
                        if not begun(g, j, c):
                            mlp_up_act(act, g, j, c)
                    if j + 2 < GRP:
                        mlp_hi(act, g, j + 2, 0)
                    if j + 1 < GRP:
                        mlp_hi(act, g, j + 1, 1)
            groups(act, group)
            for t in range(TT):
                end_act(act, t)

        @block.vector
        def _(v):
            norm_dve(v)
            for c in range(3):
                lf_dve_z(v, c)
            lf_dve(v)
            for n, dst, r in ((2, nB, 3), (3, nC, 0)):
                for c in range(3):
                    kv_read(v, Unit(n), c, 0, dst, r)
            fox_step_dve(v, FoxStep(0))
            with v.Fori(1, 3) as it:
                fox_step_dve(v, FoxStep(None, it))
            fox_step_dve(v, FoxStep(3))
            with v.Fori(0, 3) as it:
                swa_step_dve(v, SwaStep(None, it))
            swa_step_dve(v, SwaStep(3))
            attention_done(v)
            nc.vector.memset(one8[:, :], 1.0).then_inc(one_set, 1)
            v.wait_ge(one_set, 1)
            streams(v, sam_dve_gate0, sam_rest_dve)
            enter_mix(v)
            M = Mix(0, 0)
            after = {3: [(0, 0)], 5: [(1, 0)], 6: [(0, 1)], 7: [(1, 1), (0, 2), (1, 2)]}
            for t in range(8):
                split_dve(v, t, Oh3, Ol3, tp, o_hi, tp_free)
                if t == 7:
                    v.wait_ge(o_hi, 17)
                    nc.vector.tensor_tensor(Ol3[:, :, SEQ:TOK], osT3[:, :, :], Oh3[:, :, SEQ:TOK].bitcast(F32),
                                            ALU.subtract).then_inc(o_lo, 1)
                for y, c in after.get(t, ()):
                    mix_dve(v, M, y, c)
            for c in range(3):
                mix_split(v, M, c)
            mix_tile_dve(v, Mix(0, 1))
            with v.Fori(1, 3) as it:
                for s in range(2):
                    mix_tile_dve(v, Mix(it, s))
            mix_tile_dve(v, Mix(3, 0))
            mix_tile_dve(v, Mix(3, 1), lambda: out_lo(v, nc.vector.tensor_tensor, 0))
            for k in range(2, 8, 2):
                out_lo(v, nc.vector.tensor_tensor, k)
            v.wait_ge(g2_in, 32)
            v.sem_inc(u_lo, U_B)
            for t in range(TT):
                out_dve_a(v, t)
                out_dve_b(v, t)
                if t >= 1:
                    split_dve(v, t - 1, Mh3, Ml3, hb, h_hi, hT_free)
            mlp_up_dve(v, 0, 0, 0)
            mlp_up_dve(v, 0, 0, 1)
            split_dve(v, TT - 1, Mh3, Ml3, hb, h_hi, hT_free)

            def group(g):
                for j in range(GRP):
                    for c in range(3):
                        if not begun(g, j, c):
                            mlp_up_dve(v, g, j, c)
                for t in range(TT):
                    for h in range(2):
                        mlp_down_dve(v, g, t, h)
                    if isinstance(g, int) and g > 0 and t:
                        end_dve(v, t - 1)
            groups(v, group)
            end_dve(v, TT - 1)

        @block.gpsimd
        def _(pool):
            for n in range(2):
                lo(pool, Unit(n))
            pool.wait_ge(tp_full, NORM_R)
            pool.wait_ge(tp_free[1], NORM_R // 2)
            for s in range(2):
                nc.gpsimd.memset(u[s][:, :], 0.0).then_inc(zero_u, 1)
            for n in range(2, 6):
                lo(pool, Unit(n))
            fox_step_pool(pool, FoxStep(0))
            with pool.Fori(1, 3) as it:
                fox_step_pool(pool, FoxStep(None, it))
            fox_step_pool(pool, FoxStep(3))
            swa_pre_pool(pool)
            with pool.Fori(0, 3) as it:
                swa_step_pool(pool, SwaStep(None, it))
            fox_buffers_free(pool)
            for t_ in (qz, qzs):
                nc.gpsimd.memset(t_[:, :], 0.0).then_inc(zero_s, 1)
            swa_step_pool(pool, SwaStep(3))
            attention_done(pool)
            for t_ in (Ps, Pw):
                nc.gpsimd.memset(t_[:, :], 0.0).then_inc(zero_s, 1)
            pool.wait_ge(zero_s, 4)
            with pool.Fori(0, 4) as it:
                sam_pool(pool, it)

            def mix_step(M, more):
                for c in range(3):
                    mix_pool(pool, M, c)
                if more:
                    lo(pool, ahead(M.U))
            with pool.Fori(0, 3) as it:
                for s in range(2):
                    mix_step(Mix(it, s), True)
            for s in range(2):
                mix_step(Mix(3, s), False)
            for k in range(1, 8, 2):
                out_lo(pool, nc.gpsimd.tensor_tensor, k)
            pool.wait_ge(wo_lo[0], 4)
            pool.sem_inc(d_lo, 1)
            for t in range(TT):
                out_pool(pool, t)
                if t in (3, 5):
                    mlp_lo(pool, 0, t // 4, 0)

            def group(g):
                if not isinstance(g, int) or g > 0:
                    mlp_lo(pool, g, 0, 0)
                    mlp_lo(pool, g, 1, 0)
                mlp_lo(pool, g, 0, 1)
                for j in range(GRP):
                    if j + 2 < GRP:
                        mlp_lo(pool, g, j + 2, 0)
                    if j + 1 < GRP:
                        mlp_lo(pool, g, j + 1, 1)
            groups(pool, group)
            end_pool(pool)

        @block.tensor
        def _(pe):
            norm_pe(pe)
            for n in (1, 2, 3):
                for c in range(3):
                    gemm(pe, Unit(n), c, CHUNK_ALL[c])
            pe.wait_ge(cst_r, 2)
            pe.wait_ge(zero_u, 2)
            fox_step_pe(pe, FoxStep(0))
            with pe.Fori(1, 3) as it:
                fox_step_pe(pe, FoxStep(None, it))
            fox_step_pe(pe, FoxStep(3))
            swa_pre_pe(pe)
            pe.sem_inc(sam_free, 2)
            with pe.Fori(0, 3) as it:
                swa_step_pe(pe, SwaStep(None, it))
            swa_step_pe(pe, SwaStep(3))
            streams(pe, sam_first_pe, sam_rest_pe)
            M = Mix(0, 0)
            for t in range(8):
                split_o_pe(pe, t)
                for y, c in {2: [(0, 0)], 5: [(1, 0), (0, 1)], 7: [(1, 1), (0, 2), (1, 2)]}.get(t, ()):
                    mix_pe(pe, M, y, c)
            mix_tile_pe(pe, Mix(0, 1))
            with pe.Fori(1, 4) as it:
                for s in range(2):
                    mix_tile_pe(pe, Mix(it, s))
            out_pe(pe, (0, 1))
            for t in range(2, TT):
                out_pe(pe, (t,))
                out_turn(pe, t - 2)
            out_turn(pe, TT - 2)
            mlp_up_pe(pe, 0, 0, 0)
            mlp_up_pe(pe, 0, 0, 1)
            out_turn(pe, TT - 1)

            def group(g):
                for j in range(GRP):
                    for c in range(3):
                        if not begun(g, j, c):
                            mlp_up_pe(pe, g, j, c)
                for t in range(TT):
                    for h in range(2):
                        mlp_down_pe(pe, g, t, h)
            groups(pe, group)


def tables():
    import numpy as np

    cst = np.zeros((P, C_ALL), np.float32)
    row = np.arange(P)
    cst[:, C_ID:C_ID + P] = np.eye(P, dtype=np.float32)
    cst[:, C_MASK:C_MASK + P] = np.where(row[None, :] <= row[:, None], 0.0, -BIG)
    band = np.zeros((P, META + 2 * P), np.float32)
    band[P // 2:, META:META + 64] = BIG
    band[:P // 2, META + 192:META + 256] = BIG
    cst[:, C_BAND:C_BAND + META + 2 * P] = band
    cst[:P // 2, C_BAND0 + META + 64:C_BAND0 + META + P] = BIG
    cst[:, C_NEW:C_NEW + NEW] = np.where(np.arange(NEW)[None, :] <= row[:, None] % NEW, 0.0, -BIG)
    for h in range(HEADS):
        cst[h, C_SEL + P * h:C_SEL + P * h + P] = 1.0
        cst[h, C_NSEL + NEW * h:C_NSEL + NEW * h + NEW] = -1.0
    half = DH // 2
    inv_freq = np.float32(10000.0) ** (-np.arange(half, dtype=np.float32) / np.float32(half))
    pos = np.concatenate([np.arange(-META, SEQ), np.tile(PAST + np.arange(NEW), STREAMS)]).astype(np.float32)
    ang = (pos[None, :] * inv_freq[:, None]).astype(np.float32).astype(np.float64)
    cos = np.tile(np.cos(ang), (4, 1)).astype(np.float32)
    sin = np.tile(np.concatenate([-np.sin(ang), np.sin(ang)]), (2, 1)).astype(np.float32)
    return {"cst": cst, "cos": cos, "sin": sin}


_INS = ["x_prompt", "x_sample", "cache_fox_k", "cache_fox_v", "cache_fox_logf", "cache_swa_k", "cache_swa_v",
        "meta_tokens", "w_in", "b_forget", "attn_sinks", "w_o_fox", "w_o_swa", "w_out", "g_pre_mix", "g_post_mix",
        "g_pre_mlp", "g_post_mlp", "w_up", "w_down"]
_OUTS = [("y_prompt", (1, SEQ, D)), ("y_sample", (STREAMS, NEW, D)),
         ("fox_k_p", (1, 1, KEYS, HEADS, DH)), ("fox_v_p", (1, 1, KEYS, HEADS, DH)), ("fox_f_p", (1, 1, KEYS, HEADS)),
         ("swa_k_p", (1, 1, P, 2, DH)), ("swa_v_p", (1, 1, P, 2, DH)),
         ("fox_k_s", (1, STREAMS, NEW, HEADS, DH)), ("fox_v_s", (1, STREAMS, NEW, HEADS, DH)),
         ("fox_f_s", (1, STREAMS, NEW, HEADS)),
         ("swa_k_s", (1, STREAMS, NEW, 2, DH)), ("swa_v_s", (1, STREAMS, NEW, 2, DH))]


def kernel(**inputs):
    import numpy as np
    import concourse.bacc as bacc
    from concourse.bass_utils import run_bass_kernel_spmd as run

    nc = bacc.Bacc("TRN2", target_bir_lowering=False, num_devices=1)
    arrays, I = {}, {}
    for name, a in [(n, inputs[n]) for n in _INS] + list(tables().items()):
        a = np.ascontiguousarray(a)
        arrays[f"in_{name}"] = a
        I[name] = nc.dram_tensor(f"in_{name}", a.shape, F32, kind="ExternalInput").ap()
    for name in ("w_in", "w_o_fox", "w_o_swa", "w_out", "w_up", "w_down"):
        I[name] = I[name].rearrange("o k n -> (o k) n")
    O = {}
    for name, shape in _OUTS:
        ap = nc.dram_tensor(f"out_{name}", shape, F32, kind="ExternalOutput").ap()
        O[name] = ap.rearrange({3: "a b c -> (a b) c", 4: "o a b c -> (o a b) c", 5: "o a b c d -> (o a b) (c d)"}[len(shape)])
    scratch = [nc.dram_tensor(n, s, F32, kind="Internal").ap()
               for n, s in (("o_scr", (SEQ, D)), ("sig_scr", (2 * D, TOK)), ("h_scr", (TOK, D)))]
    layer(nc, I, O, scratch)
    r = run(nc, [arrays], core_ids=[0])
    return tuple(r.results[0][f"out_{name}"] for name, _ in _OUTS)
```
